# Optimizing a Trainium2 kernel written in Bass

```python
import math
import jax, jax.numpy as jnp
from jax import lax
import numpy as np

D_MODEL = 1024
BATCH = 1
SEQ = 512
DEPTH = 2

CTX_LEN = 256
GRID_W = 64
N_MOD = 9
ATTN_WIDTH = 512
CONV_WIDTH = 256
FOURIER_WIDTH = 256
MIX_WIDTH = ATTN_WIDTH + CONV_WIDTH + FOURIER_WIDTH
N_HEADS = 4
HEAD_DIM = 64
V_DIM = 2 * HEAD_DIM
QK_WIDTH = N_HEADS * 2 * HEAD_DIM
V_WIDTH = N_HEADS * V_DIM
ATTN_IN = 2 * QK_WIDTH + V_WIDTH
CONV_IN = 2 * CONV_WIDTH
IN_WIDTH = ATTN_IN + CONV_IN + FOURIER_WIDTH
CONV_K = 31
FOURIER_GROUPS = 4
FOURIER_GDIM = FOURIER_WIDTH // FOURIER_GROUPS
D_FF = 2816
ROPE_BASE = 10000.0
ROT_AXIS = HEAD_DIM // 2
Q_BLOCK = 128
EPS = 1e-6

kernel_name = "hybrid_diffattn_conformer_fnet_macaron_dit"

def rmsnorm(x, g):
    xf = x.astype(jnp.float32)
    y = xf * lax.rsqrt(jnp.mean(xf * xf, axis=-1, keepdims=True) + EPS)
    return (y * g.astype(jnp.float32)).astype(x.dtype)

def modulate(h, shift, scale):
    return h * (1 + scale) + shift

def swiglu(h, wg, wu, wd):
    return (jax.nn.silu(h @ wg) * (h @ wu)) @ wd

def axial_rope_tables(n):
    rows = n // GRID_W
    row = jnp.broadcast_to(jnp.arange(rows)[:, None], (rows, GRID_W)).reshape(-1)
    col = jnp.broadcast_to(jnp.arange(GRID_W)[None, :], (rows, GRID_W)).reshape(-1)
    inv = ROPE_BASE ** (-jnp.arange(0, ROT_AXIS, 2, dtype=jnp.float32) / ROT_AXIS)
    ang_r = row.astype(jnp.float32)[:, None] * inv
    ang_c = col.astype(jnp.float32)[:, None] * inv
    shp = (n, 1, 1, ROT_AXIS // 2)
    return (jnp.cos(ang_r).reshape(shp), jnp.sin(ang_r).reshape(shp),
            jnp.cos(ang_c).reshape(shp), jnp.sin(ang_c).reshape(shp))

def rotate(x, cos, sin):
    x1, x2 = jnp.split(x, 2, axis=-1)
    return jnp.concatenate([x1 * cos - x2 * sin, x2 * cos + x1 * sin], axis=-1)

def apply_axial_rope(x, rope):
    cos_r, sin_r, cos_c, sin_c = rope
    xf = x.astype(jnp.float32)
    out = jnp.concatenate([rotate(xf[..., :ROT_AXIS], cos_r, sin_r),
                           rotate(xf[..., ROT_AXIS:], cos_c, sin_c)], axis=-1)
    return out.astype(x.dtype)

def split_qkv(u):
    b, n = u.shape[0], u.shape[1]
    q = u[..., :QK_WIDTH].reshape(b, n, N_HEADS, 2, HEAD_DIM)
    k = u[..., QK_WIDTH:2 * QK_WIDTH].reshape(b, n, N_HEADS, 2, HEAD_DIM)
    v = u[..., 2 * QK_WIDTH:].reshape(b, n, N_HEADS, V_DIM)
    return q, k, v

def diff_scores_to_out(qb, k, v, lam):
    s = jnp.einsum('bhiqd,bhikd->bhiqk', qb, k, preferred_element_type=jnp.float32) * (HEAD_DIM ** -0.5)
    p = jax.nn.softmax(s, axis=-1)
    p_diff = p[:, :, 0] - lam * p[:, :, 1]
    return jnp.einsum('bhqk,bhkd->bhqd', p_diff.astype(v.dtype), v)

def diff_head_norm(o, g_subln, lam_init):
    o = rmsnorm(o, g_subln) * (1.0 - lam_init)
    return o.reshape(o.shape[0], o.shape[1], V_WIDTH)

def diff_attention(u_lat, u_ctx, lam, lam_init, g_subln, rope, need_ctx_out):
    b, n = u_lat.shape[0], u_lat.shape[1]
    q_l, k_l, v_l = split_qkv(u_lat)
    q_c, k_c, v_c = split_qkv(u_ctx)
    q_l = apply_axial_rope(q_l, rope)
    k_l = apply_axial_rope(k_l, rope)
    q_l = q_l.transpose(0, 2, 3, 1, 4)
    k_l = k_l.transpose(0, 2, 3, 1, 4)
    q_c = q_c.transpose(0, 2, 3, 1, 4)
    k_c = k_c.transpose(0, 2, 3, 1, 4)
    v_l = v_l.transpose(0, 2, 1, 3)
    v_c = v_c.transpose(0, 2, 1, 3)
    k_all = jnp.concatenate([k_l, k_c], axis=3)
    v_all = jnp.concatenate([v_l, v_c], axis=2)
    nb = n // Q_BLOCK
    q_blocks = jnp.moveaxis(q_l.reshape(b, N_HEADS, 2, nb, Q_BLOCK, HEAD_DIM), 3, 0)
    o = lax.map(lambda qb: diff_scores_to_out(qb, k_all, v_all, lam), q_blocks)
    o = o.transpose(1, 0, 3, 2, 4).reshape(b, n, N_HEADS, V_DIM)
    o_lat = diff_head_norm(o, g_subln, lam_init)
    o_ctx = None
    if need_ctx_out:
        oc = diff_scores_to_out(q_c, k_c, v_c, lam).transpose(0, 2, 1, 3)
        o_ctx = diff_head_norm(oc, g_subln, lam_init)
    return o_lat, o_ctx

def conformer_conv(u, w_dw, b_dw, g_ln, b_ln, w_pw, b_pw):
    a, gate = jnp.split(u, 2, axis=-1)
    y = a * jax.nn.sigmoid(gate)
    y = lax.conv_general_dilated(y, w_dw[:, None, :], window_strides=(1,),
                                 padding=[(CONV_K // 2, CONV_K // 2)],
                                 dimension_numbers=('NWC', 'WIO', 'NWC'),
                                 feature_group_count=CONV_WIDTH) + b_dw
    yf = y.astype(jnp.float32)
    mu = jnp.mean(yf, axis=-1, keepdims=True)
    var = jnp.mean(jnp.square(yf - mu), axis=-1, keepdims=True)
    yf = (yf - mu) * lax.rsqrt(var + EPS) * g_ln.astype(jnp.float32) + b_ln.astype(jnp.float32)
    y = jax.nn.silu(yf).astype(u.dtype)
    return y @ w_pw + b_pw

def fourier_mix(u, w_f, b_f):
    b, n = u.shape[0], u.shape[1]
    uf = u.astype(jnp.float32).reshape(b, n, FOURIER_GROUPS, FOURIER_GDIM)
    f = jnp.fft.fft2(uf, axes=(1, 3), norm='ortho').real
    f = f.reshape(b, n, FOURIER_WIDTH).astype(u.dtype)
    return f @ w_f + b_f

def ffn_sublayer(s, m, i, g, wg, wu, wd):
    h = modulate(rmsnorm(s, g), m[3 * i], m[3 * i + 1])
    return s + 0.5 * m[3 * i + 2] * swiglu(h, wg, wu, wd)

def hybrid_layer(x, ctx, mod_x, mod_c, p, lam_init, rope, need_ctx_out):
    mx = jnp.split(mod_x, N_MOD, axis=-1)
    mc = jnp.split(mod_c, N_MOD, axis=-1)
    x = ffn_sublayer(x, mx, 0, p['g_ffn1'], p['w1g'], p['w1u'], p['w1d'])
    ctx = ffn_sublayer(ctx, mc, 0, p['g_ffn1'], p['w1g'], p['w1u'], p['w1d'])
    h = modulate(rmsnorm(x, p['g_mix']), mx[3], mx[4])
    hc = modulate(rmsnorm(ctx, p['g_mix']), mc[3], mc[4])
    u = h @ p['w_in']
    uc = hc @ p['w_in']
    lam = (jnp.exp(jnp.sum(p['lq1'].astype(jnp.float32) * p['lk1'].astype(jnp.float32)))
           - jnp.exp(jnp.sum(p['lq2'].astype(jnp.float32) * p['lk2'].astype(jnp.float32)))
           + lam_init)
    a_lat, a_ctx = diff_attention(u[..., :ATTN_IN], uc[..., :ATTN_IN], lam, lam_init,
                                  p['g_subln'], rope, need_ctx_out)
    conv_args = (p['w_dw'], p['b_dw'], p['g_cln'], p['b_cln'], p['w_pw'], p['b_pw'])
    conv_lat = conformer_conv(u[..., ATTN_IN:ATTN_IN + CONV_IN], *conv_args)
    four_lat = fourier_mix(u[..., ATTN_IN + CONV_IN:], p['w_f'], p['b_f'])
    y = jnp.concatenate([a_lat, conv_lat, four_lat], axis=-1) @ p['w_out']
    x = x + mx[5] * y
    if need_ctx_out:
        conv_ctx = conformer_conv(uc[..., ATTN_IN:ATTN_IN + CONV_IN], *conv_args)
        four_ctx = fourier_mix(uc[..., ATTN_IN + CONV_IN:], p['w_f'], p['b_f'])
        yc = jnp.concatenate([a_ctx, conv_ctx, four_ctx], axis=-1) @ p['w_out']
        ctx = ctx + mc[5] * yc
        ctx = ffn_sublayer(ctx, mc, 2, p['g_ffn2'], p['w2g'], p['w2u'], p['w2d'])
    x = ffn_sublayer(x, mx, 2, p['g_ffn2'], p['w2g'], p['w2u'], p['w2d'])
    return x, ctx

def setup_inputs(seed: int = 0) -> dict:
    key = jax.random.key(seed)
    ks = jax.random.split(key, 40)
    f32 = jnp.float32

    def nrm(k, shape, scale):
        return jax.random.normal(k, shape, f32) * scale

    def gain(k, shape):
        return 1.0 + 0.02 * jax.random.normal(k, shape, f32)

    L = DEPTH
    return {
        "x": nrm(ks[0], (BATCH, SEQ, D_MODEL), 1.0),
        "c": nrm(ks[1], (BATCH, D_MODEL), 1.0),
        "ctx": nrm(ks[2], (BATCH, CTX_LEN, D_MODEL), 1.0),
        "c_ctx": nrm(ks[3], (D_MODEL,), 1.0),
        "w_ada": nrm(ks[4], (L, D_MODEL, N_MOD * D_MODEL), 0.5 * D_MODEL ** -0.5),
        "b_ada": nrm(ks[5], (L, N_MOD * D_MODEL), 0.01),
        "g_ffn1": gain(ks[6], (L, D_MODEL)),
        "g_mix": gain(ks[7], (L, D_MODEL)),
        "g_ffn2": gain(ks[8], (L, D_MODEL)),
        "w_ffn1_gate": nrm(ks[9], (L, D_MODEL, D_FF), D_MODEL ** -0.5),
        "w_ffn1_up": nrm(ks[10], (L, D_MODEL, D_FF), D_MODEL ** -0.5),
        "w_ffn1_down": nrm(ks[11], (L, D_FF, D_MODEL), D_FF ** -0.5),
        "w_ffn2_gate": nrm(ks[12], (L, D_MODEL, D_FF), D_MODEL ** -0.5),
        "w_ffn2_up": nrm(ks[13], (L, D_MODEL, D_FF), D_MODEL ** -0.5),
        "w_ffn2_down": nrm(ks[14], (L, D_FF, D_MODEL), D_FF ** -0.5),
        "w_in": nrm(ks[15], (L, D_MODEL, IN_WIDTH), D_MODEL ** -0.5),
        "lambda_q1": nrm(ks[16], (L, HEAD_DIM), 0.1),
        "lambda_k1": nrm(ks[17], (L, HEAD_DIM), 0.1),
        "lambda_q2": nrm(ks[18], (L, HEAD_DIM), 0.1),
        "lambda_k2": nrm(ks[19], (L, HEAD_DIM), 0.1),
        "g_subln": gain(ks[20], (L, V_DIM)),
        "w_dw": nrm(ks[21], (L, CONV_K, CONV_WIDTH), CONV_K ** -0.5),
        "b_dw": nrm(ks[22], (L, CONV_WIDTH), 0.01),
        "g_conv_ln": gain(ks[23], (L, CONV_WIDTH)),
        "b_conv_ln": nrm(ks[24], (L, CONV_WIDTH), 0.01),
        "w_pw": nrm(ks[25], (L, CONV_WIDTH, CONV_WIDTH), CONV_WIDTH ** -0.5),
        "b_pw": nrm(ks[26], (L, CONV_WIDTH), 0.01),
        "w_fourier": nrm(ks[27], (L, FOURIER_WIDTH, FOURIER_WIDTH), FOURIER_WIDTH ** -0.5),
        "b_fourier": nrm(ks[28], (L, FOURIER_WIDTH), 0.01),
        "w_out": nrm(ks[29], (L, MIX_WIDTH, D_MODEL), MIX_WIDTH ** -0.5),
        "g_final": gain(ks[30], (D_MODEL,)),
    }

def reference(x, c, ctx, c_ctx, w_ada, b_ada, g_ffn1, g_mix, g_ffn2,
              w_ffn1_gate, w_ffn1_up, w_ffn1_down, w_ffn2_gate, w_ffn2_up, w_ffn2_down,
              w_in, lambda_q1, lambda_k1, lambda_q2, lambda_k2, g_subln,
              w_dw, b_dw, g_conv_ln, b_conv_ln, w_pw, b_pw, w_fourier, b_fourier,
              w_out, g_final):
    n = x.shape[1]
    rope = axial_rope_tables(n)
    for l in range(DEPTH):
        lam_init = 0.8 - 0.6 * math.exp(-0.3 * l)
        mod_x = (jax.nn.silu(c) @ w_ada[l] + b_ada[l])[:, None, :]
        mod_c = (jax.nn.silu(c_ctx) @ w_ada[l] + b_ada[l])[None, None, :]
        p = dict(g_ffn1=g_ffn1[l], g_mix=g_mix[l], g_ffn2=g_ffn2[l],
                 w1g=w_ffn1_gate[l], w1u=w_ffn1_up[l], w1d=w_ffn1_down[l],
                 w2g=w_ffn2_gate[l], w2u=w_ffn2_up[l], w2d=w_ffn2_down[l],
                 w_in=w_in[l], lq1=lambda_q1[l], lk1=lambda_k1[l],
                 lq2=lambda_q2[l], lk2=lambda_k2[l], g_subln=g_subln[l],
                 w_dw=w_dw[l], b_dw=b_dw[l], g_cln=g_conv_ln[l], b_cln=b_conv_ln[l],
                 w_pw=w_pw[l], b_pw=b_pw[l], w_f=w_fourier[l], b_f=b_fourier[l],
                 w_out=w_out[l])
        x, ctx = hybrid_layer(x, ctx, mod_x, mod_c, p, lam_init, rope,
                              need_ctx_out=(l < DEPTH - 1))
    return rmsnorm(x, g_final)


_drawn_inputs = setup_inputs


def setup_inputs(seed=0):
    import zlib

    import numpy as np

    out = dict(_drawn_inputs(seed))
    spreads = {}
    factors = {'b_ada': 3.601,
     'g_ffn1': 8.0,
     'g_mix': 8.0,
     'g_ffn2': 8.0,
     'lambda_q1': 2.947,
     'lambda_k1': 4.965,
     'lambda_q2': 6.335,
     'lambda_k2': 64.0,
     'g_subln': 53.634,
     'b_dw': 64.0,
     'g_conv_ln': 64.0,
     'b_conv_ln': 64.0,
     'b_pw': 64.0,
     'b_fourier': 64.0,
     'g_final': 7.822}
    for name, (base, spread) in spreads.items():
        noise = np.random.default_rng([zlib.crc32(name.encode()), seed]).standard_normal(out[name].shape)
        drawn = base * np.exp(spread * noise) if base else spread * noise
        out[name] = __import__('jax').numpy.asarray(drawn.astype(out[name].dtype))
    for name, factor in factors.items():
        out[name] = (out[name] * factor).astype(out[name].dtype)
    return out
```

```python
import math
from contextlib import ExitStack

import numpy as np

import concourse.bass as bass
from concourse import mybir

DEPTH = 2
D = 1024
LAT, CTX = 512, 256
TOK = LAT + CTX
KD = D // 128
FF = 2816
GW = 256
NG = FF // GW
HEADS = 4
HD = 64
QKW = 512
CONVW = 256
TAPS = 31
HALF = TAPS // 2
INW = 2304
EPS = 1e-6
GRID_W = 64
RING = 3
TILE = 2048
LINE = HALF + LAT + HALF + CTX + HALF
BOTH = ((0, LAT), (LAT, CTX))
ONLY_LAT = ((0, LAT),)
C_LAT = HALF
C_CTX = HALF + LAT + HALF

ROW = {}
_at = 0
for _name, _n in (("b_ada", 72), ("g_ffn1", 8), ("g_mix", 8), ("g_ffn2", 8), ("g_subln", 1), ("b_dw", 2),
                  ("g_conv_ln", 2), ("b_conv_ln", 2), ("b_pw", 2), ("b_fourier", 2)):
    ROW[_name] = (_at, _n)
    _at += _n
NROW = _at
NADA = 9 * D // 512
FIRST_BLOCKS = (0, 1, 2, 3, 4, 5, NADA - 1)
SIDE_GROUPS = ({g: (0, 6 + g) for g in range(NG)}, {g: (1, g - 1) for g in range(1, NG)},
               {g: (1, NG - 2 + g) for g in range(1, NADA - (NG - 1) + 1)}, {})
SIDE_AT = 5


def segs_of(norm):
    return ONLY_LAT if norm >= 5 else BOTH


def mix_segs(l):
    return BOTH if l < DEPTH - 1 else ONLY_LAT


def units_of(l):
    return [(h, s, t) for h in range(HEADS) for s in range(len(mix_segs(l))) for t in range(mix_segs(l)[s][1] // 128)]


class Plan:

    def __init__(self):
        self.n = 0
        self.bank = 0
        self.uses = [0] * 8
        self.slots = {}
        self.tiles = []
        self.raw = {}
        self.split = {}
        self.lastuse = {}
        self.before_att = []
        self.nsplit = 0
        self.build()

    def slot(self, key, bank=None):
        if bank is None:
            bank = self.bank
            self.bank = (bank + 1) % 8
        self.slots[key] = (self.n, bank, self.uses[bank])
        self.n += 1
        self.uses[bank] += 1

    def tile(self, key, split=True):
        self.raw[key] = len(self.tiles)
        self.tiles.append(key)
        if split:
            self.split[key] = self.nsplit
            self.nsplit += 1

    def used(self, key, slot):
        self.lastuse[key] = slot

    def norm(self, q):
        for s in range(len(segs_of(q))):
            self.slot(("stat", q, s))

    def ada(self, l):
        last = None
        for b in FIRST_BLOCKS:
            self.slot(("ada", l, b))
            if last is not None:
                self.slot(("adaT", l, last))
            last = b
            self.tile(("ada", l, b, 0), split=False)
            self.tile(("ada", l, b, 1), split=False)
            self.used(("ada", l, b, 0), ("ada", l, b))
            self.used(("ada", l, b, 1), ("ada", l, b))
        self.slot(("adaT", l, last))

    def side(self, f, g):
        if g in SIDE_GROUPS[f]:
            self.slot(("side", f, g), (self.bank + 4) % 8)

    def ffn(self, f):
        ns = len(segs_of((0, 2, 3, 5)[f]))

        def gate_up(g):
            for c in range(2):
                for w in "gu":
                    for s in range(ns):
                        self.slot((w, f, g, c, s))
            self.used(("G", f, g), ("g", f, g, 1, ns - 1))
            self.used(("U", f, g), ("u", f, g, 1, ns - 1))

        def down(g):
            for j in range(KD):
                for s in range(ns):
                    self.slot(("d", f, g, j, s))
                if j == SIDE_AT:
                    self.side(f, g + 1)
            self.used(("D", f, g), ("d", f, g, KD - 1, ns - 1))

        gate_up(0)
        self.side(f, 0)
        self.tile(("G", f, 0))
        self.tile(("U", f, 0))
        for g in range(1, NG):
            self.tile(("G", f, g))
            self.tile(("U", f, g))
            self.tile(("D", f, g - 1))
            gate_up(g)
            down(g - 1)
        self.tile(("D", f, NG - 1))
        down(NG - 1)

    def mix(self, l):
        ms = mix_segs(l)
        for c in range(2):
            self.tile(("conv", l, c))
            for w in "ga":
                for s in range(len(ms)):
                    self.slot(("conv" + w, l, c, s))
            self.used(("conv", l, c), ("conva", l, c, len(ms) - 1))
        self.tile(("four", l))
        nt = sum(n for _, n in ms) // 128
        for t in range(nt):
            self.slot(("X", l, t))
        self.used(("four", l), ("X", l, nt - 1))
        for v in range(2):
            self.tile(("V", l, v))
            for t in range(TOK // 128):
                self.slot(("V", l, v, t))
            self.used(("V", l, v), ("V", l, v, TOK // 128 - 1))
        for w, ss in (("K", BOTH), ("Q", ms)):
            for v in range(2):
                self.tile((w, l, v))
                for c in range(2):
                    for s in range(len(ss)):
                        self.slot((w, l, 2 * v + c, s))
                self.used((w, l, v), (w, l, 2 * v + 1, len(ss) - 1))
        for k in ("C", "S", "W"):
            self.tile((k, l), split=False)
        for j in range(2):
            for w in "CS":
                for s in range(len(ms)):
                    self.slot(("Z", l, j, w, s))
        self.used(("C", l), ("Z", l, 1, "S", len(ms) - 1))
        self.used(("S", l), ("Z", l, 1, "S", len(ms) - 1))
        for j in range(2):
            for s in range(len(ms)):
                self.slot(("F", l, j, s))
        for o in range(2):
            for s in range(len(ms)):
                self.slot(("Fo", l, o, s))
        for s in range(len(ms)):
            self.slot(("mean", l, s))
        for s in range(len(ms)):
            self.slot(("var", l, s))
        for o in range(2):
            for s in range(len(ms)):
                self.slot(("pw", l, o, s))
        self.used(("W", l), ("pw", l, 1, len(ms) - 1))
        u = units_of(l)
        self.before_att.append(list(self.uses))
        for i in range(len(u) + 3):
            if i < len(u):
                self.slots[("score", l, i)] = (self.n, None, None)
                self.n += 1
            if 0 <= i - 2 < len(u):
                self.slot(("T", l, i - 2, 0), 6)
            if 0 <= i - 3 < len(u):
                h, s, t = u[i - 3]
                if t == 0:
                    self.slots[("O", l, h, s)] = (None, 7, self.uses[7])
                    self.uses[7] += 1
                if t == ms[s][1] // 128 - 1:
                    self.slots[("O", l, h, s)] = (self.n,) + self.slots[("O", l, h, s)][1:]
                    self.n += 1
            if 0 <= i - 2 < len(u) and u[i - 2][1] == 0:
                self.slot(("T", l, i - 2, 1), 6)
        self.bank = 0
        for h in range(HEADS):
            for s in range(len(ms)):
                self.slot(("hn", l, h, s))
        for v in range(4):
            self.tile(("out", l, v))
            for c in range(2):
                for s in range(len(ms)):
                    self.slot(("out", l, 2 * v + c, s))
            self.used(("out", l, v), ("out", l, 2 * v + 1, len(ms) - 1))

    def build(self):
        for i in range(4):
            self.slot(("vec", i))
        for s in range(2):
            for j in range(KD):
                self.slot(("xin", s, j))
        self.ada(0)
        for l in range(DEPTH):
            self.norm(3 * l)
            self.ffn(2 * l)
            self.norm(3 * l + 1)
            self.mix(l)
            self.norm(3 * l + 2)
            self.ffn(2 * l + 1)
        self.norm(3 * DEPTH)
        for t in range(LAT // 128):
            for half in range(2):
                self.slot(("xout", t, half))


def trunk(nc, a):
    F, R = mybir.dt.float32, mybir.dt.float32r
    ALU, ACT, AX = mybir.AluOpType, mybir.ActivationFunctionType, mybir.AxisListType
    plan = Plan()
    ctx = ExitStack()
    with ctx:
        used = [0]
        used[0] = (nc.sbuf_base + 31) // 32 * 32

        def at(name, shape, dt, offset):
            return nc.alloc_sbuf_tensor_at(name, shape, dt, offset=offset, align_bytes=4)

        def sb(name, shape, dt=F):
            t = at(name, shape, dt, used[0])
            used[0] += 4 * math.prod(shape[1:])
            return t

        xT = sb("xT", [128, KD, TOK])
        h_at = used[0]
        h_hi = sb("h_hi", [128, KD, TOK], R)
        h_lo_at = used[0]
        h_lo = sb("h_lo", [128, KD, TOK], R)
        raw = [sb(f"raw{i}", [128, TILE]) for i in range(RING)]
        w_hi = [sb(f"w_hi{i}", [128, TILE], R) for i in range(RING)]
        w_lo = [sb(f"w_lo{i}", [128, TILE], R) for i in range(RING)]
        ones = sb("ones", [128, 128])
        ident = sb("ident", [128, 128])
        rope_c = sb("rope_c", [128, LAT])
        rope_s = sb("rope_s", [128, LAT])
        dft = sb("dft", [128, 2, 128])
        vcol = sb("vcol", [128, DEPTH, NROW])
        wdw = sb("wdw", [128, DEPTH, TAPS, 2])
        ccol = sb("ccol", [128, 3, KD])
        mod = sb("mod", [128, DEPTH, 72, 2])
        amul = sb("amul", [128, DEPTH, 3, KD, 2])
        gate = sb("gate", [128, DEPTH, 3, KD, 2])
        gsub = sb("gsub", [128, DEPTH])
        epsc = sb("epsc", [128, 1])
        neglam = sb("neglam", [128, DEPTH])
        mx = sb("mx", [128, 2, 2])
        nb = sb("nb", [128, 2, 2])
        sums = sb("sums", [128, 2, 2])
        rs = sb("rs", [128, 2, 2])
        M = (used[0] + 31) // 32 * 32
        S3 = 4 * TOK
        hid_hi = at("hid_hi", [128, 2, 2, TOK], R, M)
        hid_lo = at("hid_lo", [128, 2, 2, TOK], R, M + 4 * S3)
        sil = at("sil", [128, 2, TOK], F, M + 8 * S3)
        prod = at("prod", [128, 2, TOK], F, M + 10 * S3)
        sq = at("sq", [128, 2, TOK], F, M + 12 * S3)
        std = at("std", [128, TOK], F, M + 2 * S3)
        rstd = at("rstd", [128, TOK], F, M + 3 * S3)
        tn = at("tn", [128, 2, TOK], F, M + 4 * S3)
        cpad = at("cpad", [128, KD, 32], F, M + 14 * S3)
        side_raw = [at(f"side_raw{i}", [128, 2, 512], F, M + 14 * S3 + 4096 * i) for i in range(2)]
        side_acc = at("side_acc", [128, 2, 512], F, M + 14 * S3 + 8192)
        side_col = at("side_col", [128, 8, 32], F, M + 12 * S3)
        sel = at("sel", [128, 2], F, M + 14 * S3 + 1024)
        lamw = at("lamw", [128, 4], F, M + 14 * S3 + 1024 + 8)
        xnat = at("xnat", [128, TOK // 128, D], F, M)
        vstage = at("vstage", [128, 4, 128], F, M + 24576)
        lamv = at("lamv", [128, DEPTH, 4, HD], F, M + 24576 + 2048)
        lamp = at("lamp", [128, HD], F, M + 24576 + 2048 + 2048)
        part = at("part", [128, 2, 512], F, M + 24576 + 2048 + 2048 + 256)
        kT = at("kT", [128, HEADS, TOK], F, M)
        qT = at("qT", [128, HEADS, TOK], F, M + 4 * S3)
        vN = at("vN", [128, TOK // 128, QKW], F, M + 8 * S3)
        xN = at("xN", [128, TOK // 128, CONVW], F, M + 12 * S3)
        yline = at("yline", [128, 2, LINE], F, M + 14 * S3)
        acc_at = M + 14 * S3 + 4 * 2 * LINE
        acc = at("acc", [128, 2, LINE - 2 * HALF], F, (acc_at + 31) // 32 * 32)
        e0 = at("e0", [128, 3, TOK], F, M + 12 * S3)
        pT = at("pT", [128, 2, TOK // 128, 128], F, M + 15 * S3)
        zT = at("zT", [128, 2, 2, TOK], F, h_lo_at)
        fT = at("fT", [128, 2, TOK], F, h_at)
        csq = at("csq", [128, 2, TOK], F, h_at + 2 * S3)
        cst = at("cst", [128, TOK], F, h_lo_at + 4 * S3)
        crs = at("crs", [128, TOK], F, h_lo_at + 5 * S3)
        cs = at("cs", [128, 2, TOK], F, M + 14 * S3)
        krope = at("krope", [128, LAT], F, M + 14 * S3)
        e1 = at("e1", [128, 2, TOK], F, h_lo_at + 2 * S3)
        qpad = at("qpad", [128, 2, 2, TOK], F, h_at)
        qrope = at("qrope", [128, 2, LAT], F, h_lo_at)
        hsq = at("hsq", [128, HEADS, TOK], F, M)
        hst = at("hst", [128, HEADS, TOK], F, M + 8 * S3)
        onat = at("onat", [128, 2, D], F, M)

        ps = ctx.enter_context(nc.psum_tensor("ps", [128, 8, 512], F))
        pflat = ps[:].rearrange("p b n -> p (b n)")

        def sem(name):
            return ctx.enter_context(nc.semaphore(name))

        products = sem("products")
        bank_free = [sem(f"bank_free{b}") for b in range(8)]
        raw_landed = [sem(f"raw_landed{i}") for i in range(RING)]
        w_hi_done = sem("w_hi_done")
        w_split = sem("w_split")
        const_landed = sem("const_landed")
        x_landed = sem("x_landed")
        out_landed = [sem(f"out_landed{i}") for i in range(2)]
        out_ready = sem("out_ready")
        pool_const = sem("pool_const")
        act_step = sem("act_step")
        dve_step = sem("dve_step")
        cpad_ready = sem("cpad_ready")
        side_landed = [sem(f"side_landed{i}") for i in range(2)]
        side_summed = sem("side_summed")
        side_done = sem("side_done")
        sq_done = sem("sq_done")
        stat_used = sem("stat_used")
        t_done = sem("t_done")
        h_hi_done = sem("h_hi_done")
        h_ready = sem("h_ready")
        hid_hi_done = sem("hid_hi_done")
        hid_ready = sem("hid_ready")
        line_ready = sem("line_ready")
        k_ready = sem("k_ready")
        acc_ready = sem("acc_ready")
        csq_done = sem("csq_done")
        cn_done = sem("cn_done")
        cs_done = sem("cs_done")
        q_ready = sem("q_ready")
        max_done = sem("max_done")
        exp_done = sem("exp_done")
        p_ready = sem("p_ready")
        mix_hi_done = sem("mix_hi_done")
        mix_ready = sem("mix_ready")
        hsq_done = sem("hsq_done")
        ht_done = sem("ht_done")
        y_done = sem("y_done")
        lam_dot = sem("lam_dot")
        lam_exp = sem("lam_exp")
        pad_zeroed = sem("pad_zeroed")
        block = ctx.enter_context(nc.Block())

        def lin(value, key, g, it):
            v = value(key(g))
            if it is None:
                return v
            step = value(key(g + 2)) - v
            return it * step + v

        def number(key):
            return plan.slots[key][0] + 1

        def freed(key):
            return plan.slots[key][2] + 1

        def wait_products(eng, key, g=None, it=None):
            eng.wait_ge(products, number(key) if g is None else lin(number, key, g, it))

        def wait_bank(pe, key, g=None, it=None):
            k0 = key if g is None else key(g)
            use = plan.slots[k0][2]
            if use or it is not None:
                pe.wait_ge(bank_free[plan.slots[k0][1]], use if g is None else lin(lambda k: plan.slots[k][2], key, g, it))

        def wait_freed(eng, key, g=None, it=None):
            k0 = key if g is None else key(g)
            eng.wait_ge(bank_free[plan.slots[k0][1]], freed(key) if g is None else lin(freed, key, g, it))

        def bank_of(key):
            return plan.slots[key][1]

        def pt(key, n=512):
            return ps[:, plan.slots[key][1], 0:n]

        def raw_of(key):
            return raw[plan.raw[key] % RING]

        arrived, total = {}, [0] * RING
        for key in plan.tiles:
            total[plan.raw[key] % RING] += 16 * {"conv": 2, "W": 4}.get(key[0], 1)
            arrived[key] = total[plan.raw[key] % RING]

        def wait_landed(eng, key, g=None, it=None):
            k0 = key if g is None else key(g)
            eng.wait_ge(raw_landed[plan.raw[k0] % RING],
                        arrived[key] if g is None else lin(arrived.__getitem__, key, g, it))

        def ring(key):
            return plan.split[key] % RING

        split_keys = [k for k in plan.tiles if k in plan.split]

        def hcount(q, j, s):
            return 8 * sum(len(segs_of(x)) for x in range(q)) + j * len(segs_of(q)) + s + 1

        NORM_OF = (0, 2, 3, 5)
        side_list = [(f, g) for f in range(2 * DEPTH) for g in SIDE_GROUPS[f]]

        def side_number(key):
            return side_list.index(key)

        consts = []

        def load_sizes(key):
            dst = raw_of(key)
            k = key[0]
            if k == "ada":
                _, l, b, half = key
                return [(a["w_ada"][l, 512 * half:512 * half + 512, 512 * b:512 * b + 512]
                         .rearrange("(k p) n -> p k n", p=128), dst[:].rearrange("p (k n) -> p k n", k=4))]
            if k in ("C", "S"):
                src = a["dft_cos"] if k == "C" else a["dft_sin"]
                return [(src.rearrange("(k p) n -> p k n", p=128), dst[:].rearrange("p (k n) -> p k n", k=4))]
            l = key[1]
            if k == "W":
                out = []
                for i, src in enumerate((a["w_pw"][l, :, :], a["w_fourier"][l, :, :], a["dft_cos_ctx"], a["dft_sin_ctx"])):
                    out.append((src.rearrange("(k p) n -> p k n", p=128),
                                dst[:, 512 * i:512 * i + 512].rearrange("p (k n) -> p k n", k=2)))
                return out
            d8 = dst[:].rearrange("p (k n) -> p k n", k=KD)
            if k == "conv":
                c = key[2]
                out = []
                for i, at_ in enumerate((1536 + 128 * c, 1536 + 256 + 128 * c)):
                    out.append((a["w_in"][l, :, at_:at_ + 128].rearrange("(k p) n -> p k n", p=128),
                                d8[:, :, 128 * i:128 * i + 128]))
                return out
            if k == "out":
                at_, src = 256 * key[2], a["w_out"]
            else:
                at_ = {"four": 2048, "V": 1024, "K": 512, "Q": 0}[k] + (256 * key[2] if k != "four" else 0)
                src = a["w_in"]
            return [(src[l, :, at_:at_ + 256].rearrange("(k p) n -> p k n", p=128), d8)]

        def ffn_source(f, k, col):
            l, which = f // 2, f % 2 + 1
            if k == "D":
                return a[f"w_ffn{which}_down"][l, bass.ds(col, GW), :].rearrange("(c p) n -> p c n", p=128)
            name = f"w_ffn{which}_{'gate' if k == 'G' else 'up'}"
            return a[name][l, :, bass.ds(col, GW)].rearrange("(k p) n -> p k n", p=128)

        @block.sync
        def _(sp):
            for src, dst in ((a["vec0"], vstage[0:NROW, 0, :]), (a["vec1"], vstage[0:NROW, 1, :]),
                             (a["vecw"], vstage[0:4 * TAPS, 2, :]), (a["vecc"], vstage[0:3 * KD, 3, :])):
                sp.dma_start(dst, src).then_inc(const_landed, 16)
            for dst, name in ((ident[:], "ident"), (sel[:], "sel"), (rope_c[:], "rope_cos"), (rope_s[:], "rope_sin"),
                              (dft[:], "dft_groups")):
                sp.dma_start(dst, a[name]).then_inc(const_landed, 16)
            sp.dma_start(lamv[:].rearrange("p l i n -> p (l i n)"), a["lams"].broadcast_to((128, DEPTH * 4 * HD))).then_inc(const_landed, 16)
            for t in range(TOK // 128):
                src = a["x"][0, 128 * t:128 * t + 128, :] if t < 4 else a["ctx"][0, 128 * (t - 4):128 * (t - 4) + 128, :]
                sp.dma_start(xnat[:, t, :], src).then_inc(x_landed, 16)

            def release(key):
                t = plan.raw[key] - RING
                if t < 0:
                    return
                old = plan.tiles[t]
                if old in plan.split:
                    sp.wait_ge(w_split, plan.split[old] + 1)
                else:
                    wait_products(sp, plan.lastuse[old])

            def load(key):
                release(key)
                if key[0] in "GUD":
                    pairs = [(ffn_source(key[1], key[0], GW * key[2]), ffn_dst(key))]
                else:
                    pairs = load_sizes(key)
                for i, (src, dst) in enumerate(pairs):
                    sp.dma_start(dst, src).then_inc(raw_landed[plan.raw[key] % RING], 16)

            def ffn_dst(key):
                return raw_of(key)[:].rearrange("p (k n) -> p k n", k=2 if key[0] == "D" else KD)

            def in_loop(f, k, g, it):
                key = (k, f, g)
                old, later = plan.tiles[plan.raw[key] - RING], plan.tiles[plan.raw[(k, f, g + 2)] - RING]
                was, step = plan.split[old] + 1, plan.split[later] - plan.split[old]
                sp.wait_ge(w_split, it * step + was)
                sp.dma_start(ffn_dst(key), ffn_source(f, k, it * (2 * GW) + GW * g))\
                    .then_inc(raw_landed[plan.raw[key] % RING], 16)

            def side(f, g, quarters, it=None):
                if g not in SIDE_GROUPS[f]:
                    return
                l, b = SIDE_GROUPS[f][g]
                n = side_number((f, g))
                for q in quarters:
                    done = 16 * n + 4 * (q - 1)
                    if it is None:
                        if done > 0:
                            sp.wait_ge(side_summed, done)
                        src = a["w_ada"][l, 256 * q:256 * q + 256, 512 * b:512 * b + 512]
                    else:
                        sp.wait_ge(side_summed, it * 32 + done)
                        src = a["w_ada"][l, 256 * q:256 * q + 256, bass.ds(it * 1024 + 512 * b, 512)]
                    sp.dma_start(side_raw[q % 2][:], src.rearrange("(k p) n -> p k n", p=128)).then_inc(side_landed[q % 2], 16)

            order = list(plan.tiles)
            i = 0
            while i < len(order):
                key = order[i]
                if key[0] == "G" and key[2] == 3:
                    f = key[1]
                    with sp.Fori(0, 3) as it:
                        for g in (3, 4):
                            in_loop(f, "G", g, it)
                            in_loop(f, "U", g, it)
                            in_loop(f, "D", g - 1, it)
                            side(f, g - 1, (2, 3), it)
                            side(f, g, (0, 1), it)
                    i += 18
                    continue
                load(key)
                i += 1
                if key[0] == "U" and key[2] == 0:
                    f = key[1]
                    if f == 0:
                        wait_products(sp, ("adaT", 0, FIRST_BLOCKS[-1]))
                    elif f == 1:
                        wait_products(sp, ("O", 0, HEADS - 1, len(mix_segs(0)) - 1))
                    side(f, 0, (0, 1))
                if key[0] == "D":
                    f, g = key[1], key[2]
                    side(f, g, (2, 3))
                    side(f, g + 1, (0, 1))
            for t in range(LAT // 128):
                wait_freed(sp, ("xout", t, 1))
                sp.dma_start(a["out"][0, 128 * t:128 * t + 128, :], onat[:, t % 2, :]).then_inc(out_landed[t % 2], 16)
            for i in range(2):
                sp.wait_ge(out_landed[i], 16 * (LAT // 128 // 2))

        @block.gpsimd
        def _(pool):
            nc.gpsimd.memset(ones[:], 1.0).then_inc(pool_const, 1)
            nc.gpsimd.memset(epsc[:], EPS).then_inc(pool_const, 1)

        mm = nc.tensor.matmul

        def mm3(out, wh, wl, xh, xl, start, stop):
            mm(out, wh, xh, start=start, stop=False)
            mm(out, wh, xl, start=False, stop=False)
            return mm(out, wl, xh, start=False, stop=stop)

        def wk(key, k):
            i = ring(key)
            return (w_hi[i][:].rearrange("p (k n) -> p k n", k=k), w_lo[i][:].rearrange("p (k n) -> p k n", k=k))

        @block.tensor
        def _(pe):
            def wait_h(q, j, s):
                pe.wait_ge(h_ready, hcount(q, j, s))

            def wait_split(key, g=None, it=None):
                pe.wait_ge(w_split, (plan.split[key] + 1) if g is None else lin(lambda k: plan.split[k] + 1, key, g, it))

            def norm(q):
                ss = segs_of(q)
                for s in range(len(ss)):
                    wait_bank(pe, ("stat", q, s))
                n0 = 8 * sum(len(segs_of(x)) for x in range(q))
                for j in range(KD):
                    for s, (o, n) in enumerate(ss):
                        pe.wait_ge(sq_done, n0 + j * len(ss) + s + 1)
                        last = mm(pt(("stat", q, s), n), ones[:], sq[:, j % 2, o:o + n], start=(j == 0), stop=(j == KD - 1))
                        last.then_inc(products if j == KD - 1 else stat_used, 1)

            def ada(l):
                pe.wait_ge(cpad_ready, 4)
                for n, b in enumerate(FIRST_BLOCKS):
                    key = ("ada", l, b)
                    wait_bank(pe, key)
                    for k in range(KD):
                        if k % 4 == 0:
                            wait_landed(pe, key + (k // 4,))
                        q = k % 4
                        src = raw_of(key + (k // 4,))[:].rearrange("p (k n) -> p k n", k=4)
                        last = mm(ps[32 * q:32 * q + 32, bank_of(key), :], cpad[:, k, :], src[:, q, :],
                                  start=(k < 4), stop=(k >= 4), skip_group_check=True)
                    last.then_inc(products, 1)
                    if n:
                        turn(l, n - 1)
                turn(l, len(FIRST_BLOCKS) - 1)

            def turn(l, n):
                wait_freed(pe, ("ada", l, FIRST_BLOCKS[n]))
                key = ("adaT", l, FIRST_BLOCKS[n])
                wait_bank(pe, key)
                for i in range(4):
                    last = mm(ps[:, bank_of(key), 2 * i:2 * i + 2], part[:, n % 2, 128 * i:128 * i + 128], sel[:],
                              start=True, stop=True, skip_group_check=True)
                last.then_inc(products, 1)

            def ffn(f):
                q = NORM_OF[f]
                ss = segs_of(q)

                def gate_up(g, it=None):
                    both = [(w, s) for w in "gu" for s in range(len(ss))]
                    for c, outs in [(c, o) for c in range(2) for o in ([both] if g == 0 else [both[:len(ss)], both[len(ss):]])]:
                        if c == 0:
                            wait_split(lambda x: ("G" if outs[-1][0] == "g" else "U", f, x), g, it)
                        for w, s in outs:
                            wait_bank(pe, lambda x: (w, f, x, c, s), g, it)
                        for k in range(KD):
                            for w, s in outs:
                                o, n = ss[s]
                                wh, wl = wk(("G" if w == "g" else "U", f, g), KD)
                                if g == 0 and c == 0 and w == "g":
                                    wait_h(q, k, s)
                                last = mm3(pt((w, f, g, c, s), n), wh[:, k, 128 * c:128 * c + 128],
                                           wl[:, k, 128 * c:128 * c + 128], h_hi[:, k, o:o + n], h_lo[:, k, o:o + n],
                                           k == 0, k == KD - 1)
                                if k == KD - 1:
                                    last.then_inc(products, 1)

                def down(g, it=None):
                    wait_split(lambda x: ("D", f, x), g, it)
                    n0 = 2 * NG * f + 2 * g + 2
                    pe.wait_ge(hid_ready, n0 if it is None else it * 4 + n0)
                    wh, wl = wk(("D", f, g), 2)
                    for j in range(KD):
                        for s, (o, n) in enumerate(ss):
                            wait_bank(pe, lambda x: ("d", f, x, j, s), g, it)
                            for c in range(2):
                                last = mm3(pt(("d", f, g, j, s), n), wh[:, c, 128 * j:128 * j + 128],
                                           wl[:, c, 128 * j:128 * j + 128], hid_hi[:, g % 2, c, o:o + n],
                                           hid_lo[:, g % 2, c, o:o + n], c == 0, c == 1)
                            last.then_inc(products, 1)
                        if j == SIDE_AT:
                            side(g + 1, it)

                def side(g, it=None):
                    if g not in SIDE_GROUPS[f]:
                        return
                    key = lambda x: ("side", f, x)
                    n16 = 16 * (side_number((f, g)) + 1)
                    pe.wait_ge(side_summed, n16 if it is None else it * 32 + n16)
                    wait_bank(pe, key, g, it)
                    rows = side_acc[:].rearrange("p v (j q n) -> p q (v j) n", q=4, n=32)
                    for q in range(4):
                        last = mm(ps[32 * q:32 * q + 32, bank_of(key(g)), 0:256].rearrange("p (j n) -> p j n", n=32),
                                  ones[:, 0:32], rows[:, q], start=True, stop=True, skip_group_check=True)
                    last.then_inc(products, 1)

                gate_up(0)
                side(0)
                with pe.Fori(0, (NG - 3) // 2) as it:
                    gate_up(1, it)
                    down(0, it)
                    gate_up(2, it)
                    down(1, it)
                for g in (NG - 2, NG - 1):
                    gate_up(g)
                    down(g - 1)
                down(NG - 1)

            def columns(key, outs, q):
                wait_split(key)
                wh, wl = wk(key, KD)
                for slot, _, _ in outs:
                    wait_bank(pe, slot)
                for k in range(KD):
                    for slot, col, (o, n) in outs:
                        if key[0] == "conv":
                            wait_h(q, k, 1)
                        last = mm3(pt(slot, n), wh[:, k, col:col + 128], wl[:, k, col:col + 128],
                                   h_hi[:, k, o:o + n], h_lo[:, k, o:o + n], k == 0, k == KD - 1)
                        if k == KD - 1:
                            last.then_inc(products, 1)

            def rows(key, slots):
                wait_split(key)
                wh, wl = wk(key, KD)
                for t, slot in enumerate(slots):
                    wait_bank(pe, slot)
                    for k in range(KD):
                        last = mm3(pt(slot, 256), h_hi[:, k, 128 * t:128 * t + 128], h_lo[:, k, 128 * t:128 * t + 128],
                                   wh[:, k, :], wl[:, k, :], k == 0, k == KD - 1)
                    last.then_inc(products, 1)

            def mix(l):
                ms = mix_segs(l)
                ns = len(ms)
                q = 3 * l + 1
                for c in range(2):
                    columns(("conv", l, c), [(("conv" + w, l, c, s), 128 if w == "g" else 0, ms[s])
                                             for w in "ga" for s in range(ns)], q)
                rows(("four", l), [("X", l, t) for t in range(sum(n for _, n in ms) // 128)])
                for v in range(2):
                    rows(("V", l, v), [("V", l, v, t) for t in range(TOK // 128)])
                for w, ss in (("K", BOTH), ("Q", ms)):
                    for v in range(2):
                        columns((w, l, v), [((w, l, 2 * v + c, s), 128 * c, ss[s]) for c in range(2)
                                            for s in range(len(ss))], q)
                fourier(l)
                conv_tail(l)
                attention(l)
                for h in range(HEADS):
                    for s, (o, n) in enumerate(ms):
                        key = ("hn", l, h, s)
                        wait_bank(pe, key)
                        pe.wait_ge(hsq_done, HEADS * sum(len(mix_segs(x)) for x in range(l)) + h * ns + s + 1)
                        mm(pt(key, n), ones[:], hsq[:, h, o:o + n], start=True, stop=True).then_inc(products, 1)
                for v in range(4):
                    key = ("out", l, v)
                    wait_split(key)
                    wh, wl = wk(key, KD)
                    outs = [(("out", l, 2 * v + c, s), 128 * c, s) for c in range(2) for s in range(ns)]
                    for slot, _, _ in outs:
                        wait_bank(pe, slot)
                    order = (6, 7, 4, 5, 0, 1, 2, 3)
                    for i, k in enumerate(order):
                        for slot, col, s in outs:
                            o, n = ms[s]
                            if v == 0 and k >= 6:
                                wait_freed(pe, ("Fo", l, k - 6, s))
                            elif v == 0 and k >= 4:
                                wait_freed(pe, ("pw", l, k - 4, s))
                            elif v == 0:
                                pe.wait_ge(mix_ready, HEADS * sum(len(mix_segs(x)) for x in range(l)) + k * ns + s + 1)
                            last = mm3(pt(slot, n), wh[:, k, col:col + 128], wl[:, k, col:col + 128],
                                       h_hi[:, k, o:o + n], h_lo[:, k, o:o + n], i == 0, i == KD - 1)
                            if i == KD - 1:
                                last.then_inc(products, 1)

            def fourier(l):
                ms = mix_segs(l)
                small = raw_of(("W", l))[:].rearrange("p (i k n) -> p i k n", i=4, k=2)
                wait_landed(pe, ("C", l))
                wait_landed(pe, ("S", l))
                wait_landed(pe, ("W", l))
                wait_freed(pe, ("X", l, sum(n for _, n in ms) // 128 - 1))
                wait_freed(pe, ("X", l, sum(n for _, n in ms) // 128 - 2))
                for j in range(2):
                    for w in "CS":
                        big = raw_of((w, l))[:].rearrange("p (k n) -> p k n", k=4)
                        for s, (o, n) in enumerate(ms):
                            key = ("Z", l, j, w, s)
                            wait_bank(pe, key)
                            nk = n // 128
                            for k in range(nk):
                                table = big[:, k, :] if s == 0 else small[:, 2 if w == "C" else 3, k, :]
                                last = mm(pt(key, n), xN[:, o // 128 + k, 128 * j:128 * j + 128], table,
                                          start=(k == 0), stop=(k == nk - 1))
                            last.then_inc(products, 1)
                for j in range(2):
                    for s, (o, n) in enumerate(ms):
                        key = ("F", l, j, s)
                        wait_bank(pe, key)
                        for i, w in enumerate("CS"):
                            wait_freed(pe, ("Z", l, j, w, s))
                            last = mm(pt(key, n), dft[:, i, :], zT[:, j, i, o:o + n], start=(i == 0), stop=(i == 1))
                        last.then_inc(products, 1)
                for p in range(2):
                    for s, (o, n) in enumerate(ms):
                        key = ("Fo", l, p, s)
                        wait_bank(pe, key)
                        for j in range(2):
                            wait_freed(pe, ("F", l, j, s))
                            last = mm(pt(key, n), small[:, 1, j, 128 * p:128 * p + 128], fT[:, j, o:o + n],
                                      start=(j == 0), stop=(j == 1))
                        last.then_inc(products, 1)

            def conv_tail(l):
                ms = mix_segs(l)
                small = raw_of(("W", l))[:].rearrange("p (i k n) -> p i k n", i=4, k=2)
                ns = len(ms)
                pe.wait_ge(acc_ready, 2 * (l + 1))
                for s, (o, n) in enumerate(ms):
                    key = ("mean", l, s)
                    wait_bank(pe, key)
                    ao = 0 if s == 0 else C_CTX - HALF
                    for c in range(2):
                        last = mm(pt(key, n), ones[:], acc[:, c, ao:ao + n], start=(c == 0), stop=(c == 1))
                    last.then_inc(products, 1)
                before = 2 * sum(len(mix_segs(x)) for x in range(l))
                for s, (o, n) in enumerate(ms):
                    key = ("var", l, s)
                    wait_bank(pe, key)
                    pe.wait_ge(csq_done, before + 2 * s + 2)
                    for c in range(2):
                        last = mm(pt(key, n), ones[:], csq[:, c, o:o + n], start=(c == 0), stop=(c == 1))
                    last.then_inc(products, 1)
                for p in range(2):
                    for s, (o, n) in enumerate(ms):
                        key = ("pw", l, p, s)
                        wait_bank(pe, key)
                        pe.wait_ge(cs_done, before + 2 * s + 2)
                        for c in range(2):
                            last = mm(pt(key, n), small[:, 0, c, 128 * p:128 * p + 128], cs[:, c, o:o + n],
                                      start=(c == 0), stop=(c == 1))
                        last.then_inc(products, 1)

            def attention(l):
                us = units_of(l)
                ms = mix_segs(l)
                e_before = 2 * sum(len(units_of(x)) for x in range(l))
                u_before = e_before // 2
                for b in range(6):
                    pe.wait_ge(bank_free[b], plan.before_att[l][b])
                for i in range(len(us) + 3):
                    if i < len(us):
                        h, s, t = us[i]
                        if t == 0 and s == 0:
                            pe.wait_ge(q_ready, HEADS * l + h + 1)
                            pe.wait_ge(k_ready, HEADS * l + h + 1)
                            wait_freed(pe, ("K", l, h, 1))
                        if i >= 2:
                            pe.wait_ge(exp_done, e_before + 2 * (i - 1))
                        at0 = 1536 * (i % 2)
                        o = ms[s][0] + 128 * t
                        if s == 0:
                            parts = ((0, 0, 0, 512), (0, 512, 512, 256), (1, 768, 512, 256), (1, 1024, 0, 512))
                        else:
                            parts = ((0, 0, 512, 256), (1, 256, 512, 256))
                        for st, po, ko, n in parts:
                            last = mm(pflat[:, at0 + po:at0 + po + n], qpad[:, h % 2, st, o:o + 128],
                                      kT[:, h, ko:ko + n], start=True, stop=True, skip_group_check=True)
                        last.then_inc(products, 1)

                    def turn_p(half):
                        u = i - 2
                        h, s, t = us[u]
                        key = ("T", l, u, half)
                        wait_bank(pe, key)
                        if half == 0:
                            pe.wait_ge(p_ready, u_before + u + 1)
                        ks = range(0, 4) if (s == 0 and half == 0) else range(4, 6) if s == 0 else range(2)
                        for n, k in enumerate(ks):
                            last = nc.tensor.transpose(ps[:, 6, 128 * n:128 * n + 128], e0[:, u % 3, 128 * k:128 * k + 128], ident[:])
                        last.then_inc(products, 1)

                    if 0 <= i - 2 < len(us):
                        turn_p(0)
                    if 0 <= i - 3 < len(us):
                        u = i - 3
                        h, s, t = us[u]
                        key = ("O", l, h, s)
                        if t == 0:
                            wait_bank(pe, key)
                        wait_freed(pe, ("T", l, u, 1 if s == 0 else 0))
                        ks = range(6) if s == 0 else range(4, 6)
                        for k in ks:
                            last = mm(ps[:, 7, 128 * t:128 * t + 128], vN[:, k, 128 * h:128 * h + 128],
                                      pT[:, u % 2, k if s == 0 else k - 4, :], start=(k == ks[0]), stop=(k == 5),
                                      skip_group_check=True)
                        if t == ms[s][1] // 128 - 1:
                            last.then_inc(products, 1)
                    if 0 <= i - 2 < len(us) and us[i - 2][1] == 0:
                        turn_p(1)
                pe.wait_ge(exp_done, e_before + 2 * len(us))

            pe.wait_ge(const_landed, 16 * N_CONST)
            for i, n in enumerate((NROW, NROW, 2 * 2 * TAPS, 3 * KD)):
                nc.tensor.transpose(ps[:, bank_of(("vec", i)), 0:n], vstage[0:n, i, :], ident[0:n, 0:n]).then_inc(products, 1)
            pe.wait_ge(x_landed, 16 * (TOK // 128))
            for s, (o, n) in enumerate(BOTH):
                for j in range(KD):
                    key = ("xin", s, j)
                    wait_bank(pe, key)
                    for t in range(n // 128):
                        last = nc.tensor.transpose(ps[:, bank_of(key), 128 * t:128 * t + 128],
                                                   xnat[:, o // 128 + t, 128 * j:128 * j + 128], ident[:])
                    last.then_inc(products, 1)
            pe.wait_ge(pool_const, 2)
            ada(0)
            for l in range(DEPTH):
                norm(3 * l)
                ffn(2 * l)
                norm(3 * l + 1)
                mix(l)
                norm(3 * l + 2)
                ffn(2 * l + 1)
            norm(3 * DEPTH)
            pe.wait_ge(y_done, KD)
            for t in range(LAT // 128):
                for half in range(2):
                    key = ("xout", t, half)
                    wait_bank(pe, key)
                    for i in range(4):
                        last = nc.tensor.transpose(ps[:, bank_of(key), 128 * i:128 * i + 128],
                                                   xT[:, 4 * half + i, 128 * t:128 * t + 128], ident[:])
                    last.then_inc(products, 1)

        act_fn = nc.scalar.activation

        def x_written(q, j, s):
            if q == 0:
                return ("xin", s, j)
            return ("out", (q - 2) // 3, j, s) if q % 3 == 2 else ("d", {1: 0, 3: 1, 4: 2, 6: 3}[q], NG - 1, j, s)

        @block.scalar
        def _(act):
            steps = [0]

            def split(key, g=None, it=None):
                k0 = key if g is None else key(g)
                wait_landed(act, key, g, it)
                s = plan.split[k0]
                if s >= RING:
                    old = plan.lastuse[split_keys[s - RING]]
                    if g is None:
                        wait_products(act, old)
                    else:
                        step = number(plan.lastuse[split_keys[plan.split[key(g + 2)] - RING]]) - number(old)
                        act.wait_ge(products, number(old) if it is None else it * step + number(old))
                act_fn(w_hi[s % RING][:], raw_of(k0)[:], ACT.Copy).then_inc(w_hi_done, 1)

            def norm(q):
                ss = segs_of(q)
                before = 7 * sum(len(segs_of(x)) for x in range(q))
                for j in range(KD):
                    for s, (o, n) in enumerate(ss):
                        wait_freed(act, x_written(q, j, s))
                        if j >= 2:
                            act.wait_ge(stat_used, before + (j - 2) * len(ss) + s + 1)
                        act_fn(sq[:, j % 2, o:o + n], xT[:, j, o:o + n], ACT.Square).then_inc(sq_done, 1)
                for s, (o, n) in enumerate(ss):
                    key = ("stat", q, s)
                    wait_products(act, key)
                    act_fn(std[:, o:o + n], pt(key, n), ACT.Sqrt, bias=epsc[:], scale=1.0 / D)\
                        .then_inc(bank_free[bank_of(key)], 1)
                if q == 3 * DEPTH:
                    return
                i = q % 3
                for j in range(KD):
                    for s, (o, n) in enumerate(ss):
                        act.wait_ge(t_done, hcount(q, j, s))
                        act_fn(h_hi[:, j, o:o + n], tn[:, j % 2, o:o + n], ACT.Identity,
                               bias=mod[:, q // 3, 24 * i + j, s:s + 1], scale=1.0).then_inc(h_hi_done, 1)

            def ada(l):
                act.wait_ge(pad_zeroed, l + 1)
                for v in range(2):
                    act_fn(cpad[:, :, v], ccol[:, v, :], ACT.Silu).then_inc(cpad_ready, 1)
                    act_fn(ccol[:, v, :], ccol[:, v, :], ACT.Silu).then_inc(cpad_ready, 1)
                for n, b in enumerate(FIRST_BLOCKS):
                    key = ("ada", l, b)
                    wait_products(act, key)
                    if n >= 2:
                        wait_products(act, ("adaT", l, FIRST_BLOCKS[n - 2]))
                    act_fn(part[:, n % 2, :], pt(key), ACT.Copy).then_inc(bank_free[bank_of(key)], 1)

            def ffn(f, nxt):
                ss = segs_of(NORM_OF[f])

                def hidden(g, it=None):
                    for c in range(2):
                        for s, (o, n) in enumerate(ss):
                            wait_products(act, lambda x: ("g", f, x, c, s), g, it)
                            act_fn(sil[:, c, o:o + n], pt(("g", f, g, c, s), n), ACT.Silu)\
                                .then_inc(bank_free[bank_of(("g", f, g, c, s))], 1)
                        wait_freed(act, lambda x: ("u", f, x, c, len(ss) - 1), g, it)
                        last_o = ss[-1][0] + ss[-1][1]
                        act_fn(hid_hi[:, g % 2, c, 0:last_o], prod[:, c, 0:last_o], ACT.Copy).then_inc(hid_hi_done, 1)

                def groups(g, it=None):
                    hidden(g, it)
                    split(lambda x: ("G", f, x), g + 1, it)
                    split(lambda x: ("U", f, x), g + 1, it)
                    split(lambda x: ("D", f, x), g, it)

                split(("G", f, 1))
                hidden(0)
                split(("U", f, 1))
                split(("D", f, 0))
                with act.Fori(0, (NG - 3) // 2) as it:
                    groups(1, it)
                    groups(2, it)
                hidden(NG - 2)
                split(("G", f, NG - 1))
                split(("U", f, NG - 1))
                split(("D", f, NG - 2))
                hidden(NG - 1)
                split(("D", f, NG - 1))
                for key in nxt:
                    split(key)

            def mix(l):
                ms = mix_segs(l)
                ns = len(ms)

                def copy(key, dst, n):
                    wait_products(act, key)
                    act_fn(dst, pt(key, n), ACT.Copy).then_inc(bank_free[bank_of(key)], 1)

                rest = iter([("V", l, 0), ("V", l, 1), ("K", l, 0), ("K", l, 1), ("Q", l, 0), ("Q", l, 1),
                             ("out", l, 0), ("out", l, 1), ("out", l, 2), ("out", l, 3)])
                for c in range(2):
                    for s, (o, n) in enumerate(ms):
                        key = ("convg", l, c, s)
                        wait_products(act, key)
                        at0 = (C_LAT, C_CTX)[s]
                        act_fn(yline[:, c, at0:at0 + n], pt(key, n), ACT.Sigmoid).then_inc(bank_free[bank_of(key)], 1)
                    split(next(rest))
                for t in range(sum(n for _, n in ms) // 128):
                    copy(("X", l, t), xN[:, t, :], 256)
                split(next(rest))
                for v in range(2):
                    for t in range(TOK // 128):
                        copy(("V", l, v, t), vN[:, t, 256 * v:256 * v + 256], 256)
                    split(next(rest))
                for h in range(HEADS):
                    copy(("K", l, h, 1), kT[:, h, LAT:TOK], CTX)
                    if h == 1:
                        split(next(rest))
                for h in range(HEADS):
                    for s, (o, n) in enumerate(ms):
                        copy(("Q", l, h, s), qT[:, h, o:o + n], n)
                for j in range(2):
                    for i, w in enumerate("CS"):
                        for s, (o, n) in enumerate(ms):
                            copy(("Z", l, j, w, s), zT[:, j, i, o:o + n], n)
                for j in range(2):
                    for s, (o, n) in enumerate(ms):
                        copy(("F", l, j, s), fT[:, j, o:o + n], n)

                def biased(kind, name, chunk0):
                    for p in range(2):
                        for s, (o, n) in enumerate(ms):
                            key = (kind, l, p, s)
                            wait_products(act, key)
                            col = ROW[name][0] + p
                            act_fn(h_hi[:, chunk0 + p, o:o + n], pt(key, n), ACT.Identity,
                                   bias=vcol[:, l, col:col + 1], scale=1.0).then_inc(mix_hi_done, 1)

                biased("Fo", "b_fourier", 6)
                before = 2 * sum(len(mix_segs(x)) for x in range(l))
                for s, (o, n) in enumerate(ms):
                    wait_freed(act, ("mean", l, s))
                    ao = 0 if s == 0 else C_CTX - HALF
                    for c in range(2):
                        act_fn(csq[:, c, o:o + n], acc[:, c, ao:ao + n], ACT.Square).then_inc(csq_done, 1)
                for s, (o, n) in enumerate(ms):
                    key = ("var", l, s)
                    wait_products(act, key)
                    act_fn(cst[:, o:o + n], pt(key, n), ACT.Sqrt, bias=epsc[:], scale=1.0 / CONVW)\
                        .then_inc(bank_free[bank_of(key)], 1)
                g0, b0 = ROW["g_conv_ln"][0], ROW["b_conv_ln"][0]
                for s, (o, n) in enumerate(ms):
                    ao = 0 if s == 0 else C_CTX - HALF
                    for c in range(2):
                        act.wait_ge(cn_done, before + 2 * s + c + 1)
                        act_fn(cs[:, c, o:o + n], acc[:, c, ao:ao + n], ACT.Silu, bias=vcol[:, l, b0 + c:b0 + c + 1],
                               scale=vcol[:, l, g0 + c:g0 + c + 1]).then_inc(cs_done, 1)
                biased("pw", "b_pw", 4)
                us = units_of(l)
                u_before = sum(len(units_of(x)) for x in range(l))
                for i in range(len(us) + 3):
                    if 0 <= i - 2 < len(us):
                        u = i - 2
                        h, s, t = us[u]
                        for half in range(2 if s == 0 else 1):
                            key = ("T", l, u, half)
                            wait_products(act, key)
                            k0, n = (4, 2) if half else (0, 4 if s == 0 else 2)
                            act_fn(pT[:, u % 2, k0:k0 + n, :], ps[:, 6, 0:128 * n].rearrange("p (k n) -> p k n", k=n),
                                   ACT.Copy).then_inc(bank_free[6], 1)
                    if i < len(us):
                        h, s, t = us[i]
                        act.wait_ge(max_done, u_before + i + 1)
                        at0, n = 1536 * (i % 2), TOK if s == 0 else CTX
                        for st, dst in ((0, e0[:, i % 3, 0:n]), (1, e1[:, i % 2, 0:n])):
                            act_fn(dst, pflat[:, at0 + n * st:at0 + n * st + n], ACT.Exp, bias=nb[:, i % 2, st:st + 1],
                                   scale=HD ** -0.5, accum_out=sums[:, i % 2, st:st + 1]).then_inc(exp_done, 1)
                    if 0 <= i - 3 < len(us):
                        h, s, t = us[i - 3]
                        if t == ms[s][1] // 128 - 1:
                            o, n = ms[s]
                            copy(("O", l, h, s), qT[:, h, o:o + n], n)
                    if i in (4, 6, 8):
                        split(next(rest))
                for h in range(HEADS):
                    for s, (o, n) in enumerate(ms):
                        if h == HEADS - 1 or h == 0:
                            wait_freed(act, ("O", l, h, s))
                        act_fn(hsq[:, h, o:o + n], qT[:, h, o:o + n], ACT.Square).then_inc(hsq_done, 1)
                for h in range(HEADS):
                    for s, (o, n) in enumerate(ms):
                        key = ("hn", l, h, s)
                        wait_products(act, key)
                        act_fn(hst[:, h, o:o + n], pt(key, n), ACT.Sqrt, bias=epsc[:], scale=1.0 / 128)\
                            .then_inc(bank_free[bank_of(key)], 1)
                hbefore = HEADS * sum(len(mix_segs(x)) for x in range(l))
                for h in range(HEADS):
                    for s, (o, n) in enumerate(ms):
                        act.wait_ge(ht_done, hbefore + h * ns + s + 1)
                        act_fn(h_hi[:, h, o:o + n], qT[:, h, o:o + n], ACT.Copy).then_inc(mix_hi_done, 1)
                split(next(rest))
                split(("G", 2 * l + 1, 0))
                split(("U", 2 * l + 1, 0))

            for i, (n, dst) in enumerate(((NROW, vcol[:, 0, :]), (NROW, vcol[:, 1, :]),
                                          (4 * TAPS, wdw[:].rearrange("p l t c -> p (l t c)")),
                                          (3 * KD, ccol[:].rearrange("p i k -> p (i k)")))):
                wait_products(act, ("vec", i))
                act_fn(dst, ps[:, bank_of(("vec", i)), 0:n], ACT.Copy).then_inc(bank_free[bank_of(("vec", i))], 1)
            act.wait_ge(pool_const, 2)
            wait_freed(act, ("vec", 3))
            act.wait_ge(lam_dot, 1)
            act_fn(lamw[:, 0:2 * DEPTH], lamw[:, 0:2 * DEPTH], ACT.Exp).then_inc(lam_exp, 1)
            ada(0)
            split(("G", 0, 0))
            split(("U", 0, 0))
            for l in range(DEPTH):
                norm(3 * l)
                ffn(2 * l, [("conv", l, 0), ("conv", l, 1)])
                split(("four", l))
                norm(3 * l + 1)
                mix(l)
                norm(3 * l + 2)
                ffn(2 * l + 1, [("G", 2 * l + 2, 0), ("U", 2 * l + 2, 0)] if l < DEPTH - 1 else [])
            norm(3 * DEPTH)
            for t in range(LAT // 128):
                if t >= 2:
                    act.wait_ge(out_landed[t % 2], 16 * (t // 2))
                for half in range(2):
                    key = ("xout", t, half)
                    wait_products(act, key)
                    act_fn(onat[:, t % 2, 512 * half:512 * half + 512], pt(key), ACT.Copy)\
                        .then_inc(bank_free[bank_of(key)], 1)

        dve_ = nc.vector
        tt, stt = dve_.tensor_tensor, dve_.scalar_tensor_tensor

        @block.vector
        def _(dve):
            steps = [0]

            def step(ins):
                ins.then_inc(dve_step, 1)
                steps[0] += 1
                return steps[0]

            def settle(back=0):
                if steps[0] - back > 0:
                    dve.wait_ge(dve_step, steps[0] - back)

            def split(key, g=None, it=None):
                k0 = key if g is None else key(g)
                s = plan.split[k0]
                dve.wait_ge(w_hi_done, s + 1 if g is None else lin(lambda k: plan.split[k] + 1, key, g, it))
                tt(w_lo[s % RING][:], raw_of(k0)[:], w_hi[s % RING][:].bitcast(F), ALU.subtract).then_inc(w_split, 1)

            def norm(q):
                ss = segs_of(q)
                for s, (o, n) in enumerate(ss):
                    wait_freed(dve, ("stat", q, s))
                    step(dve_.reciprocal(rstd[:, o:o + n], std[:, o:o + n]))
                settle()
                if q == 3 * DEPTH:
                    for j in range(KD):
                        stt(out=xT[:, j, 0:LAT], in0=xT[:, j, 0:LAT], scalar=ccol[:, 2, j:j + 1], in1=rstd[:, 0:LAT],
                            op0=ALU.mult, op1=ALU.mult).then_inc(y_done, 1)
                    return
                i = q % 3

                def low(j):
                    for s, (o, n) in enumerate(ss):
                        dve.wait_ge(h_hi_done, hcount(q, j, s))
                        stt(out=h_lo[:, j, o:o + n], in0=tn[:, j % 2, o:o + n], scalar=mod[:, q // 3, 24 * i + j, s:s + 1],
                            in1=h_hi[:, j, o:o + n].bitcast(F), op0=ALU.add, op1=ALU.subtract).then_inc(h_ready, 1)

                for j in range(KD):
                    for s, (o, n) in enumerate(ss):
                        if j >= 2:
                            dve.wait_ge(h_ready, hcount(q, j - 2, s))
                        stt(out=tn[:, j % 2, o:o + n], in0=xT[:, j, o:o + n], scalar=amul[:, q // 3, i, j, s:s + 1],
                            in1=rstd[:, o:o + n], op0=ALU.mult, op1=ALU.mult).then_inc(t_done, 1)
                    if j:
                        low(j - 1)
                low(KD - 1)

            def ada(l):
                dve_.memset(cpad[:], 0.0).then_inc(pad_zeroed, 1)
                for b in FIRST_BLOCKS:
                    key = ("adaT", l, b)
                    wait_products(dve, key)
                    dve_.tensor_copy(mod[:, l, 4 * b:4 * b + 4, :],
                                     ps[:, bank_of(key), 0:8].rearrange("p (j v) -> p j v", v=2)).then_inc(bank_free[bank_of(key)], 1)
                for b in FIRST_BLOCKS:
                    wait_freed(dve, ("adaT", l, b))
                dve.wait_ge(cpad_ready, 4)
                modulation(l, 0)

            def modulation(l, i):
                m = slice(24 * i, 24 * i + 24)
                for v in range(2):
                    step(tt(mod[:, l, m, v], mod[:, l, m, v], vcol[:, l, m], ALU.add))
                settle()
                g0 = ROW[("g_ffn1", "g_mix", "g_ffn2")[i]][0]
                for v in range(2):
                    step(stt(out=amul[:, l, i, :, v], in0=mod[:, l, 24 * i + 8:24 * i + 16, v], scalar=1.0,
                             in1=vcol[:, l, g0:g0 + KD], op0=ALU.add, op1=ALU.mult))
                step(dve_.tensor_scalar(gate[:, l, i, :, :], mod[:, l, 24 * i + 16:24 * i + 24, :],
                                        1.0 if i == 1 else 0.5, None, ALU.mult))
                settle()

            def ffn(f, nxt):
                ss = segs_of(NORM_OF[f])
                i = 2 * (f % 2)

                def side(g, quarters, it=None):
                    if g not in SIDE_GROUPS[f]:
                        return
                    n = side_number((f, g))

                    def counted(extra):
                        return 16 * n + extra if it is None else it * 32 + (16 * n + extra)

                    for q in quarters:
                        landed = 16 * (2 * n + q // 2 + 1)
                        dve.wait_ge(side_landed[q % 2], landed if it is None else it * 64 + landed)
                        for k in range(2):
                            for v in range(2):
                                w, c = side_raw[q % 2][:, k, :], ccol[:, v, 2 * q + k:2 * q + k + 1]
                                m = 4 * q + 2 * k + v
                                if m < 2:
                                    ins = dve_.tensor_scalar(side_acc[:, v, :], w, c, None, ALU.mult)
                                else:
                                    dve.wait_ge(side_summed, counted(m - 1))
                                    ins = stt(out=side_acc[:, v, :], in0=w, scalar=c, in1=side_acc[:, v, :],
                                              op0=ALU.mult, op1=ALU.add)
                                ins.then_inc(side_summed, 1)

                def side_end(g, it=None):
                    if g not in SIDE_GROUPS[f]:
                        return
                    key = lambda x: ("side", f, x)
                    l, b = SIDE_GROUPS[f][g]
                    n = side_number((f, g))
                    wait_products(dve, key, g, it)
                    if n:
                        dve.wait_ge(side_done, n if it is None else it * 2 + n)
                    dve_.transpose(side_col[:].rearrange("p j n -> p (j n)"), ps[:, bank_of(key(g)), 0:256])\
                        .then_inc(bank_free[bank_of(key(g))], 1)
                    wait_freed(dve, key, g, it)
                    at_ = 4 * b if it is None else it * 8 + 4 * b
                    dve_.tensor_copy(mod[:, l, bass.ds(at_, 4), :],
                                     side_col[:, :, 0].rearrange("p (v j) -> p j v", v=2)).then_inc(side_done, 1)

                def hidden(g, it=None):
                    side(g, (0, 1), it)
                    for c in range(2):
                        if c == 1:
                            side(g, (2, 3), it)
                        n0 = 2 * NG * f + 2 * g + c + 1
                        if n0 > 2:
                            dve.wait_ge(hid_ready, n0 - 2 if it is None else it * 4 + (n0 - 2))
                        for s, (o, n) in enumerate(ss):
                            wait_freed(dve, lambda x: ("g", f, x, c, s), g, it)
                            wait_products(dve, lambda x: ("u", f, x, c, s), g, it)
                            tt(prod[:, c, o:o + n], sil[:, c, o:o + n], pt(("u", f, g, c, s), n), ALU.mult)\
                                .then_inc(bank_free[bank_of(("u", f, g, c, s))], 1)
                        dve.wait_ge(hid_hi_done, n0 if it is None else it * 4 + n0)
                        e = ss[-1][0] + ss[-1][1]
                        tt(hid_lo[:, g % 2, c, 0:e], prod[:, c, 0:e], hid_hi[:, g % 2, c, 0:e].bitcast(F), ALU.subtract)\
                            .then_inc(hid_ready, 1)

                def add(g, js, it=None):
                    for j in js:
                        for s, (o, n) in enumerate(ss):
                            wait_products(dve, lambda x: ("d", f, x, j, s), g, it)
                            stt(out=xT[:, j, o:o + n], in0=pt(("d", f, g, j, s), n), scalar=gate[:, f // 2, i, j, s:s + 1],
                                in1=xT[:, j, o:o + n], op0=ALU.mult, op1=ALU.add)\
                                .then_inc(bank_free[bank_of(("d", f, g, j, s))], 1)

                def groups(g, it=None):
                    hidden(g, it)
                    add(g - 1, range(0, 2), it)
                    split(lambda x: ("G", f, x), g + 1, it)
                    add(g - 1, range(2, 4), it)
                    split(lambda x: ("U", f, x), g + 1, it)
                    add(g - 1, range(4, SIDE_AT + 1), it)
                    side_end(g, it)
                    add(g - 1, range(SIDE_AT + 1, KD), it)
                    split(lambda x: ("D", f, x), g, it)

                split(("G", f, 1))
                hidden(0)
                split(("U", f, 1))
                split(("D", f, 0))
                side_end(0)
                with dve.Fori(0, (NG - 3) // 2) as it:
                    groups(1, it)
                    groups(2, it)
                groups_last = NG - 2
                hidden(groups_last)
                add(groups_last - 1, range(0, 2))
                split(("G", f, NG - 1))
                add(groups_last - 1, range(2, 4))
                split(("U", f, NG - 1))
                add(groups_last - 1, range(4, SIDE_AT + 1))
                side_end(NG - 2)
                add(groups_last - 1, range(SIDE_AT + 1, KD))
                split(("D", f, NG - 2))
                hidden(NG - 1)
                add(NG - 2, range(0, 4))
                split(("D", f, NG - 1))
                add(NG - 2, range(4, SIDE_AT + 1))
                side_end(NG - 1)
                add(NG - 2, range(SIDE_AT + 1, KD))
                add(NG - 1, range(0, 2))
                for n, key in enumerate(nxt):
                    split(key)
                    add(NG - 1, range(2 + n, 3 + n))
                add(NG - 1, range(2 + len(nxt), KD))
                if SIDE_GROUPS[f]:
                    dve.wait_ge(side_done, side_number((f, max(SIDE_GROUPS[f]))) + 1)
                    for l, m in (((0, 1), (0, 2)), ((1, 0),), ((1, 1), (1, 2)))[f]:
                        modulation(l, m)

            def mix(l):
                ms = mix_segs(l)
                ns = len(ms)
                n_line = LAT if ns == 1 else LAT + HALF + CTX
                for c in range(2):
                    for at0 in (0, C_LAT + LAT, C_CTX + CTX)[:ns + 1]:
                        step(dve_.memset(yline[:, c, at0:at0 + HALF], 0.0))
                rest = iter([("V", l, 0), ("V", l, 1), ("K", l, 0), ("K", l, 1), ("Q", l, 0), ("Q", l, 1),
                             ("out", l, 0), ("out", l, 1), ("out", l, 2), ("out", l, 3)])
                for c in range(2):
                    for s, (o, n) in enumerate(ms):
                        at0 = (C_LAT, C_CTX)[s]
                        wait_freed(dve, ("convg", l, c, s))
                        key = ("conva", l, c, s)
                        wait_products(dve, key)
                        tt(yline[:, c, at0:at0 + n], pt(key, n), yline[:, c, at0:at0 + n], ALU.mult)\
                            .then_inc(bank_free[bank_of(key)], 1)
                    split(next(rest))
                settle()
                for c in range(2):
                    for s in range(ns):
                        wait_freed(dve, ("conva", l, c, s))
                b0 = ROW["b_dw"][0]
                for tap in range(TAPS):
                    for c in range(2):
                        w = wdw[:, l, tap, c:c + 1]
                        src = yline[:, c, tap:tap + n_line]
                        if tap == 0:
                            step(dve_.tensor_scalar(acc[:, c, 0:n_line], src, w, vcol[:, l, b0 + c:b0 + c + 1], ALU.mult, ALU.add))
                            continue
                        settle(0 if tap == TAPS - 1 and c == 1 else 1)
                        ins = stt(out=acc[:, c, 0:n_line], in0=src, scalar=w, in1=acc[:, c, 0:n_line], op0=ALU.mult, op1=ALU.add)
                        if tap < TAPS - 1:
                            step(ins)
                        else:
                            ins.then_inc(acc_ready, 1)
                    if tap in (5, 17, 29):
                        split(next(rest))
                for h in range(HEADS):
                    key = ("K", l, h, 0)
                    wait_products(dve, key)
                    dve.wait_ge(acc_ready, 2 * (l + 1))
                    if h:
                        dve.wait_ge(k_ready, HEADS * l + h)
                    step(dve_.stream_shuffle(krope[:], pt(key), SWAP))
                    step(tt(kT[:, h, 0:LAT], pt(key), rope_c[:], ALU.mult))
                    settle(1)
                    tt(krope[:], krope[:], rope_s[:], ALU.mult).then_inc(bank_free[bank_of(key)], 1)
                    wait_freed(dve, key)
                    settle()
                    tt(kT[:, h, 0:LAT], kT[:, h, 0:LAT], krope[:], ALU.add).then_inc(k_ready, 1)
                    if h == 1:
                        split(next(rest))

                def biased_low(kind, name, chunk0, before):
                    for p in range(2):
                        for s, (o, n) in enumerate(ms):
                            key = (kind, l, p, s)
                            col = ROW[name][0] + p
                            dve.wait_ge(mix_hi_done, before + p * ns + s + 1)
                            stt(out=h_lo[:, chunk0 + p, o:o + n], in0=pt(key, n), scalar=vcol[:, l, col:col + 1],
                                in1=h_hi[:, chunk0 + p, o:o + n].bitcast(F), op0=ALU.add, op1=ALU.subtract)\
                                .then_inc(bank_free[bank_of(key)], 1)

                mbefore = 8 * sum(len(mix_segs(x)) for x in range(l))
                biased_low("Fo", "b_fourier", 6, mbefore)
                for s, (o, n) in enumerate(ms):
                    ao = 0 if s == 0 else C_CTX - HALF
                    key = ("mean", l, s)
                    wait_products(dve, key)
                    dve.wait_ge(acc_ready, 2 * (l + 1))
                    for c in range(2):
                        ins = stt(out=acc[:, c, ao:ao + n], in0=pt(key, n), scalar=-1.0 / CONVW, in1=acc[:, c, ao:ao + n],
                                  op0=ALU.mult, op1=ALU.add)
                        if c == 0:
                            step(ins)
                        else:
                            ins.then_inc(bank_free[bank_of(key)], 1)
                for s, (o, n) in enumerate(ms):
                    ao = 0 if s == 0 else C_CTX - HALF
                    wait_freed(dve, ("var", l, s))
                    step(dve_.reciprocal(crs[:, o:o + n], cst[:, o:o + n]))
                    settle()
                    for c in range(2):
                        tt(acc[:, c, ao:ao + n], acc[:, c, ao:ao + n], crs[:, o:o + n], ALU.mult).then_inc(cn_done, 1)
                biased_low("pw", "b_pw", 4, mbefore + 2 * ns)
                us = units_of(l)
                u_before = sum(len(units_of(x)) for x in range(l))
                wait_products(dve, ("pw", l, 1, ns - 1))
                for b in range(2):
                    step(dve_.memset(qpad[64:128, b, 0, :], 0.0))
                    step(dve_.memset(qpad[0:64, b, 1, :], 0.0))

                def rope_q(h):
                    for s in range(ns):
                        wait_freed(dve, ("Q", l, h, s))
                    if h >= 2:
                        last = max(i for i, u in enumerate(us) if u[0] == h - 2)
                        wait_products(dve, ("score", l, last))
                    settle()
                    if h:
                        dve.wait_ge(q_ready, HEADS * l + h)
                    step(dve_.stream_shuffle(qrope[:, 0, :], qT[:, h, 0:LAT], SWAP))
                    step(tt(qrope[:, 1, :], qT[:, h, 0:LAT], rope_c[:], ALU.mult))
                    settle(1)
                    step(tt(qrope[:, 0, :], qrope[:, 0, :], rope_s[:], ALU.mult))
                    for st in range(2):
                        r = slice(64 * st, 64 * st + 64)
                        if ns == 2:
                            step(dve_.tensor_copy(qpad[r, h % 2, st, LAT:TOK], qT[r, h, LAT:TOK]))
                    settle()
                    for st in range(2):
                        r = slice(64 * st, 64 * st + 64)
                        ins = tt(qpad[r, h % 2, st, 0:LAT], qrope[r, 0, :], qrope[r, 1, :], ALU.add)
                        if st == 0:
                            step(ins)
                        else:
                            ins.then_inc(q_ready, 1)

                def combine(i):
                    h, s, t = us[i]
                    dve.wait_ge(exp_done, 2 * (u_before + i + 1))
                    p, n = i % 2, TOK if s == 0 else CTX
                    if i >= 2:
                        dve.wait_ge(p_ready, u_before + i - 1)
                    step(dve_.reciprocal(rs[:, p, :], sums[:, p, :]))
                    settle()
                    step(tt(rs[:, p, 1:2], rs[:, p, 1:2], neglam[:, l:l + 1], ALU.mult))
                    settle()
                    step(dve_.tensor_scalar(e1[:, p, 0:n], e1[:, p, 0:n], rs[:, p, 1:2], None, ALU.mult))
                    settle()
                    pieces = ((0, LAT, CTX), (LAT, CTX, 0)) if s == 0 else ((0, CTX, 0),)
                    for k, (o, m, o1) in enumerate(pieces):
                        ins = stt(out=e0[:, i % 3, o:o + m], in0=e0[:, i % 3, o:o + m], scalar=rs[:, p, 0:1],
                                  in1=e1[:, p, o1:o1 + m], op0=ALU.mult, op1=ALU.add)
                        if k == len(pieces) - 1:
                            ins.then_inc(p_ready, 1)
                        else:
                            step(ins)

                rope_q(0)
                for i in range(len(us) + 1):
                    if i < len(us):
                        h, s, t = us[i]
                        wait_products(dve, ("score", l, i))
                        at0, n, p = 1536 * (i % 2), TOK if s == 0 else CTX, i % 2
                        if i >= 2:
                            dve.wait_ge(max_done, u_before + i - 1)
                        for st in range(2):
                            step(dve_.reduce_max(mx[:, p, st:st + 1], pflat[:, at0 + n * st:at0 + n * st + n], AX.X))
                        settle()
                        dve_.tensor_scalar(nb[:, p, :], mx[:, p, :], -(HD ** -0.5), None, ALU.mult).then_inc(max_done, 1)
                    if i >= 1:
                        combine(i - 1)
                    if i < len(us) and s == 0 and t == 1 and h < HEADS - 1:
                        rope_q(h + 1)
                    if i in (4, 6, 8):
                        split(next(rest))
                hbefore = HEADS * sum(len(mix_segs(x)) for x in range(l))
                for h in range(HEADS):
                    for s, (o, n) in enumerate(ms):
                        wait_freed(dve, ("hn", l, h, s))
                        step(dve_.reciprocal(hst[:, h, o:o + n], hst[:, h, o:o + n]))
                        settle()
                        stt(out=qT[:, h, o:o + n], in0=qT[:, h, o:o + n], scalar=gsub[:, l:l + 1], in1=hst[:, h, o:o + n],
                            op0=ALU.mult, op1=ALU.mult).then_inc(ht_done, 1)
                    if h:
                        head_low(l, h - 1, mbefore + 4 * ns)
                head_low(l, HEADS - 1, mbefore + 4 * ns)
                first = True
                for j in range(KD):
                    for s, (o, n) in enumerate(ms):
                        key = ("out", l, j, s)
                        wait_products(dve, key)
                        stt(out=xT[:, j, o:o + n], in0=pt(key, n), scalar=gate[:, l, 1, j, s:s + 1], in1=xT[:, j, o:o + n],
                            op0=ALU.mult, op1=ALU.add).then_inc(bank_free[bank_of(key)], 1)
                    if j == 1:
                        split(next(rest))
                    if j == 3:
                        split(("G", 2 * l + 1, 0))
                    if j == 5:
                        split(("U", 2 * l + 1, 0))

            def head_low(l, h, before):
                ms = mix_segs(l)
                for s, (o, n) in enumerate(ms):
                    dve.wait_ge(mix_hi_done, before + h * len(ms) + s + 1)
                    tt(h_lo[:, h, o:o + n], qT[:, h, o:o + n], h_hi[:, h, o:o + n].bitcast(F), ALU.subtract)\
                        .then_inc(mix_ready, 1)

            dve.wait_ge(const_landed, 16 * N_CONST)
            for l in range(DEPTH):
                for i in range(2):
                    settle()
                    step(tt(lamp[:], lamv[:, l, 2 * i, :], lamv[:, l, 2 * i + 1, :], ALU.mult))
                    settle()
                    ins = dve_.reduce_sum(lamw[:, 2 * l + i:2 * l + i + 1], lamp[:], AX.X)
                    if l == DEPTH - 1 and i == 1:
                        ins.then_inc(lam_dot, 1)
                    else:
                        step(ins)
            dve.wait_ge(lam_exp, 1)
            for l in range(DEPTH):
                step(tt(neglam[:, l:l + 1], lamw[:, 2 * l + 1:2 * l + 2], lamw[:, 2 * l:2 * l + 1], ALU.subtract))
                settle()
                step(dve_.tensor_scalar(neglam[:, l:l + 1], neglam[:, l:l + 1], -LAM_INIT[l], None, ALU.add))
                wait_freed(dve, ("vec", l))
                g0 = ROW["g_subln"][0]
                step(dve_.tensor_scalar(gsub[:, l:l + 1], vcol[:, l, g0:g0 + 1], 1.0 - LAM_INIT[l], None, ALU.mult))
            for s, (o, n) in enumerate(BOTH):
                for j in range(KD):
                    key = ("xin", s, j)
                    wait_products(dve, key)
                    dve_.tensor_copy(xT[:, j, o:o + n], pt(key, n)).then_inc(bank_free[bank_of(key)], 1)
            for i in range(4):
                wait_freed(dve, ("vec", i))
            ada(0)
            split(("G", 0, 0))
            split(("U", 0, 0))
            for l in range(DEPTH):
                norm(3 * l)
                ffn(2 * l, [("conv", l, 0), ("conv", l, 1)])
                split(("four", l))
                norm(3 * l + 1)
                mix(l)
                norm(3 * l + 2)
                ffn(2 * l + 1, [("G", 2 * l + 2, 0), ("U", 2 * l + 2, 0)] if l < DEPTH - 1 else [])
            norm(3 * DEPTH)


LAM_INIT = [0.8 - 0.6 * math.exp(-0.3 * l) for l in range(DEPTH)]
SWAP = [(i + 16) % 32 for i in range(32)]
SMALL = ("dft_cos", "dft_sin", "dft_cos_ctx", "dft_sin_ctx")
N_CONST = 4 + 6


def shape_tables():
    def dft(n, norm):
        i = np.arange(n)
        ang = 2.0 * np.pi * ((i[:, None] * i[None, :]) % n) / n
        return (np.cos(ang) * norm).astype(np.float32), (np.sin(ang) * norm).astype(np.float32)

    c, s = dft(LAT, LAT ** -0.5)
    cc, sc = dft(CTX, CTX ** -0.5)
    cd, sd = dft(64, 64 ** -0.5)
    both = np.zeros((128, 2, 128), np.float32)
    for g in range(2):
        both[64 * g:64 * g + 64, 0, 64 * g:64 * g + 64] = cd
        both[64 * g:64 * g + 64, 1, 64 * g:64 * g + 64] = -sd
    rot = HD // 2
    inv = (10000.0 ** (-np.arange(0, rot, 2, dtype=np.float32) / np.float32(rot))).astype(np.float32)
    t = np.arange(LAT)
    pos = np.stack([t // GRID_W, t % GRID_W]).astype(np.float32)
    rc, rsn = np.zeros((128, LAT), np.float32), np.zeros((128, LAT), np.float32)
    for p in range(128):
        d = p % HD
        ang = (pos[d // rot] * inv[d % (rot // 2)]).astype(np.float32)
        rc[p] = np.cos(ang)
        rsn[p] = np.sin(ang) * (-1.0 if d % rot < rot // 2 else 1.0)
    sel = np.zeros((128, 2), np.float32)
    for v in range(2):
        sel[v::32, v] = 1.0
    return {"dft_cos": c, "dft_sin": s, "dft_cos_ctx": cc, "dft_sin_ctx": sc, "dft_groups": both,
            "rope_cos": rc, "rope_sin": rsn, "ident": np.eye(128, dtype=np.float32), "sel": sel}


WEIGHTS = ("x", "ctx", "w_ada", "w_ffn1_gate", "w_ffn1_up", "w_ffn1_down", "w_ffn2_gate", "w_ffn2_up", "w_ffn2_down",
           "w_in", "w_pw", "w_fourier", "w_out")


def kernel(**inputs):
    import concourse.bacc as bacc
    from concourse.bass_utils import run_bass_kernel_spmd

    nc = bacc.Bacc("TRN2", target_bir_lowering=False, num_devices=1)
    arr = {k: np.ascontiguousarray(inputs[k]) for k in WEIGHTS}

    def stack(parts):
        return np.ascontiguousarray(np.concatenate([np.asarray(p).reshape(-1, 128) for p in parts], axis=0))

    for l in range(DEPTH):
        arr[f"vec{l}"] = stack([np.asarray(inputs[n])[l] for n in ROW])
    arr["vecw"] = stack([inputs["w_dw"]])
    arr["vecc"] = stack([inputs["c"], inputs["c_ctx"], inputs["g_final"]])
    arr["lams"] = np.ascontiguousarray(np.stack([np.asarray(inputs[n]) for n in ("lambda_q1", "lambda_k1", "lambda_q2", "lambda_k2")], axis=1)).reshape(1, -1)
    arr.update(shape_tables())
    a = {k: nc.dram_tensor(f"in_{k}", v.shape, mybir.dt.from_np(v.dtype), kind="ExternalInput").ap() for k, v in arr.items()}
    a["out"] = nc.dram_tensor("out_0", (1, LAT, D), mybir.dt.float32, kind="ExternalOutput").ap()
    trunk(nc, a)
    r = run_bass_kernel_spmd(nc, [{f"in_{k}": v for k, v in arr.items()}], core_ids=[0])
    return r.results[0]["out_0"]
```

```python
import math
from contextlib import ExitStack

import numpy as np

import concourse.bass as bass
from concourse import mybir

DEPTH = 2
D = 1024
LAT, CTX = 512, 256
TOK = LAT + CTX
KD = D // 128
FF = 2816
GW = 256
NG = FF // GW
HEADS = 4
HD = 64
QKW = 512
CONVW = 256
TAPS = 31
HALF = TAPS // 2
INW = 2304
EPS = 1e-6
GRID_W = 64
RING = 3
TILE = 2048
LINE = HALF + LAT + HALF + CTX + HALF
BOTH = ((0, LAT), (LAT, CTX))
ONLY_LAT = ((0, LAT),)
C_LAT = HALF
C_CTX = HALF + LAT + HALF

ROW = {}
_at = 0
for _name, _n in (("b_ada", 72), ("g_ffn1", 8), ("g_mix", 8), ("g_ffn2", 8), ("g_subln", 1), ("b_dw", 2),
                  ("g_conv_ln", 2), ("b_conv_ln", 2), ("b_pw", 2), ("b_fourier", 2)):
    ROW[_name] = (_at, _n)
    _at += _n
NROW = _at
NADA = 9 * D // 512
FIRST_BLOCKS = (0, 1, 2, 3, 4, 5, NADA - 1)
BEFORE, BETWEEN = FIRST_BLOCKS[:4], FIRST_BLOCKS[4:]
SIDE_GROUPS = ({g: (0, 6 + g) for g in range(NG)}, {g: (1, g - 1) for g in range(1, NG)},
               {g: (1, NG - 2 + g) for g in range(1, NADA - (NG - 1) + 1)}, {})
SIDE_AT = 5


def segs_of(norm):
    return ONLY_LAT if norm >= 5 else BOTH


def seg_order(q):
    return (1, 0) if len(segs_of(q)) == 2 else (0,)


def square_order(q):
    if q % 3 == 2 and len(segs_of(q)) == 2:
        return [(s, j) for j in range(4) for s in (0, 1)] + [(s, j) for s in (1, 0) for j in range(4, KD)]
    return [(s, j) for s in seg_order(q) for j in range(KD)]


def out_order(l):
    if len(mix_segs(l)) == 1:
        return [(v, 0) for v in range(4)]
    return [(0, 0), (0, 1), (1, 0), (1, 1), (2, 1), (3, 1), (2, 0), (3, 0)]


def mix_segs(l):
    return BOTH if l < DEPTH - 1 else ONLY_LAT


def units_of(l):
    return [(h, s, t) for h in range(HEADS) for s in range(len(mix_segs(l))) for t in range(mix_segs(l)[s][1] // 128)]


class Plan:

    def __init__(self):
        self.n = 0
        self.bank = 0
        self.uses = [0] * 8
        self.slots = {}
        self.tiles = []
        self.raw = {}
        self.split = {}
        self.lastuse = {}
        self.before_att = []
        self.nsplit = 0
        self.build()

    def slot(self, key, bank=None):
        if bank is None:
            bank = self.bank
            self.bank = (bank + 1) % 8
        self.slots[key] = (self.n, bank, self.uses[bank])
        self.n += 1
        self.uses[bank] += 1

    def tile(self, key, split=True):
        self.raw[key] = len(self.tiles)
        self.tiles.append(key)
        if split:
            self.split[key] = self.nsplit
            self.nsplit += 1

    def used(self, key, slot):
        self.lastuse[key] = slot

    def ada(self, blocks):
        def bank(i):
            return (self.bank + i) % 8 if blocks is BETWEEN else None

        for n, b in enumerate(blocks):
            if b == 3:
                for s in seg_order(0):
                    self.slot(("stat", 0, s))
            self.slot(("ada", 0, b), bank(n % 2))
            if n:
                self.slot(("adaT", 0, blocks[n - 1]), bank(2 + (n - 1) % 2))
            self.tile(("ada", 0, b, 0), split=False)
            self.tile(("ada", 0, b, 1), split=False)
            self.used(("ada", 0, b, 0), ("ada", 0, b))
            self.used(("ada", 0, b, 1), ("ada", 0, b))
        self.slot(("adaT", 0, blocks[-1]), bank(2 + (len(blocks) - 1) % 2))

    def side(self, f, g):
        if g in SIDE_GROUPS[f]:
            self.slot(("side", f, g), (self.bank + 4) % 8)

    def ffn(self, f):
        ns = len(segs_of((0, 2, 3, 5)[f]))
        after = (1, 3, 4, 6)[f]

        def gate_up(g):
            if g == 0 and ns == 2:
                slots = [(w, f, g, c, s) for s in (1, 0) for c in range(2) for w in "gu"]
            else:
                slots = [(w, f, g, c, s) for c in range(2) for w in "gu" for s in range(ns)]
            for key in slots:
                self.slot(key)
                if f == 0 and key == ("u", 0, 0, 1, 1):
                    self.ada(BETWEEN)
            self.used(("G", f, g), ("g", f, g, 1, 0 if g == 0 else ns - 1))
            self.used(("U", f, g), ("u", f, g, 1, 0 if g == 0 else ns - 1))

        def down(g):
            for j in range(KD):
                for s in range(ns):
                    self.slot(("d", f, g, j, s))
                if j == SIDE_AT:
                    self.side(f, g + 1)
            self.used(("D", f, g), ("d", f, g, KD - 1, ns - 1))

        self.tile(("G", f, 0))
        self.tile(("U", f, 0))
        gate_up(0)
        self.side(f, 0)
        for g in range(1, NG):
            self.tile(("G", f, g))
            self.tile(("U", f, g))
            self.tile(("D", f, g - 1))
            gate_up(g)
            down(g - 1)
        self.tile(("D", f, NG - 1))
        for s in seg_order(after - 1 if ns == 2 else 5):
            for j in range(KD):
                self.slot(("d", f, NG - 1, j, s))
                if s == 0 and j == 3 and ns == 2:
                    self.slot(("stat", after, 1))
        self.used(("D", f, NG - 1), ("d", f, NG - 1, KD - 1, 0))
        self.slot(("stat", after, 0))

    def mix(self, l):
        ms = mix_segs(l)
        for v in range(2):
            self.tile(("V", l, v))
        for ts in ((4, 5), (0, 1, 2, 3)):
            for v in range(2):
                for t in ts:
                    self.slot(("V", l, v, t))
        for v in range(2):
            self.used(("V", l, v), ("V", l, v, 3))
        for c in range(2):
            self.tile(("conv", l, c))
            for w in "ga":
                for s in range(len(ms)):
                    self.slot(("conv" + w, l, c, s))
            self.used(("conv", l, c), ("conva", l, c, len(ms) - 1))
        self.tile(("four", l))
        nt = sum(n for _, n in ms) // 128
        for t in range(nt):
            self.slot(("X", l, t))
        self.used(("four", l), ("X", l, nt - 1))
        for w, ss in (("Q", ms), ("K", BOTH)):
            for v in range(2):
                self.tile((w, l, v))
                for c in range(2):
                    for s in range(len(ss)):
                        self.slot((w, l, 2 * v + c, s))
                self.used((w, l, v), (w, l, 2 * v + 1, len(ss) - 1))
        for k in ("C", "S", "W"):
            self.tile((k, l), split=False)
        for j in range(2):
            for w in "CS":
                for s in range(len(ms)):
                    self.slot(("Z", l, j, w, s))
        self.used(("C", l), ("Z", l, 1, "S", len(ms) - 1))
        self.used(("S", l), ("Z", l, 1, "S", len(ms) - 1))
        for j in range(2):
            for s in range(len(ms)):
                self.slot(("F", l, j, s))
        for o in range(2):
            for s in range(len(ms)):
                self.slot(("Fo", l, o, s))
        for s in range(len(ms)):
            self.slot(("mean", l, s))
        for s in range(len(ms)):
            self.slot(("var", l, s))
        for o in range(2):
            for s in range(len(ms)):
                self.slot(("pw", l, o, s))
        self.used(("W", l), ("pw", l, 1, len(ms) - 1))
        u = units_of(l)
        self.before_att.append(list(self.uses))
        for i in range(len(u) + 3):
            if i < len(u):
                self.slots[("score", l, i)] = (self.n, None, None)
                self.n += 1
            if 0 <= i - 2 < len(u):
                self.slot(("T", l, i - 2, 0), 6)
            if 0 <= i - 3 < len(u):
                h, s, t = u[i - 3]
                if t == 0:
                    self.slots[("O", l, h, s)] = (None, 7, self.uses[7])
                    self.uses[7] += 1
                if t == ms[s][1] // 128 - 1:
                    self.slots[("O", l, h, s)] = (self.n,) + self.slots[("O", l, h, s)][1:]
                    self.n += 1
            if 0 <= i - 2 < len(u) and u[i - 2][1] == 0:
                self.slot(("T", l, i - 2, 1), 6)
        self.bank = 0
        for h in range(HEADS):
            for s in range(len(ms)):
                self.slot(("hn", l, h, s))
        for v in range(4):
            self.tile(("out", l, v))
        for v, s in out_order(l):
            for c in range(2):
                self.slot(("out", l, 2 * v + c, s))
                if (v, c, s) == (2, 0, 0) and len(ms) == 2:
                    self.slot(("stat", 3 * l + 2, 1))
            self.used(("out", l, v), ("out", l, 2 * v + 1, s))
        self.slot(("stat", 3 * l + 2, 0))

    def build(self):
        for i in range(4):
            self.slot(("vec", i))
        for s in range(2):
            for j in range(KD):
                self.slot(("xin", s, j))
        self.ada(BEFORE)
        for l in range(DEPTH):
            self.ffn(2 * l)
            self.mix(l)
            self.ffn(2 * l + 1)
        for t in range(LAT // 128):
            for half in range(2):
                self.slot(("xout", t, half))


POOL_SPLITS = {1: (("V", 0, 0), ("V", 0, 1)), 2: (("U", 1, 0),), 3: (("G", 2, 0), ("U", 2, 0)),
               4: (("V", 1, 0), ("V", 1, 1)), 5: (("U", 3, 0),)}


def trunk(nc, a):
    F, R = mybir.dt.float32, mybir.dt.float32r
    ALU, ACT, AX = mybir.AluOpType, mybir.ActivationFunctionType, mybir.AxisListType
    plan = Plan()
    ctx = ExitStack()
    with ctx:
        used = [0]
        used[0] = (nc.sbuf_base + 31) // 32 * 32

        def at(name, shape, dt, offset):
            return nc.alloc_sbuf_tensor_at(name, shape, dt, offset=offset, align_bytes=4)

        def sb(name, shape, dt=F):
            t = at(name, shape, dt, used[0])
            used[0] += 4 * math.prod(shape[1:])
            return t

        xT = sb("xT", [128, KD, TOK])
        h_at = used[0]
        h_hi = sb("h_hi", [128, KD, TOK], R)
        h_lo_at = used[0]
        h_lo = sb("h_lo", [128, KD, TOK], R)
        raw = [sb(f"raw{i}", [128, TILE]) for i in range(RING)]
        w_hi = [sb(f"w_hi{i}", [128, TILE], R) for i in range(RING)]
        w_lo = [sb(f"w_lo{i}", [128, TILE], R) for i in range(RING)]
        ones = sb("ones", [128, 128])
        ident = sb("ident", [128, 128])
        rope_c = sb("rope_c", [128, LAT])
        rope_s = sb("rope_s", [128, LAT])
        dft = sb("dft", [128, 2, 128])
        vcol = sb("vcol", [128, DEPTH, NROW])
        wdw = sb("wdw", [128, DEPTH, TAPS, 2])
        ccol = sb("ccol", [128, 3, KD])
        mod = sb("mod", [128, DEPTH, 72, 2])
        amul = sb("amul", [128, DEPTH, 3, KD, 2])
        gate = sb("gate", [128, DEPTH, 3, KD, 2])
        gsub = sb("gsub", [128, DEPTH])
        epsc = sb("epsc", [128, 1])
        neglam = sb("neglam", [128, DEPTH])
        mx = sb("mx", [128, 2, 2])
        nb = sb("nb", [128, 2, 2])
        sums = sb("sums", [128, 2, 2])
        rs = sb("rs", [128, 2, 2])
        M = (used[0] + 31) // 32 * 32
        S3 = 4 * TOK
        hid_hi = at("hid_hi", [128, 2, 2, TOK], R, M)
        hid_lo = at("hid_lo", [128, 2, 2, TOK], R, M + 4 * S3)
        sil = at("sil", [128, 2, TOK], F, M + 8 * S3)
        prod = at("prod", [128, 2, TOK], F, M + 10 * S3)
        sq = at("sq", [128, 2, TOK], F, M + 12 * S3)
        std = at("std", [128, TOK], F, M + 2 * S3)
        rstd = at("rstd", [128, TOK], F, M + 3 * S3)
        tn = at("tn", [128, 2, TOK], F, M + 6 * S3)
        sqsum = at("sqsum", [128, TOK], F, M + 8 * S3)
        cpad = at("cpad", [128, KD, 32], F, M + 9 * S3)
        side_raw = [at(f"side_raw{i}", [128, 2, 512], F, M + 14 * S3 + 4096 * i) for i in range(2)]
        side_acc = at("side_acc", [128, 2, 512], F, M + 14 * S3 + 8192)
        side_col = at("side_col", [128, 8, 32], F, M + 12 * S3)
        sel = at("sel", [128, 2], F, M + 9 * S3 + 1024)
        lamw = at("lamw", [128, 4], F, M + 9 * S3 + 1024 + 8)
        xnat = at("xnat", [128, TOK // 128, D], F, M)
        vstage = at("vstage", [128, 4, 128], F, M + 10 * S3)
        lamv = at("lamv", [128, DEPTH, 4, HD], F, M + 10 * S3 + 2048)
        lamp = at("lamp", [128, HD], F, M + 10 * S3 + 2048 + 2048)
        part = at("part", [128, 2, 512], F, M + 10 * S3)
        kT = at("kT", [128, HEADS, TOK], F, M)
        qT = at("qT", [128, HEADS, TOK], F, M + 4 * S3)
        vN = at("vN", [128, TOK // 128, QKW], F, M + 8 * S3)
        xN = at("xN", [128, TOK // 128, CONVW], F, M + 12 * S3)
        yline = at("yline", [128, 2, LINE], F, M + 14 * S3)
        acc_at = M + 14 * S3 + 4 * 2 * LINE
        acc = at("acc", [128, 2, LINE - 2 * HALF], F, (acc_at + 31) // 32 * 32)
        e0 = at("e0", [128, 3, TOK], F, M + 12 * S3)
        pT = at("pT", [128, 2, TOK // 128, 128], F, M + 15 * S3)
        zT = at("zT", [128, 2, 2, TOK], F, h_lo_at)
        fT = at("fT", [128, 2, TOK], F, h_at)
        csq = at("csq", [128, 2, TOK], F, h_at + 2 * S3)
        cst = at("cst", [128, TOK], F, h_lo_at + 4 * S3)
        crs = at("crs", [128, TOK], F, h_lo_at + 5 * S3)
        cs = at("cs", [128, 2, TOK], F, M + 14 * S3)
        krope = at("krope", [128, LAT], F, M + 14 * S3)
        e1 = at("e1", [128, 2, TOK], F, h_lo_at + 2 * S3)
        qpad = at("qpad", [128, 2, 2, TOK], F, h_at)
        qrope = at("qrope", [128, 2, LAT], F, h_lo_at)
        hsq = at("hsq", [128, HEADS, TOK], F, M)
        hst = at("hst", [128, HEADS, TOK], F, M + 8 * S3)
        onat = at("onat", [128, 2, D], F, M)

        ps = ctx.enter_context(nc.psum_tensor("ps", [128, 8, 512], F))
        pflat = ps[:].rearrange("p b n -> p (b n)")

        def sem(name):
            return ctx.enter_context(nc.semaphore(name))

        products = sem("products")
        bank_free = [sem(f"bank_free{b}") for b in range(8)]
        raw_landed = [sem(f"raw_landed{i}") for i in range(RING)]
        w_hi_done = sem("w_hi_done")
        w_split = sem("w_split")
        const_landed = sem("const_landed")
        x_landed = sem("x_landed")
        out_landed = [sem(f"out_landed{i}") for i in range(2)]
        out_ready = sem("out_ready")
        pool_const = sem("pool_const")
        act_step = sem("act_step")
        dve_step = sem("dve_step")
        cpad_ready = sem("cpad_ready")
        side_landed = [sem(f"side_landed{i}") for i in range(2)]
        side_summed = sem("side_summed")
        side_done = sem("side_done")
        sq_done = sem("sq_done")
        squares_added = sem("squares_added")
        ada_half = sem("ada_half")
        t_done = sem("t_done")
        h_hi_done = sem("h_hi_done")
        h_ready = sem("h_ready")
        hid_hi_done = sem("hid_hi_done")
        hid_ready = sem("hid_ready")
        line_ready = sem("line_ready")
        k_ready = sem("k_ready")
        acc_ready = sem("acc_ready")
        csq_done = sem("csq_done")
        cn_done = sem("cn_done")
        cs_done = sem("cs_done")
        q_ready = sem("q_ready")
        max_done = sem("max_done")
        exp_done = sem("exp_done")
        p_ready = sem("p_ready")
        mix_hi_done = sem("mix_hi_done")
        mix_ready = sem("mix_ready")
        hsq_done = sem("hsq_done")
        ht_done = sem("ht_done")
        y_done = sem("y_done")
        lam_dot = sem("lam_dot")
        lam_exp = sem("lam_exp")
        pad_zeroed = sem("pad_zeroed")
        block = ctx.enter_context(nc.Block())

        def lin(value, key, g, it):
            v = value(key(g))
            if it is None:
                return v
            step = value(key(g + 2)) - v
            return it * step + v

        def number(key):
            return plan.slots[key][0] + 1

        def freed(key):
            return plan.slots[key][2] + 1

        def wait_products(eng, key, g=None, it=None):
            eng.wait_ge(products, number(key) if g is None else lin(number, key, g, it))

        def wait_bank(pe, key, g=None, it=None):
            k0 = key if g is None else key(g)
            use = plan.slots[k0][2]
            if use or it is not None:
                pe.wait_ge(bank_free[plan.slots[k0][1]], use if g is None else lin(lambda k: plan.slots[k][2], key, g, it))

        def wait_freed(eng, key, g=None, it=None):
            k0 = key if g is None else key(g)
            eng.wait_ge(bank_free[plan.slots[k0][1]], freed(key) if g is None else lin(freed, key, g, it))

        def bank_of(key):
            return plan.slots[key][1]

        def pt(key, n=512):
            return ps[:, plan.slots[key][1], 0:n]

        def raw_of(key):
            return raw[plan.raw[key] % RING]

        arrived, total = {}, [0] * RING
        for key in plan.tiles:
            total[plan.raw[key] % RING] += 16 * {"conv": 2, "W": 4}.get(key[0], 1)
            arrived[key] = total[plan.raw[key] % RING]

        def wait_landed(eng, key, g=None, it=None):
            k0 = key if g is None else key(g)
            eng.wait_ge(raw_landed[plan.raw[k0] % RING],
                        arrived[key] if g is None else lin(arrived.__getitem__, key, g, it))

        def ring(key):
            return plan.split[key] % RING

        split_keys = [k for k in plan.tiles if k in plan.split]

        def hcount(q, j, s):
            return 8 * sum(len(segs_of(x)) for x in range(q)) + 8 * seg_order(q).index(s) + j + 1

        def sqcount(q, s, j):
            return 8 * sum(len(segs_of(x)) for x in range(q)) + square_order(q).index((s, j)) + 1

        def addcount(q, s, j):
            o = square_order(q)
            return 7 * sum(len(segs_of(x)) for x in range(q)) + sum(1 for x in o[:o.index((s, j)) + 1] if x[1])

        NORM_OF = (0, 2, 3, 5)
        side_list = [(f, g) for f in range(2 * DEPTH) for g in SIDE_GROUPS[f]]

        def side_number(key):
            return side_list.index(key)

        consts = []

        def load_sizes(key):
            dst = raw_of(key)
            k = key[0]
            if k == "ada":
                _, l, b, half = key
                return [(a["w_ada"][l, 512 * half:512 * half + 512, 512 * b:512 * b + 512]
                         .rearrange("(k p) n -> p k n", p=128), dst[:].rearrange("p (k n) -> p k n", k=4))]
            if k in ("C", "S"):
                src = a["dft_cos"] if k == "C" else a["dft_sin"]
                return [(src.rearrange("(k p) n -> p k n", p=128), dst[:].rearrange("p (k n) -> p k n", k=4))]
            l = key[1]
            if k == "W":
                out = []
                for i, src in enumerate((a["w_pw"][l, :, :], a["w_fourier"][l, :, :], a["dft_cos_ctx"], a["dft_sin_ctx"])):
                    out.append((src.rearrange("(k p) n -> p k n", p=128),
                                dst[:, 512 * i:512 * i + 512].rearrange("p (k n) -> p k n", k=2)))
                return out
            d8 = dst[:].rearrange("p (k n) -> p k n", k=KD)
            if k == "conv":
                c = key[2]
                out = []
                for i, at_ in enumerate((1536 + 128 * c, 1536 + 256 + 128 * c)):
                    out.append((a["w_in"][l, :, at_:at_ + 128].rearrange("(k p) n -> p k n", p=128),
                                d8[:, :, 128 * i:128 * i + 128]))
                return out
            if k == "out":
                at_, src = 256 * key[2], a["w_out"]
            else:
                at_ = {"four": 2048, "V": 1024, "K": 512, "Q": 0}[k] + (256 * key[2] if k != "four" else 0)
                src = a["w_in"]
            return [(src[l, :, at_:at_ + 256].rearrange("(k p) n -> p k n", p=128), d8)]

        def ffn_source(f, k, col):
            l, which = f // 2, f % 2 + 1
            if k == "D":
                return a[f"w_ffn{which}_down"][l, bass.ds(col, GW), :].rearrange("(c p) n -> p c n", p=128)
            name = f"w_ffn{which}_{'gate' if k == 'G' else 'up'}"
            return a[name][l, :, bass.ds(col, GW)].rearrange("(k p) n -> p k n", p=128)

        @block.sync
        def _(sp):
            for src, dst in ((a["vec0"], vstage[0:NROW, 0, :]), (a["vec1"], vstage[0:NROW, 1, :]),
                             (a["vecw"], vstage[0:4 * TAPS, 2, :]), (a["vecc"], vstage[0:3 * KD, 3, :])):
                sp.dma_start(dst, src).then_inc(const_landed, 16)
            for dst, name in ((ident[:], "ident"), (sel[:], "sel"), (rope_c[:], "rope_cos"), (rope_s[:], "rope_sin"),
                              (dft[:], "dft_groups")):
                sp.dma_start(dst, a[name]).then_inc(const_landed, 16)
            sp.dma_start(lamv[:].rearrange("p l i n -> p (l i n)"), a["lams"].broadcast_to((128, DEPTH * 4 * HD))).then_inc(const_landed, 16)
            for t in range(TOK // 128):
                src = a["x"][0, 128 * t:128 * t + 128, :] if t < 4 else a["ctx"][0, 128 * (t - 4):128 * (t - 4) + 128, :]
                sp.dma_start(xnat[:, t, :], src).then_inc(x_landed, 16)

            def release(key):
                t = plan.raw[key] - RING
                if t < 0:
                    return
                old = plan.tiles[t]
                if old in plan.split:
                    sp.wait_ge(w_split, plan.split[old] + 1)
                elif old[0] == "ada" and old[3] == 0:
                    sp.wait_ge(ada_half, FIRST_BLOCKS.index(old[2]) + 1)
                else:
                    wait_products(sp, plan.lastuse[old])

            def load(key):
                release(key)
                if key[0] in "GUD":
                    pairs = [(ffn_source(key[1], key[0], GW * key[2]), ffn_dst(key))]
                else:
                    pairs = load_sizes(key)
                for i, (src, dst) in enumerate(pairs):
                    sp.dma_start(dst, src).then_inc(raw_landed[plan.raw[key] % RING], 16)

            def ffn_dst(key):
                return raw_of(key)[:].rearrange("p (k n) -> p k n", k=2 if key[0] == "D" else KD)

            def in_loop(f, k, g, it):
                key = (k, f, g)
                old, later = plan.tiles[plan.raw[key] - RING], plan.tiles[plan.raw[(k, f, g + 2)] - RING]
                was, step = plan.split[old] + 1, plan.split[later] - plan.split[old]
                sp.wait_ge(w_split, it * step + was)
                sp.dma_start(ffn_dst(key), ffn_source(f, k, it * (2 * GW) + GW * g))\
                    .then_inc(raw_landed[plan.raw[key] % RING], 16)

            def side(f, g, quarters, it=None):
                if g not in SIDE_GROUPS[f]:
                    return
                l, b = SIDE_GROUPS[f][g]
                n = side_number((f, g))
                for q in quarters:
                    done = 16 * n + 4 * (q - 1)
                    if it is None:
                        if done > 0:
                            sp.wait_ge(side_summed, done)
                        src = a["w_ada"][l, 256 * q:256 * q + 256, 512 * b:512 * b + 512]
                    else:
                        sp.wait_ge(side_summed, it * 32 + done)
                        src = a["w_ada"][l, 256 * q:256 * q + 256, bass.ds(it * 1024 + 512 * b, 512)]
                    sp.dma_start(side_raw[q % 2][:], src.rearrange("(k p) n -> p k n", p=128)).then_inc(side_landed[q % 2], 16)

            order = list(plan.tiles)
            i = 0
            while i < len(order):
                key = order[i]
                if key[0] == "G" and key[2] == 3:
                    f = key[1]
                    with sp.Fori(0, 3) as it:
                        for g in (3, 4):
                            in_loop(f, "G", g, it)
                            in_loop(f, "U", g, it)
                            in_loop(f, "D", g - 1, it)
                            side(f, g - 1, (2, 3), it)
                            side(f, g, (0, 1), it)
                    i += 18
                    continue
                load(key)
                i += 1
                if key[0] == "U" and key[2] == 0:
                    f = key[1]
                    if f == 1:
                        wait_products(sp, ("O", 0, HEADS - 1, len(mix_segs(0)) - 1))
                    side(f, 0, (0, 1))
                if key[0] == "D":
                    f, g = key[1], key[2]
                    side(f, g, (2, 3))
                    side(f, g + 1, (0, 1))
            for t in range(LAT // 128):
                wait_freed(sp, ("xout", t, 1))
                sp.dma_start(a["out"][0, 128 * t:128 * t + 128, :], onat[:, t % 2, :]).then_inc(out_landed[t % 2], 16)
            for i in range(2):
                sp.wait_ge(out_landed[i], 16 * (LAT // 128 // 2))

        @block.gpsimd
        def _(pool):
            nc.gpsimd.memset(ones[:], 1.0).then_inc(pool_const, 1)
            nc.gpsimd.memset(epsc[:], EPS).then_inc(pool_const, 1)

            def split(key):
                n = plan.split[key]
                pool.wait_ge(w_hi_done, n + 1)
                pool.wait_ge(w_split, n)
                nc.gpsimd.tensor_tensor(w_lo[n % RING][:], raw_of(key)[:], w_hi[n % RING][:].bitcast(F), ALU.subtract)\
                    .then_inc(w_split, 1)

            for q in range(3 * DEPTH + 1):
                for key in POOL_SPLITS.get(q, ()):
                    if q % 3 != 2:
                        split(key)
                for s, j in square_order(q):
                    if q % 3 == 2 and (s, j) == (0, 6):
                        for key in POOL_SPLITS[q]:
                            split(key)
                    if j == 0:
                        continue
                    o, n = BOTH[s]
                    pool.wait_ge(sq_done, sqcount(q, s, j))
                    if j > 1:
                        pool.wait_ge(squares_added, addcount(q, s, j - 1))
                    nc.gpsimd.tensor_tensor(sqsum[:, o:o + n], sqsum[:, o:o + n], sq[:, j % 2, o:o + n], ALU.add)\
                        .then_inc(squares_added, 1)

        mm = nc.tensor.matmul

        def mm3(out, wh, wl, xh, xl, start, stop):
            mm(out, wh, xh, start=start, stop=False)
            mm(out, wh, xl, start=False, stop=False)
            return mm(out, wl, xh, start=False, stop=stop)

        def wk(key, k):
            i = ring(key)
            return (w_hi[i][:].rearrange("p (k n) -> p k n", k=k), w_lo[i][:].rearrange("p (k n) -> p k n", k=k))

        @block.tensor
        def _(pe):
            def wait_h(q, j, s):
                pe.wait_ge(h_ready, hcount(q, j, s))

            def wait_split(key, g=None, it=None):
                pe.wait_ge(w_split, (plan.split[key] + 1) if g is None else lin(lambda k: plan.split[k] + 1, key, g, it))

            def stat(q, s):
                o, n = BOTH[s]
                wait_bank(pe, ("stat", q, s))
                pe.wait_ge(squares_added, addcount(q, s, KD - 1))
                mm(pt(("stat", q, s), n), ones[:], sqsum[:, o:o + n], start=True, stop=True).then_inc(products, 1)

            def ada(blocks):
                pe.wait_ge(cpad_ready, 4)
                for n, b in enumerate(blocks):
                    if b == 3:
                        for s in seg_order(0):
                            stat(0, s)
                    key = ("ada", 0, b)
                    wait_bank(pe, key)
                    for k in range(KD):
                        if k % 4 == 0:
                            wait_landed(pe, key + (k // 4,))
                        q = k % 4
                        src = raw_of(key + (k // 4,))[:].rearrange("p (k n) -> p k n", k=4)
                        last = mm(ps[32 * q:32 * q + 32, bank_of(key), :], cpad[:, k, :], src[:, q, :],
                                  start=(k < 4), stop=(k >= 4), skip_group_check=True)
                        if k == 3:
                            last.then_inc(ada_half, 1)
                    last.then_inc(products, 1)
                    if n:
                        turn(blocks[n - 1])
                turn(blocks[-1])

            def turn(b):
                wait_freed(pe, ("ada", 0, b))
                key = ("adaT", 0, b)
                wait_bank(pe, key)
                for i in range(4):
                    last = mm(ps[:, bank_of(key), 2 * i:2 * i + 2],
                              part[:, FIRST_BLOCKS.index(b) % 2, 128 * i:128 * i + 128], sel[:],
                              start=True, stop=True, skip_group_check=True)
                last.then_inc(products, 1)

            def ffn(f):
                q = NORM_OF[f]
                ss = segs_of(q)

                def gate_up(g, it=None):
                    for c in range(2):
                        for w in "gu":
                            if c == 0:
                                wait_split(lambda x: (w.upper(), f, x), g, it)
                            for s in range(len(ss)):
                                wait_bank(pe, lambda x: (w, f, x, c, s), g, it)
                            wh, wl = wk((w.upper(), f, g), KD)
                            for k in range(KD):
                                for s, (o, n) in enumerate(ss):
                                    last = mm3(pt((w, f, g, c, s), n), wh[:, k, 128 * c:128 * c + 128],
                                               wl[:, k, 128 * c:128 * c + 128], h_hi[:, k, o:o + n], h_lo[:, k, o:o + n],
                                               k == 0, k == KD - 1)
                                    if k == KD - 1:
                                        last.then_inc(products, 1)

                def gate_up_first():
                    wait_split(("U", f, 0))
                    for s in seg_order(q):
                        o, n = ss[s]
                        for cs_ in ((0, 1),) if s == 1 else ((0,), (1,)):
                            for c in cs_:
                                for w in "gu":
                                    wait_bank(pe, (w, f, 0, c, s))
                            for k in range(KD):
                                if k == 2 and s == 1 and q:
                                    stat(q, 0)
                                wait_h(q, k, s)
                                for c in cs_:
                                    for w in "gu":
                                        wh, wl = wk((w.upper(), f, 0), KD)
                                        last = mm3(pt((w, f, 0, c, s), n), wh[:, k, 128 * c:128 * c + 128],
                                                   wl[:, k, 128 * c:128 * c + 128], h_hi[:, k, o:o + n],
                                                   h_lo[:, k, o:o + n], k == 0, k == KD - 1)
                                        if k == KD - 1:
                                            last.then_inc(products, 1)
                        if f == 0 and s == 1:
                            ada(BETWEEN)

                def down(g, it=None):
                    wait_split(lambda x: ("D", f, x), g, it)
                    n0 = 2 * NG * f + 2 * g + 2
                    pe.wait_ge(hid_ready, n0 if it is None else it * 4 + n0)
                    wh, wl = wk(("D", f, g), 2)
                    for j in range(KD):
                        for s, (o, n) in enumerate(ss):
                            wait_bank(pe, lambda x: ("d", f, x, j, s), g, it)
                            for c in range(2):
                                last = mm3(pt(("d", f, g, j, s), n), wh[:, c, 128 * j:128 * j + 128],
                                           wl[:, c, 128 * j:128 * j + 128], hid_hi[:, g % 2, c, o:o + n],
                                           hid_lo[:, g % 2, c, o:o + n], c == 0, c == 1)
                            last.then_inc(products, 1)
                        if j == SIDE_AT:
                            side(g + 1, it)

                def side(g, it=None):
                    if g not in SIDE_GROUPS[f]:
                        return
                    key = lambda x: ("side", f, x)
                    n16 = 16 * (side_number((f, g)) + 1)
                    pe.wait_ge(side_summed, n16 if it is None else it * 32 + n16)
                    wait_bank(pe, key, g, it)
                    rows = side_acc[:].rearrange("p v (j q n) -> p q (v j) n", q=4, n=32)
                    for q in range(4):
                        last = mm(ps[32 * q:32 * q + 32, bank_of(key(g)), 0:256].rearrange("p (j n) -> p j n", n=32),
                                  ones[:, 0:32], rows[:, q], start=True, stop=True, skip_group_check=True)
                    last.then_inc(products, 1)

                gate_up_first()
                side(0)
                with pe.Fori(0, (NG - 3) // 2) as it:
                    gate_up(1, it)
                    down(0, it)
                    gate_up(2, it)
                    down(1, it)
                for g in (NG - 2, NG - 1):
                    gate_up(g)
                    down(g - 1)
                g, after = NG - 1, (1, 3, 4, 6)[f]
                wait_split(("D", f, g))
                pe.wait_ge(hid_ready, 2 * NG * f + 2 * g + 2)
                wh, wl = wk(("D", f, g), 2)
                for s in seg_order(q):
                    o, n = ss[s]
                    for j in range(KD):
                        key = ("d", f, g, j, s)
                        wait_bank(pe, key)
                        for c in range(2):
                            last = mm3(pt(key, n), wh[:, c, 128 * j:128 * j + 128], wl[:, c, 128 * j:128 * j + 128],
                                       hid_hi[:, g % 2, c, o:o + n], hid_lo[:, g % 2, c, o:o + n], c == 0, c == 1)
                        last.then_inc(products, 1)
                        if s == 0 and j == 3 and len(ss) == 2:
                            stat(after, 1)
                if len(ss) == 1:
                    stat(after, 0)

            def columns(key, outs, q):
                wait_split(key)
                wh, wl = wk(key, KD)
                for slot, _, _ in outs:
                    wait_bank(pe, slot)
                for k in range(KD):
                    for slot, col, (o, n) in outs:
                        last = mm3(pt(slot, n), wh[:, k, col:col + 128], wl[:, k, col:col + 128],
                                   h_hi[:, k, o:o + n], h_lo[:, k, o:o + n], k == 0, k == KD - 1)
                        if k == KD - 1:
                            last.then_inc(products, 1)

            def rows(key, slots, q=None):
                wait_split(key)
                wh, wl = wk(key, KD)
                for t, slot in slots:
                    wait_bank(pe, slot)
                for k in range(KD):
                    if q is not None:
                        if k == 5 and slots[0][1] == ("V", key[1], 0, 4):
                            stat(q, 0)
                        wait_h(q, k, 0 if slots[0][0] < 4 else 1)
                    for t, slot in slots:
                        last = mm3(pt(slot, 256), h_hi[:, k, 128 * t:128 * t + 128], h_lo[:, k, 128 * t:128 * t + 128],
                                   wh[:, k, :], wl[:, k, :], k == 0, k == KD - 1)
                        if k == KD - 1:
                            last.then_inc(products, 1)

            def mix(l):
                ms = mix_segs(l)
                ns = len(ms)
                q = 3 * l + 1
                for ts in ((4, 5), (0, 1, 2, 3)):
                    for v in range(2):
                        rows(("V", l, v), [(t, ("V", l, v, t)) for t in ts], q)
                for c in range(2):
                    columns(("conv", l, c), [(("conv" + w, l, c, s), 128 if w == "g" else 0, ms[s])
                                             for w in "ga" for s in range(ns)], q)
                rows(("four", l), [(t, ("X", l, t)) for t in range(sum(n for _, n in ms) // 128)])
                for w, ss in (("Q", ms), ("K", BOTH)):
                    for v in range(2):
                        columns((w, l, v), [((w, l, 2 * v + c, s), 128 * c, ss[s]) for c in range(2)
                                            for s in range(len(ss))], q)
                fourier(l)
                conv_tail(l)
                attention(l)
                for h in range(HEADS):
                    for s, (o, n) in enumerate(ms):
                        key = ("hn", l, h, s)
                        wait_bank(pe, key)
                        pe.wait_ge(hsq_done, HEADS * sum(len(mix_segs(x)) for x in range(l)) + h * ns + s + 1)
                        mm(pt(key, n), ones[:], hsq[:, h, o:o + n], start=True, stop=True).then_inc(products, 1)
                order = (6, 7, 4, 5, 0, 1, 2, 3)
                for v, s in out_order(l):
                    key = ("out", l, v)
                    wait_split(key)
                    wh, wl = wk(key, KD)
                    o, n = ms[s]
                    outs = [(("out", l, 2 * v + c, s), 128 * c) for c in range(2)]
                    for slots in ((outs,) if v == 0 else ((x,) for x in outs)):
                        for slot, _ in slots:
                            wait_bank(pe, slot)
                        for i, k in enumerate(order):
                            if v == 0 and k >= 6:
                                wait_freed(pe, ("Fo", l, k - 6, s))
                            elif v == 0 and k >= 4:
                                wait_freed(pe, ("pw", l, k - 4, s))
                            elif v == 0:
                                pe.wait_ge(mix_ready, HEADS * sum(len(mix_segs(x)) for x in range(l)) + k * ns + s + 1)
                            for slot, col in slots:
                                last = mm3(pt(slot, n), wh[:, k, col:col + 128], wl[:, k, col:col + 128],
                                           h_hi[:, k, o:o + n], h_lo[:, k, o:o + n], i == 0, i == KD - 1)
                                if i == KD - 1:
                                    last.then_inc(products, 1)
                        if slots[0][0] == ("out", l, 4, 0) and ns == 2:
                            stat(q + 1, 1)
                if ns == 1:
                    stat(q + 1, 0)

            def fourier(l):
                ms = mix_segs(l)
                small = raw_of(("W", l))[:].rearrange("p (i k n) -> p i k n", i=4, k=2)
                wait_landed(pe, ("C", l))
                wait_landed(pe, ("S", l))
                wait_landed(pe, ("W", l))
                wait_freed(pe, ("X", l, sum(n for _, n in ms) // 128 - 1))
                wait_freed(pe, ("X", l, sum(n for _, n in ms) // 128 - 2))
                for j in range(2):
                    for w in "CS":
                        big = raw_of((w, l))[:].rearrange("p (k n) -> p k n", k=4)
                        for s, (o, n) in enumerate(ms):
                            key = ("Z", l, j, w, s)
                            wait_bank(pe, key)
                            nk = n // 128
                            for k in range(nk):
                                table = big[:, k, :] if s == 0 else small[:, 2 if w == "C" else 3, k, :]
                                last = mm(pt(key, n), xN[:, o // 128 + k, 128 * j:128 * j + 128], table,
                                          start=(k == 0), stop=(k == nk - 1))
                            last.then_inc(products, 1)
                for j in range(2):
                    for s, (o, n) in enumerate(ms):
                        key = ("F", l, j, s)
                        wait_bank(pe, key)
                        for i, w in enumerate("CS"):
                            wait_freed(pe, ("Z", l, j, w, s))
                            last = mm(pt(key, n), dft[:, i, :], zT[:, j, i, o:o + n], start=(i == 0), stop=(i == 1))
                        last.then_inc(products, 1)
                for p in range(2):
                    for s, (o, n) in enumerate(ms):
                        key = ("Fo", l, p, s)
                        wait_bank(pe, key)
                        for j in range(2):
                            wait_freed(pe, ("F", l, j, s))
                            last = mm(pt(key, n), small[:, 1, j, 128 * p:128 * p + 128], fT[:, j, o:o + n],
                                      start=(j == 0), stop=(j == 1))
                        last.then_inc(products, 1)

            def conv_tail(l):
                ms = mix_segs(l)
                small = raw_of(("W", l))[:].rearrange("p (i k n) -> p i k n", i=4, k=2)
                ns = len(ms)
                pe.wait_ge(acc_ready, 2 * (l + 1))
                for s, (o, n) in enumerate(ms):
                    key = ("mean", l, s)
                    wait_bank(pe, key)
                    ao = 0 if s == 0 else C_CTX - HALF
                    for c in range(2):
                        last = mm(pt(key, n), ones[:], acc[:, c, ao:ao + n], start=(c == 0), stop=(c == 1))
                    last.then_inc(products, 1)
                before = 2 * sum(len(mix_segs(x)) for x in range(l))
                for s, (o, n) in enumerate(ms):
                    key = ("var", l, s)
                    wait_bank(pe, key)
                    pe.wait_ge(csq_done, before + 2 * s + 2)
                    for c in range(2):
                        last = mm(pt(key, n), ones[:], csq[:, c, o:o + n], start=(c == 0), stop=(c == 1))
                    last.then_inc(products, 1)
                for p in range(2):
                    for s, (o, n) in enumerate(ms):
                        key = ("pw", l, p, s)
                        wait_bank(pe, key)
                        pe.wait_ge(cs_done, before + 2 * s + 2)
                        for c in range(2):
                            last = mm(pt(key, n), small[:, 0, c, 128 * p:128 * p + 128], cs[:, c, o:o + n],
                                      start=(c == 0), stop=(c == 1))
                        last.then_inc(products, 1)

            def attention(l):
                us = units_of(l)
                ms = mix_segs(l)
                e_before = 2 * sum(len(units_of(x)) for x in range(l))
                u_before = e_before // 2
                for b in range(6):
                    pe.wait_ge(bank_free[b], plan.before_att[l][b])
                for i in range(len(us) + 3):
                    if i < len(us):
                        h, s, t = us[i]
                        if t == 0 and s == 0:
                            pe.wait_ge(q_ready, HEADS * l + h + 1)
                            pe.wait_ge(k_ready, HEADS * l + h + 1)
                            wait_freed(pe, ("K", l, h, 1))
                        if i >= 2:
                            pe.wait_ge(exp_done, e_before + 2 * (i - 1))
                        at0 = 1536 * (i % 2)
                        o = ms[s][0] + 128 * t
                        if s == 0:
                            parts = ((0, 0, 0, 512), (0, 512, 512, 256), (1, 768, 512, 256), (1, 1024, 0, 512))
                        else:
                            parts = ((0, 0, 512, 256), (1, 256, 512, 256))
                        for st, po, ko, n in parts:
                            last = mm(pflat[:, at0 + po:at0 + po + n], qpad[:, h % 2, st, o:o + 128],
                                      kT[:, h, ko:ko + n], start=True, stop=True, skip_group_check=True)
                        last.then_inc(products, 1)

                    def turn_p(half):
                        u = i - 2
                        h, s, t = us[u]
                        key = ("T", l, u, half)
                        wait_bank(pe, key)
                        if half == 0:
                            pe.wait_ge(p_ready, u_before + u + 1)
                        ks = range(0, 4) if (s == 0 and half == 0) else range(4, 6) if s == 0 else range(2)
                        for n, k in enumerate(ks):
                            last = nc.tensor.transpose(ps[:, 6, 128 * n:128 * n + 128], e0[:, u % 3, 128 * k:128 * k + 128], ident[:])
                        last.then_inc(products, 1)

                    if 0 <= i - 2 < len(us):
                        turn_p(0)
                    if 0 <= i - 3 < len(us):
                        u = i - 3
                        h, s, t = us[u]
                        key = ("O", l, h, s)
                        if t == 0:
                            wait_bank(pe, key)
                        wait_freed(pe, ("T", l, u, 1 if s == 0 else 0))
                        ks = range(6) if s == 0 else range(4, 6)
                        for k in ks:
                            last = mm(ps[:, 7, 128 * t:128 * t + 128], vN[:, k, 128 * h:128 * h + 128],
                                      pT[:, u % 2, k if s == 0 else k - 4, :], start=(k == ks[0]), stop=(k == 5),
                                      skip_group_check=True)
                        if t == ms[s][1] // 128 - 1:
                            last.then_inc(products, 1)
                    if 0 <= i - 2 < len(us) and us[i - 2][1] == 0:
                        turn_p(1)
                pe.wait_ge(exp_done, e_before + 2 * len(us))

            pe.wait_ge(const_landed, 16 * N_CONST)
            for i, n in enumerate((NROW, NROW, 2 * 2 * TAPS, 3 * KD)):
                nc.tensor.transpose(ps[:, bank_of(("vec", i)), 0:n], vstage[0:n, i, :], ident[0:n, 0:n]).then_inc(products, 1)
            pe.wait_ge(x_landed, 16 * (TOK // 128))
            for s, (o, n) in enumerate(BOTH):
                for j in range(KD):
                    key = ("xin", s, j)
                    wait_bank(pe, key)
                    for t in range(n // 128):
                        last = nc.tensor.transpose(ps[:, bank_of(key), 128 * t:128 * t + 128],
                                                   xnat[:, o // 128 + t, 128 * j:128 * j + 128], ident[:])
                    last.then_inc(products, 1)
            pe.wait_ge(pool_const, 2)
            ada(BEFORE)
            for l in range(DEPTH):
                ffn(2 * l)
                mix(l)
                ffn(2 * l + 1)
            pe.wait_ge(y_done, KD)
            for t in range(LAT // 128):
                for half in range(2):
                    key = ("xout", t, half)
                    wait_bank(pe, key)
                    for i in range(4):
                        last = nc.tensor.transpose(ps[:, bank_of(key), 128 * i:128 * i + 128],
                                                   xT[:, 4 * half + i, 128 * t:128 * t + 128], ident[:])
                    last.then_inc(products, 1)

        act_fn = nc.scalar.activation

        def x_written(q, j, s):
            if q == 0:
                return ("xin", s, j)
            return ("out", (q - 2) // 3, j, s) if q % 3 == 2 else ("d", {1: 0, 3: 1, 4: 2, 6: 3}[q], NG - 1, j, s)

        @block.scalar
        def _(act):
            steps = [0]

            def split(key, g=None, it=None):
                k0 = key if g is None else key(g)
                wait_landed(act, key, g, it)
                s = plan.split[k0]
                if s >= RING:
                    old = plan.lastuse[split_keys[s - RING]]
                    if g is None:
                        wait_products(act, old)
                    else:
                        step = number(plan.lastuse[split_keys[plan.split[key(g + 2)] - RING]]) - number(old)
                        act.wait_ge(products, number(old) if it is None else it * step + number(old))
                act_fn(w_hi[s % RING][:], raw_of(k0)[:], ACT.Copy).then_inc(w_hi_done, 1)

            def square(q, s, j):
                o, n = BOTH[s]
                wait_freed(act, x_written(q, j, s))
                if j >= 3:
                    act.wait_ge(squares_added, addcount(q, s, j - 2))
                act_fn(sqsum[:, o:o + n] if j == 0 else sq[:, j % 2, o:o + n], xT[:, j, o:o + n], ACT.Square)\
                    .then_inc(sq_done, 1)

            def root(q, s):
                o, n = BOTH[s]
                key = ("stat", q, s)
                wait_products(act, key)
                act_fn(std[:, o:o + n], pt(key, n), ACT.Sqrt, bias=epsc[:], scale=1.0 / D).then_inc(bank_free[bank_of(key)], 1)

            def high(q, s, js=range(KD)):
                o, n = BOTH[s]
                for j in js:
                    act.wait_ge(t_done, hcount(q, j, s))
                    act_fn(h_hi[:, j, o:o + n], tn[:, j % 2, o:o + n], ACT.Identity,
                           bias=mod[:, q // 3, 24 * (q % 3) + j, s:s + 1], scale=1.0).then_inc(h_hi_done, 1)

            def ada(blocks):
                for b in blocks:
                    if b == 1:
                        for s, j in square_order(0):
                            square(0, s, j)
                    if b == 3:
                        for s in seg_order(0):
                            root(0, s)
                    key = ("ada", 0, b)
                    wait_products(act, key)
                    n = FIRST_BLOCKS.index(b)
                    if n >= 2:
                        wait_products(act, ("adaT", 0, FIRST_BLOCKS[n - 2]))
                    act_fn(part[:, n % 2, :], pt(key), ACT.Copy).then_inc(bank_free[bank_of(key)], 1)

            def ffn(f, nxt):
                ss = segs_of(NORM_OF[f])

                def hidden(g, it=None):
                    for c in range(2):
                        for s, (o, n) in enumerate(ss):
                            wait_products(act, lambda x: ("g", f, x, c, s), g, it)
                            act_fn(sil[:, c, o:o + n], pt(("g", f, g, c, s), n), ACT.Silu)\
                                .then_inc(bank_free[bank_of(("g", f, g, c, s))], 1)
                        wait_freed(act, lambda x: ("u", f, x, c, len(ss) - 1), g, it)
                        last_o = ss[-1][0] + ss[-1][1]
                        act_fn(hid_hi[:, g % 2, c, 0:last_o], prod[:, c, 0:last_o], ACT.Copy).then_inc(hid_hi_done, 1)

                def groups(g, it=None):
                    hidden(g, it)
                    split(lambda x: ("G", f, x), g + 1, it)
                    split(lambda x: ("U", f, x), g + 1, it)
                    split(lambda x: ("D", f, x), g, it)

                split(("G", f, 1))
                hidden(0)
                split(("U", f, 1))
                split(("D", f, 0))
                with act.Fori(0, (NG - 3) // 2) as it:
                    groups(1, it)
                    groups(2, it)
                hidden(NG - 2)
                split(("G", f, NG - 1))
                split(("U", f, NG - 1))
                split(("D", f, NG - 2))
                hidden(NG - 1)
                split(("D", f, NG - 1))
                for key in nxt:
                    split(key)
                q = (1, 3, 4, 6)[f]
                if len(ss) == 1:
                    for j in range(KD):
                        square(q, 0, j)
                    root(q, 0)
                    return
                for j in range(KD):
                    square(q, 1, j)
                for j in range(4):
                    square(q, 0, j)
                root(q, 1)
                for j in range(4, KD):
                    square(q, 0, j)
                    high(q, 1, (j - 4,))
                high(q, 1, range(4, KD))
                root(q, 0)
                high(q, 0)

            def mix(l):
                ms = mix_segs(l)
                ns = len(ms)

                def copy(key, dst, n):
                    wait_products(act, key)
                    act_fn(dst, pt(key, n), ACT.Copy).then_inc(bank_free[bank_of(key)], 1)

                rest = iter([("conv", l, 0), ("conv", l, 1), ("four", l), ("Q", l, 0), ("Q", l, 1), ("K", l, 0), ("K", l, 1),
                             ("out", l, 0), ("out", l, 1), ("out", l, 2), ("out", l, 3)])
                split(next(rest))
                for ts in ((4, 5), (0, 1, 2, 3)):
                    for v in range(2):
                        for t in ts:
                            copy(("V", l, v, t), vN[:, t, 256 * v:256 * v + 256], 256)
                        if t == 3:
                            split(next(rest))
                for c in range(2):
                    for s, (o, n) in enumerate(ms):
                        key = ("convg", l, c, s)
                        wait_products(act, key)
                        at0 = (C_LAT, C_CTX)[s]
                        act_fn(yline[:, c, at0:at0 + n], pt(key, n), ACT.Sigmoid).then_inc(bank_free[bank_of(key)], 1)
                    split(next(rest))
                for t in range(sum(n for _, n in ms) // 128):
                    copy(("X", l, t), xN[:, t, :], 256)
                split(next(rest))
                for h in range(HEADS):
                    for s, (o, n) in enumerate(ms):
                        copy(("Q", l, h, s), qT[:, h, o:o + n], n)
                    if h == 1:
                        split(next(rest))
                for h in range(HEADS):
                    copy(("K", l, h, 1), kT[:, h, LAT:TOK], CTX)
                for j in range(2):
                    for i, w in enumerate("CS"):
                        for s, (o, n) in enumerate(ms):
                            copy(("Z", l, j, w, s), zT[:, j, i, o:o + n], n)
                for j in range(2):
                    for s, (o, n) in enumerate(ms):
                        copy(("F", l, j, s), fT[:, j, o:o + n], n)

                def biased(kind, name, chunk0):
                    for p in range(2):
                        for s, (o, n) in enumerate(ms):
                            key = (kind, l, p, s)
                            wait_products(act, key)
                            col = ROW[name][0] + p
                            act_fn(h_hi[:, chunk0 + p, o:o + n], pt(key, n), ACT.Identity,
                                   bias=vcol[:, l, col:col + 1], scale=1.0).then_inc(mix_hi_done, 1)

                biased("Fo", "b_fourier", 6)
                before = 2 * sum(len(mix_segs(x)) for x in range(l))
                for s, (o, n) in enumerate(ms):
                    wait_freed(act, ("mean", l, s))
                    ao = 0 if s == 0 else C_CTX - HALF
                    for c in range(2):
                        act_fn(csq[:, c, o:o + n], acc[:, c, ao:ao + n], ACT.Square).then_inc(csq_done, 1)
                for s, (o, n) in enumerate(ms):
                    key = ("var", l, s)
                    wait_products(act, key)
                    act_fn(cst[:, o:o + n], pt(key, n), ACT.Sqrt, bias=epsc[:], scale=1.0 / CONVW)\
                        .then_inc(bank_free[bank_of(key)], 1)
                g0, b0 = ROW["g_conv_ln"][0], ROW["b_conv_ln"][0]
                for s, (o, n) in enumerate(ms):
                    ao = 0 if s == 0 else C_CTX - HALF
                    for c in range(2):
                        act.wait_ge(cn_done, before + 2 * s + c + 1)
                        act_fn(cs[:, c, o:o + n], acc[:, c, ao:ao + n], ACT.Silu, bias=vcol[:, l, b0 + c:b0 + c + 1],
                               scale=vcol[:, l, g0 + c:g0 + c + 1]).then_inc(cs_done, 1)
                biased("pw", "b_pw", 4)
                us = units_of(l)
                u_before = sum(len(units_of(x)) for x in range(l))
                for i in range(len(us) + 3):
                    if 0 <= i - 2 < len(us):
                        u = i - 2
                        h, s, t = us[u]
                        for half in range(2 if s == 0 else 1):
                            key = ("T", l, u, half)
                            wait_products(act, key)
                            k0, n = (4, 2) if half else (0, 4 if s == 0 else 2)
                            act_fn(pT[:, u % 2, k0:k0 + n, :], ps[:, 6, 0:128 * n].rearrange("p (k n) -> p k n", k=n),
                                   ACT.Copy).then_inc(bank_free[6], 1)
                    if i < len(us):
                        h, s, t = us[i]
                        act.wait_ge(max_done, u_before + i + 1)
                        at0, n = 1536 * (i % 2), TOK if s == 0 else CTX
                        for st, dst in ((0, e0[:, i % 3, 0:n]), (1, e1[:, i % 2, 0:n])):
                            act_fn(dst, pflat[:, at0 + n * st:at0 + n * st + n], ACT.Exp, bias=nb[:, i % 2, st:st + 1],
                                   scale=HD ** -0.5, accum_out=sums[:, i % 2, st:st + 1]).then_inc(exp_done, 1)
                    if 0 <= i - 3 < len(us):
                        h, s, t = us[i - 3]
                        if t == ms[s][1] // 128 - 1:
                            o, n = ms[s]
                            copy(("O", l, h, s), qT[:, h, o:o + n], n)
                    if i in (4, 6, 8):
                        split(next(rest))
                for h in range(HEADS):
                    for s, (o, n) in enumerate(ms):
                        if h == HEADS - 1 or h == 0:
                            wait_freed(act, ("O", l, h, s))
                        act_fn(hsq[:, h, o:o + n], qT[:, h, o:o + n], ACT.Square).then_inc(hsq_done, 1)
                for h in range(HEADS):
                    for s, (o, n) in enumerate(ms):
                        key = ("hn", l, h, s)
                        wait_products(act, key)
                        act_fn(hst[:, h, o:o + n], pt(key, n), ACT.Sqrt, bias=epsc[:], scale=1.0 / 128)\
                            .then_inc(bank_free[bank_of(key)], 1)
                hbefore = HEADS * sum(len(mix_segs(x)) for x in range(l))
                for h in range(HEADS):
                    for s, (o, n) in enumerate(ms):
                        act.wait_ge(ht_done, hbefore + h * ns + s + 1)
                        act_fn(h_hi[:, h, o:o + n], qT[:, h, o:o + n], ACT.Copy).then_inc(mix_hi_done, 1)
                split(next(rest))
                q = 3 * l + 2
                if ns == 1:
                    for j in range(4):
                        square(q, 0, j)
                    split(("G", 2 * l + 1, 0))
                    square(q, 0, 4)
                    square(q, 0, 5)
                    split(("U", 2 * l + 1, 0))
                    square(q, 0, 6)
                    square(q, 0, 7)
                    root(q, 0)
                    high(q, 0)
                    return
                for j in range(4):
                    square(q, 0, j)
                    square(q, 1, j)
                split(("G", 2 * l + 1, 0))
                for j in range(4, KD):
                    square(q, 1, j)
                square(q, 0, 4)
                root(q, 1)
                high(q, 1, (0, 1))
                square(q, 0, 5)
                split(("U", 2 * l + 1, 0))
                high(q, 1, (2, 3, 4))
                square(q, 0, 6)
                high(q, 1, (5, 6, 7))
                square(q, 0, 7)
                root(q, 0)
                high(q, 0)

            for i, (n, dst) in enumerate(((NROW, vcol[:, 0, :]), (NROW, vcol[:, 1, :]),
                                          (4 * TAPS, wdw[:].rearrange("p l t c -> p (l t c)")),
                                          (3 * KD, ccol[:].rearrange("p i k -> p (i k)")))):
                wait_products(act, ("vec", i))
                act_fn(dst, ps[:, bank_of(("vec", i)), 0:n], ACT.Copy).then_inc(bank_free[bank_of(("vec", i))], 1)
            act.wait_ge(pool_const, 2)
            wait_freed(act, ("vec", 3))
            act.wait_ge(lam_dot, 1)
            act_fn(lamw[:, 0:2 * DEPTH], lamw[:, 0:2 * DEPTH], ACT.Exp).then_inc(lam_exp, 1)
            act.wait_ge(pad_zeroed, 1)
            for v in range(2):
                act_fn(cpad[:, :, v], ccol[:, v, :], ACT.Silu).then_inc(cpad_ready, 1)
                act_fn(ccol[:, v, :], ccol[:, v, :], ACT.Silu).then_inc(cpad_ready, 1)
            ada(BEFORE)
            split(("G", 0, 0))
            split(("U", 0, 0))
            high(0, 1)
            ada(BETWEEN)
            high(0, 0)
            for l in range(DEPTH):
                ffn(2 * l, [("V", l, 0), ("V", l, 1)])
                mix(l)
                ffn(2 * l + 1, [("G", 2 * l + 2, 0), ("U", 2 * l + 2, 0)] if l < DEPTH - 1 else [])
            for t in range(LAT // 128):
                if t >= 2:
                    act.wait_ge(out_landed[t % 2], 16 * (t // 2))
                for half in range(2):
                    key = ("xout", t, half)
                    wait_products(act, key)
                    act_fn(onat[:, t % 2, 512 * half:512 * half + 512], pt(key), ACT.Copy)\
                        .then_inc(bank_free[bank_of(key)], 1)

        dve_ = nc.vector
        tt, stt = dve_.tensor_tensor, dve_.scalar_tensor_tensor

        @block.vector
        def _(dve):
            steps = [0]

            def step(ins):
                ins.then_inc(dve_step, 1)
                steps[0] += 1
                return steps[0]

            def settle(back=0):
                if steps[0] - back > 0:
                    dve.wait_ge(dve_step, steps[0] - back)

            def split(key, g=None, it=None):
                k0 = key if g is None else key(g)
                s = plan.split[k0]
                if g is None and s and any(split_keys[s - 1] in x for x in POOL_SPLITS.values()):
                    dve.wait_ge(w_split, s)
                dve.wait_ge(w_hi_done, s + 1 if g is None else lin(lambda k: plan.split[k] + 1, key, g, it))
                tt(w_lo[s % RING][:], raw_of(k0)[:], w_hi[s % RING][:].bitcast(F), ALU.subtract).then_inc(w_split, 1)

            def over_rms(q, s):
                o, n = BOTH[s]
                wait_freed(dve, ("stat", q, s))
                step(dve_.reciprocal(rstd[:, o:o + n], std[:, o:o + n]))
                settle()

            def scaled(q, s, js=range(KD)):
                o, n = BOTH[s]
                for j in js:
                    if j >= 2:
                        dve.wait_ge(h_ready, hcount(q, j - 2, s))
                    stt(out=tn[:, j % 2, o:o + n], in0=xT[:, j, o:o + n], scalar=amul[:, q // 3, q % 3, j, s:s + 1],
                        in1=rstd[:, o:o + n], op0=ALU.mult, op1=ALU.mult).then_inc(t_done, 1)
                    if j:
                        low(q, s, j - 1)
                    if j == KD - 1:
                        low(q, s, j)

            def low(q, s, j):
                o, n = BOTH[s]
                dve.wait_ge(h_hi_done, hcount(q, j, s))
                stt(out=h_lo[:, j, o:o + n], in0=tn[:, j % 2, o:o + n], scalar=mod[:, q // 3, 24 * (q % 3) + j, s:s + 1],
                    in1=h_hi[:, j, o:o + n].bitcast(F), op0=ALU.add, op1=ALU.subtract).then_inc(h_ready, 1)

            def ada(blocks):
                for b in blocks:
                    key = ("adaT", 0, b)
                    wait_products(dve, key)
                    dve_.tensor_copy(mod[:, 0, 4 * b:4 * b + 4, :],
                                     ps[:, bank_of(key), 0:8].rearrange("p (j v) -> p j v", v=2)).then_inc(bank_free[bank_of(key)], 1)
                for b in blocks:
                    wait_freed(dve, ("adaT", 0, b))

            def shift_scale(l, i):
                m = slice(24 * i, 24 * i + 16)
                for v in range(2):
                    step(tt(mod[:, l, m, v], mod[:, l, m, v], vcol[:, l, m], ALU.add))
                settle()
                g0 = ROW[("g_ffn1", "g_mix", "g_ffn2")[i]][0]
                for v in range(2):
                    step(stt(out=amul[:, l, i, :, v], in0=mod[:, l, 24 * i + 8:24 * i + 16, v], scalar=1.0,
                             in1=vcol[:, l, g0:g0 + KD], op0=ALU.add, op1=ALU.mult))
                settle()

            def gates(l, i):
                m = slice(24 * i + 16, 24 * i + 24)
                for v in range(2):
                    step(tt(mod[:, l, m, v], mod[:, l, m, v], vcol[:, l, m], ALU.add))
                settle()
                step(dve_.tensor_scalar(gate[:, l, i, :, :], mod[:, l, m, :], 1.0 if i == 1 else 0.5, None, ALU.mult))
                settle()

            def ffn(f):
                ss = segs_of(NORM_OF[f])
                i = 2 * (f % 2)

                def side(g, quarters, it=None):
                    if g not in SIDE_GROUPS[f]:
                        return
                    n = side_number((f, g))

                    def counted(extra):
                        return 16 * n + extra if it is None else it * 32 + (16 * n + extra)

                    for q in quarters:
                        landed = 16 * (2 * n + q // 2 + 1)
                        dve.wait_ge(side_landed[q % 2], landed if it is None else it * 64 + landed)
                        for k in range(2):
                            for v in range(2):
                                w, c = side_raw[q % 2][:, k, :], ccol[:, v, 2 * q + k:2 * q + k + 1]
                                m = 4 * q + 2 * k + v
                                if m < 2:
                                    ins = dve_.tensor_scalar(side_acc[:, v, :], w, c, None, ALU.mult)
                                else:
                                    dve.wait_ge(side_summed, counted(m - 1))
                                    ins = stt(out=side_acc[:, v, :], in0=w, scalar=c, in1=side_acc[:, v, :],
                                              op0=ALU.mult, op1=ALU.add)
                                ins.then_inc(side_summed, 1)

                def side_end(g, it=None):
                    if g not in SIDE_GROUPS[f]:
                        return
                    key = lambda x: ("side", f, x)
                    l, b = SIDE_GROUPS[f][g]
                    n = side_number((f, g))
                    wait_products(dve, key, g, it)
                    if n:
                        dve.wait_ge(side_done, n if it is None else it * 2 + n)
                    dve_.transpose(side_col[:].rearrange("p j n -> p (j n)"), ps[:, bank_of(key(g)), 0:256])\
                        .then_inc(bank_free[bank_of(key(g))], 1)
                    wait_freed(dve, key, g, it)
                    at_ = 4 * b if it is None else it * 8 + 4 * b
                    dve_.tensor_copy(mod[:, l, bass.ds(at_, 4), :],
                                     side_col[:, :, 0].rearrange("p (v j) -> p j v", v=2)).then_inc(side_done, 1)

                def hidden(g, it=None):
                    side(g, (0, 1), it)
                    for c in range(2):
                        if c == 1:
                            side(g, (2, 3), it)
                        n0 = 2 * NG * f + 2 * g + c + 1
                        if n0 > 2:
                            dve.wait_ge(hid_ready, n0 - 2 if it is None else it * 4 + (n0 - 2))
                        for s, (o, n) in enumerate(ss):
                            wait_freed(dve, lambda x: ("g", f, x, c, s), g, it)
                            wait_products(dve, lambda x: ("u", f, x, c, s), g, it)
                            tt(prod[:, c, o:o + n], sil[:, c, o:o + n], pt(("u", f, g, c, s), n), ALU.mult)\
                                .then_inc(bank_free[bank_of(("u", f, g, c, s))], 1)
                        dve.wait_ge(hid_hi_done, n0 if it is None else it * 4 + n0)
                        e = ss[-1][0] + ss[-1][1]
                        tt(hid_lo[:, g % 2, c, 0:e], prod[:, c, 0:e], hid_hi[:, g % 2, c, 0:e].bitcast(F), ALU.subtract)\
                            .then_inc(hid_ready, 1)

                def add(g, js, it=None):
                    for j in js:
                        for s, (o, n) in enumerate(ss):
                            wait_products(dve, lambda x: ("d", f, x, j, s), g, it)
                            stt(out=xT[:, j, o:o + n], in0=pt(("d", f, g, j, s), n), scalar=gate[:, f // 2, i, j, s:s + 1],
                                in1=xT[:, j, o:o + n], op0=ALU.mult, op1=ALU.add)\
                                .then_inc(bank_free[bank_of(("d", f, g, j, s))], 1)

                def add_one(j, s):
                    o, n = ss[s]
                    key = ("d", f, NG - 1, j, s)
                    wait_products(dve, key)
                    stt(out=xT[:, j, o:o + n], in0=pt(key, n), scalar=gate[:, f // 2, i, j, s:s + 1],
                        in1=xT[:, j, o:o + n], op0=ALU.mult, op1=ALU.add).then_inc(bank_free[bank_of(key)], 1)

                def groups(g, it=None):
                    hidden(g, it)
                    add(g - 1, range(0, 2), it)
                    split(lambda x: ("G", f, x), g + 1, it)
                    add(g - 1, range(2, 4), it)
                    split(lambda x: ("U", f, x), g + 1, it)
                    add(g - 1, range(4, SIDE_AT + 1), it)
                    side_end(g, it)
                    add(g - 1, range(SIDE_AT + 1, KD), it)
                    split(lambda x: ("D", f, x), g, it)

                split(("G", f, 1))
                hidden(0)
                split(("U", f, 1))
                split(("D", f, 0))
                side_end(0)
                with dve.Fori(0, (NG - 3) // 2) as it:
                    groups(1, it)
                    groups(2, it)
                groups_last = NG - 2
                hidden(groups_last)
                add(groups_last - 1, range(0, 2))
                split(("G", f, NG - 1))
                add(groups_last - 1, range(2, 4))
                split(("U", f, NG - 1))
                add(groups_last - 1, range(4, SIDE_AT + 1))
                side_end(NG - 2)
                add(groups_last - 1, range(SIDE_AT + 1, KD))
                split(("D", f, NG - 2))
                hidden(NG - 1)
                add(NG - 2, range(0, 4))
                split(("D", f, NG - 1))
                add(NG - 2, range(4, SIDE_AT + 1))
                side_end(NG - 1)
                add(NG - 2, range(SIDE_AT + 1, KD))
                q = (1, 3, 4, 6)[f]
                if len(ss) == 1:
                    for j in range(KD):
                        add_one(j, 0)
                    over_rms(q, 0)
                    for j in range(KD):
                        stt(out=xT[:, j, 0:LAT], in0=xT[:, j, 0:LAT], scalar=ccol[:, 2, j:j + 1], in1=rstd[:, 0:LAT],
                            op0=ALU.mult, op1=ALU.mult).then_inc(y_done, 1)
                    return
                for j in range(KD):
                    add_one(j, 1)
                for j in range(4):
                    add_one(j, 0)
                if SIDE_GROUPS[f]:
                    dve.wait_ge(side_done, side_number((f, max(SIDE_GROUPS[f]))) + 1)
                shift_scale(q // 3, q % 3)
                over_rms(q, 1)
                for j in range(4, KD):
                    add_one(j, 0)
                    scaled(q, 1, (j - 4,))
                scaled(q, 1, range(4, KD))
                over_rms(q, 0)
                scaled(q, 0)

            def mix(l):
                ms = mix_segs(l)
                ns = len(ms)
                n_line = LAT if ns == 1 else LAT + HALF + CTX
                gates(l, 1)
                shift_scale(l, 2)
                gates(l, 2)
                for c in range(2):
                    for at0 in (0, C_LAT + LAT, C_CTX + CTX)[:ns + 1]:
                        step(dve_.memset(yline[:, c, at0:at0 + HALF], 0.0))
                rest = iter([("conv", l, 0), ("conv", l, 1), ("four", l), ("Q", l, 0), ("Q", l, 1), ("K", l, 0), ("K", l, 1),
                             ("out", l, 0), ("out", l, 1), ("out", l, 2), ("out", l, 3)])
                for _ in range(3):
                    split(next(rest))
                for c in range(2):
                    for s, (o, n) in enumerate(ms):
                        at0 = (C_LAT, C_CTX)[s]
                        wait_freed(dve, ("convg", l, c, s))
                        key = ("conva", l, c, s)
                        wait_products(dve, key)
                        tt(yline[:, c, at0:at0 + n], pt(key, n), yline[:, c, at0:at0 + n], ALU.mult)\
                            .then_inc(bank_free[bank_of(key)], 1)
                    split(next(rest))
                settle()
                for c in range(2):
                    for s in range(ns):
                        wait_freed(dve, ("conva", l, c, s))
                b0 = ROW["b_dw"][0]
                for tap in range(TAPS):
                    for c in range(2):
                        w = wdw[:, l, tap, c:c + 1]
                        src = yline[:, c, tap:tap + n_line]
                        if tap == 0:
                            step(dve_.tensor_scalar(acc[:, c, 0:n_line], src, w, vcol[:, l, b0 + c:b0 + c + 1], ALU.mult, ALU.add))
                            continue
                        settle(0 if tap == TAPS - 1 and c == 1 else 1)
                        ins = stt(out=acc[:, c, 0:n_line], in0=src, scalar=w, in1=acc[:, c, 0:n_line], op0=ALU.mult, op1=ALU.add)
                        if tap < TAPS - 1:
                            step(ins)
                        else:
                            ins.then_inc(acc_ready, 1)
                    if tap in (10, 18):
                        split(next(rest))
                for h in range(HEADS):
                    key = ("K", l, h, 0)
                    wait_products(dve, key)
                    dve.wait_ge(acc_ready, 2 * (l + 1))
                    if h:
                        dve.wait_ge(k_ready, HEADS * l + h)
                    step(dve_.stream_shuffle(krope[:], pt(key), SWAP))
                    step(tt(kT[:, h, 0:LAT], pt(key), rope_c[:], ALU.mult))
                    settle(1)
                    tt(krope[:], krope[:], rope_s[:], ALU.mult).then_inc(bank_free[bank_of(key)], 1)
                    wait_freed(dve, key)
                    settle()
                    tt(kT[:, h, 0:LAT], kT[:, h, 0:LAT], krope[:], ALU.add).then_inc(k_ready, 1)

                def biased_low(kind, name, chunk0, before):
                    for p in range(2):
                        for s, (o, n) in enumerate(ms):
                            key = (kind, l, p, s)
                            col = ROW[name][0] + p
                            dve.wait_ge(mix_hi_done, before + p * ns + s + 1)
                            stt(out=h_lo[:, chunk0 + p, o:o + n], in0=pt(key, n), scalar=vcol[:, l, col:col + 1],
                                in1=h_hi[:, chunk0 + p, o:o + n].bitcast(F), op0=ALU.add, op1=ALU.subtract)\
                                .then_inc(bank_free[bank_of(key)], 1)

                mbefore = 8 * sum(len(mix_segs(x)) for x in range(l))
                biased_low("Fo", "b_fourier", 6, mbefore)
                for s, (o, n) in enumerate(ms):
                    ao = 0 if s == 0 else C_CTX - HALF
                    key = ("mean", l, s)
                    wait_products(dve, key)
                    dve.wait_ge(acc_ready, 2 * (l + 1))
                    for c in range(2):
                        ins = stt(out=acc[:, c, ao:ao + n], in0=pt(key, n), scalar=-1.0 / CONVW, in1=acc[:, c, ao:ao + n],
                                  op0=ALU.mult, op1=ALU.add)
                        if c == 0:
                            step(ins)
                        else:
                            ins.then_inc(bank_free[bank_of(key)], 1)
                for s, (o, n) in enumerate(ms):
                    ao = 0 if s == 0 else C_CTX - HALF
                    wait_freed(dve, ("var", l, s))
                    step(dve_.reciprocal(crs[:, o:o + n], cst[:, o:o + n]))
                    settle()
                    for c in range(2):
                        tt(acc[:, c, ao:ao + n], acc[:, c, ao:ao + n], crs[:, o:o + n], ALU.mult).then_inc(cn_done, 1)
                biased_low("pw", "b_pw", 4, mbefore + 2 * ns)
                us = units_of(l)
                u_before = sum(len(units_of(x)) for x in range(l))
                wait_products(dve, ("pw", l, 1, ns - 1))
                for b in range(2):
                    step(dve_.memset(qpad[64:128, b, 0, :], 0.0))
                    step(dve_.memset(qpad[0:64, b, 1, :], 0.0))

                def rope_q(h):
                    for s in range(ns):
                        wait_freed(dve, ("Q", l, h, s))
                    if h >= 2:
                        last = max(i for i, u in enumerate(us) if u[0] == h - 2)
                        wait_products(dve, ("score", l, last))
                    settle()
                    if h:
                        dve.wait_ge(q_ready, HEADS * l + h)
                    step(dve_.stream_shuffle(qrope[:, 0, :], qT[:, h, 0:LAT], SWAP))
                    step(tt(qrope[:, 1, :], qT[:, h, 0:LAT], rope_c[:], ALU.mult))
                    settle(1)
                    step(tt(qrope[:, 0, :], qrope[:, 0, :], rope_s[:], ALU.mult))
                    for st in range(2):
                        r = slice(64 * st, 64 * st + 64)
                        if ns == 2:
                            step(dve_.tensor_copy(qpad[r, h % 2, st, LAT:TOK], qT[r, h, LAT:TOK]))
                    settle()
                    for st in range(2):
                        r = slice(64 * st, 64 * st + 64)
                        ins = tt(qpad[r, h % 2, st, 0:LAT], qrope[r, 0, :], qrope[r, 1, :], ALU.add)
                        if st == 0:
                            step(ins)
                        else:
                            ins.then_inc(q_ready, 1)

                def combine(i):
                    h, s, t = us[i]
                    dve.wait_ge(exp_done, 2 * (u_before + i + 1))
                    p, n = i % 2, TOK if s == 0 else CTX
                    if i >= 2:
                        dve.wait_ge(p_ready, u_before + i - 1)
                    step(dve_.reciprocal(rs[:, p, :], sums[:, p, :]))
                    settle()
                    step(tt(rs[:, p, 1:2], rs[:, p, 1:2], neglam[:, l:l + 1], ALU.mult))
                    settle()
                    step(dve_.tensor_scalar(e1[:, p, 0:n], e1[:, p, 0:n], rs[:, p, 1:2], None, ALU.mult))
                    settle()
                    pieces = ((0, LAT, CTX), (LAT, CTX, 0)) if s == 0 else ((0, CTX, 0),)
                    for k, (o, m, o1) in enumerate(pieces):
                        ins = stt(out=e0[:, i % 3, o:o + m], in0=e0[:, i % 3, o:o + m], scalar=rs[:, p, 0:1],
                                  in1=e1[:, p, o1:o1 + m], op0=ALU.mult, op1=ALU.add)
                        if k == len(pieces) - 1:
                            ins.then_inc(p_ready, 1)
                        else:
                            step(ins)

                rope_q(0)
                for i in range(len(us) + 1):
                    if i < len(us):
                        h, s, t = us[i]
                        wait_products(dve, ("score", l, i))
                        at0, n, p = 1536 * (i % 2), TOK if s == 0 else CTX, i % 2
                        if i >= 2:
                            dve.wait_ge(max_done, u_before + i - 1)
                        for st in range(2):
                            step(dve_.reduce_max(mx[:, p, st:st + 1], pflat[:, at0 + n * st:at0 + n * st + n], AX.X))
                        settle()
                        dve_.tensor_scalar(nb[:, p, :], mx[:, p, :], -(HD ** -0.5), None, ALU.mult).then_inc(max_done, 1)
                    if i >= 1:
                        combine(i - 1)
                    if i < len(us) and s == 0 and t == 1 and h < HEADS - 1:
                        rope_q(h + 1)
                    if i in (4, 6, 8):
                        split(next(rest))
                hbefore = HEADS * sum(len(mix_segs(x)) for x in range(l))
                for h in range(HEADS):
                    for s, (o, n) in enumerate(ms):
                        wait_freed(dve, ("hn", l, h, s))
                        step(dve_.reciprocal(hst[:, h, o:o + n], hst[:, h, o:o + n]))
                        settle()
                        stt(out=qT[:, h, o:o + n], in0=qT[:, h, o:o + n], scalar=gsub[:, l:l + 1], in1=hst[:, h, o:o + n],
                            op0=ALU.mult, op1=ALU.mult).then_inc(ht_done, 1)
                    if h:
                        head_low(l, h - 1, mbefore + 4 * ns)
                head_low(l, HEADS - 1, mbefore + 4 * ns)
                def add_out(j, s):
                    o, n = ms[s]
                    key = ("out", l, j, s)
                    wait_products(dve, key)
                    stt(out=xT[:, j, o:o + n], in0=pt(key, n), scalar=gate[:, l, 1, j, s:s + 1], in1=xT[:, j, o:o + n],
                        op0=ALU.mult, op1=ALU.add).then_inc(bank_free[bank_of(key)], 1)

                q = 3 * l + 2
                for v, s in out_order(l):
                    add_out(2 * v, s)
                    if ns == 2 and (v, s) == (2, 0):
                        over_rms(q, 1)
                        scaled(q, 1, (0, 1))
                    if ns == 2 and (v, s) == (3, 0):
                        scaled(q, 1, (5, 6, 7))
                    add_out(2 * v + 1, s)
                    if ns == 2 and (v, s) == (2, 0):
                        scaled(q, 1, (2, 3, 4))
                    if (v, s) == (0, ns - 1):
                        split(next(rest))
                    if (v, s) == (1, ns - 1):
                        split(("G", 2 * l + 1, 0))
                over_rms(q, 0)
                scaled(q, 0)

            def head_low(l, h, before):
                ms = mix_segs(l)
                for s, (o, n) in enumerate(ms):
                    dve.wait_ge(mix_hi_done, before + h * len(ms) + s + 1)
                    tt(h_lo[:, h, o:o + n], qT[:, h, o:o + n], h_hi[:, h, o:o + n].bitcast(F), ALU.subtract)\
                        .then_inc(mix_ready, 1)

            dve_.memset(cpad[:], 0.0).then_inc(pad_zeroed, 1)
            dve.wait_ge(const_landed, 16 * N_CONST)
            for l in range(DEPTH):
                for i in range(2):
                    settle()
                    step(tt(lamp[:], lamv[:, l, 2 * i, :], lamv[:, l, 2 * i + 1, :], ALU.mult))
                    settle()
                    ins = dve_.reduce_sum(lamw[:, 2 * l + i:2 * l + i + 1], lamp[:], AX.X)
                    if l == DEPTH - 1 and i == 1:
                        ins.then_inc(lam_dot, 1)
                    else:
                        step(ins)
            dve.wait_ge(lam_exp, 1)
            for l in range(DEPTH):
                step(tt(neglam[:, l:l + 1], lamw[:, 2 * l + 1:2 * l + 2], lamw[:, 2 * l:2 * l + 1], ALU.subtract))
                settle()
                step(dve_.tensor_scalar(neglam[:, l:l + 1], neglam[:, l:l + 1], -LAM_INIT[l], None, ALU.add))
                wait_freed(dve, ("vec", l))
                g0 = ROW["g_subln"][0]
                step(dve_.tensor_scalar(gsub[:, l:l + 1], vcol[:, l, g0:g0 + 1], 1.0 - LAM_INIT[l], None, ALU.mult))
            for s, (o, n) in enumerate(BOTH):
                for j in range(KD):
                    key = ("xin", s, j)
                    wait_products(dve, key)
                    dve_.tensor_copy(xT[:, j, o:o + n], pt(key, n)).then_inc(bank_free[bank_of(key)], 1)
            for i in range(4):
                wait_freed(dve, ("vec", i))
            dve.wait_ge(cpad_ready, 4)
            ada(BEFORE)
            split(("G", 0, 0))
            split(("U", 0, 0))
            shift_scale(0, 0)
            over_rms(0, 1)
            scaled(0, 1)
            over_rms(0, 0)
            ada(BETWEEN)
            gates(0, 0)
            scaled(0, 0)
            for l in range(DEPTH):
                if l:
                    gates(l, 0)
                ffn(2 * l)
                mix(l)
                ffn(2 * l + 1)


LAM_INIT = [0.8 - 0.6 * math.exp(-0.3 * l) for l in range(DEPTH)]
SWAP = [(i + 16) % 32 for i in range(32)]
SMALL = ("dft_cos", "dft_sin", "dft_cos_ctx", "dft_sin_ctx")
N_CONST = 4 + 6


def shape_tables():
    def dft(n, norm):
        i = np.arange(n)
        ang = 2.0 * np.pi * ((i[:, None] * i[None, :]) % n) / n
        return (np.cos(ang) * norm).astype(np.float32), (np.sin(ang) * norm).astype(np.float32)

    c, s = dft(LAT, LAT ** -0.5)
    cc, sc = dft(CTX, CTX ** -0.5)
    cd, sd = dft(64, 64 ** -0.5)
    both = np.zeros((128, 2, 128), np.float32)
    for g in range(2):
        both[64 * g:64 * g + 64, 0, 64 * g:64 * g + 64] = cd
        both[64 * g:64 * g + 64, 1, 64 * g:64 * g + 64] = -sd
    rot = HD // 2
    inv = (10000.0 ** (-np.arange(0, rot, 2, dtype=np.float32) / np.float32(rot))).astype(np.float32)
    t = np.arange(LAT)
    pos = np.stack([t // GRID_W, t % GRID_W]).astype(np.float32)
    rc, rsn = np.zeros((128, LAT), np.float32), np.zeros((128, LAT), np.float32)
    for p in range(128):
        d = p % HD
        ang = (pos[d // rot] * inv[d % (rot // 2)]).astype(np.float32)
        rc[p] = np.cos(ang)
        rsn[p] = np.sin(ang) * (-1.0 if d % rot < rot // 2 else 1.0)
    sel = np.zeros((128, 2), np.float32)
    for v in range(2):
        sel[v::32, v] = 1.0
    return {"dft_cos": c, "dft_sin": s, "dft_cos_ctx": cc, "dft_sin_ctx": sc, "dft_groups": both,
            "rope_cos": rc, "rope_sin": rsn, "ident": np.eye(128, dtype=np.float32), "sel": sel}


WEIGHTS = ("x", "ctx", "w_ada", "w_ffn1_gate", "w_ffn1_up", "w_ffn1_down", "w_ffn2_gate", "w_ffn2_up", "w_ffn2_down",
           "w_in", "w_pw", "w_fourier", "w_out")


def kernel(**inputs):
    import concourse.bacc as bacc
    from concourse.bass_utils import run_bass_kernel_spmd

    nc = bacc.Bacc("TRN2", target_bir_lowering=False, num_devices=1)
    arr = {k: np.ascontiguousarray(inputs[k]) for k in WEIGHTS}

    def stack(parts):
        return np.ascontiguousarray(np.concatenate([np.asarray(p).reshape(-1, 128) for p in parts], axis=0))

    for l in range(DEPTH):
        arr[f"vec{l}"] = stack([np.asarray(inputs[n])[l] for n in ROW])
    arr["vecw"] = stack([inputs["w_dw"]])
    arr["vecc"] = stack([inputs["c"], inputs["c_ctx"], inputs["g_final"]])
    arr["lams"] = np.ascontiguousarray(np.stack([np.asarray(inputs[n]) for n in ("lambda_q1", "lambda_k1", "lambda_q2", "lambda_k2")], axis=1)).reshape(1, -1)
    arr.update(shape_tables())
    a = {k: nc.dram_tensor(f"in_{k}", v.shape, mybir.dt.from_np(v.dtype), kind="ExternalInput").ap() for k, v in arr.items()}
    a["out"] = nc.dram_tensor("out_0", (1, LAT, D), mybir.dt.float32, kind="ExternalOutput").ap()
    trunk(nc, a)
    r = run_bass_kernel_spmd(nc, [{f"in_{k}": v for k, v in arr.items()}], core_ids=[0])
    return r.results[0]["out_0"]
```

```python
import math
from contextlib import ExitStack

import numpy as np

import concourse.bass as bass
from concourse import mybir

DEPTH = 2
D = 1024
LAT, CTX = 512, 256
TOK = LAT + CTX
KD = D // 128
FF = 2816
GW = 256
NG = FF // GW
HEADS = 4
HD = 64
QKW = 512
CONVW = 256
TAPS = 31
HALF = TAPS // 2
INW = 2304
EPS = 1e-6
GRID_W = 64
RING = 3
TILE = 2048
LINE = HALF + LAT + HALF + CTX + HALF
BOTH = ((0, LAT), (LAT, CTX))
ONLY_LAT = ((0, LAT),)
C_LAT = HALF
C_CTX = HALF + LAT + HALF

ROW = {}
_at = 0
for _name, _n in (("b_ada", 72), ("g_ffn1", 8), ("g_mix", 8), ("g_ffn2", 8), ("g_subln", 1), ("b_dw", 2),
                  ("g_conv_ln", 2), ("b_conv_ln", 2), ("b_pw", 2), ("b_fourier", 2)):
    ROW[_name] = (_at, _n)
    _at += _n
NROW = _at
NADA = 9 * D // 512
FIRST_BLOCKS = (0, 1, 2, 3, 4, 5, NADA - 1)
BEFORE, BETWEEN = FIRST_BLOCKS[:4], FIRST_BLOCKS[4:]
SIDE_GROUPS = ({g: (0, 6 + g) for g in range(NG)}, {g: (1, g - 1) for g in range(1, NG)},
               {g: (1, NG - 2 + g) for g in range(1, NADA - (NG - 1) + 1)}, {})
SIDE_AT = 5


def segs_of(norm):
    return ONLY_LAT if norm >= 5 else BOTH


PIECES = ((0, LAT, 0), (LAT, CTX, 1), (0, LAT // 2, 0), (LAT // 2, LAT // 2, 0))


def seg_order(q):
    return (1, 0) if len(segs_of(q)) == 2 else (3, 2)


def last_slots(f):
    return seg_order((0, 2, 3, 5)[f])


def square_order(q):
    first, second = seg_order(q)
    if q % 3 == 2:
        return [(s, j) for j in range(4) for s in (second, first)] + [(s, j) for s in (first, second) for j in range(4, KD)]
    return [(s, j) for s in seg_order(q) for j in range(KD)]


def out_order(l):
    first, second = seg_order(3 * l + 2)
    return [(v, s) for v in range(2) for s in range(len(mix_segs(l)))] + [(2, first), (3, first), (2, second), (3, second)]


def mix_segs(l):
    return BOTH if l < DEPTH - 1 else ONLY_LAT


def units_of(l):
    return [(h, s, t) for h in range(HEADS) for s in range(len(mix_segs(l))) for t in range(mix_segs(l)[s][1] // 128)]


def head_end(l, h):
    return len(units_of(l)) // HEADS * (h + 1) + 2


def steps_of(l):
    return head_end(l, HEADS - 1) + 5


CONV_MEAN, CONV_VAR, CONV_PW = 1, 5, 10


def extras(l, i):
    ns = len(mix_segs(l))
    out = [("mean", l, s) for s in range(ns) if i == CONV_MEAN + s]
    out += [("var", l, s) for s in range(ns) if i == CONV_VAR + s]
    out += [("pw", l, p, s) for p in range(2) for s in range(ns) if i == CONV_PW + ns * p + s]
    out += [("hn", l, h, s) for h in range(HEADS) for s in range(ns) if i == head_end(l, h) + 1 + s]
    return out


OUT_ORDER = (2, 3, 0, 1)


class Plan:

    def __init__(self):
        self.n = 0
        self.bank = 0
        self.uses = [0] * 8
        self.slots = {}
        self.tiles = []
        self.raw = {}
        self.split = {}
        self.lastuse = {}
        self.before_att = []
        self.nsplit = 0
        self.build()

    def slot(self, key, bank=None):
        if bank is None:
            bank = self.bank
            self.bank = (bank + 1) % 8
        self.slots[key] = (self.n, bank, self.uses[bank])
        self.n += 1
        self.uses[bank] += 1

    def tile(self, key, split=True):
        self.raw[key] = len(self.tiles)
        self.tiles.append(key)
        if split:
            self.split[key] = self.nsplit
            self.nsplit += 1

    def used(self, key, slot):
        self.lastuse[key] = slot

    def ada(self, blocks):
        def bank(i):
            return (self.bank + i) % 8 if blocks is BETWEEN else None

        for n, b in enumerate(blocks):
            if b == 3:
                self.tile(("G", 0, 0))
                for s in seg_order(0):
                    self.slot(("stat", 0, s))
            self.slot(("ada", 0, b), bank(n % 2))
            if n:
                self.slot(("adaT", 0, blocks[n - 1]), bank(2 + (n - 1) % 2))
            self.tile(("ada", 0, b, 0), split=False)
            self.tile(("ada", 0, b, 1), split=False)
            self.used(("ada", 0, b, 0), ("ada", 0, b))
            self.used(("ada", 0, b, 1), ("ada", 0, b))
        self.slot(("adaT", 0, blocks[-1]), bank(2 + (len(blocks) - 1) % 2))

    def side(self, f, g):
        if g in SIDE_GROUPS[f]:
            self.slot(("side", f, g), (self.bank + 4) % 8)

    def ffn(self, f):
        ns = len(segs_of((0, 2, 3, 5)[f]))
        after = (1, 3, 4, 6)[f]

        def gate_up(g):
            first, second = last_slots(f)
            if g == 0:
                slots = [(w, f, g, c, s) for s in (first, second) for c in range(2) for w in "gu"]
            else:
                slots = [(w, f, g, c, s) for c in range(2) for w in "gu" for s in range(ns)]
            for key in slots:
                self.slot(key)
                if f == 0 and key == ("u", 0, 0, 1, 1):
                    self.ada(BETWEEN)
            self.used(("G", f, g), ("g", f, g, 1, second if g == 0 else ns - 1))
            self.used(("U", f, g), ("u", f, g, 1, second if g == 0 else ns - 1))

        def down(g):
            for j in range(KD):
                for s in range(ns):
                    self.slot(("d", f, g, j, s))
                if j == SIDE_AT:
                    self.side(f, g + 1)
            self.used(("D", f, g), ("d", f, g, KD - 1, ns - 1))

        if f:
            self.tile(("G", f, 0))
        self.tile(("U", f, 0))
        gate_up(0)
        self.side(f, 0)
        for g in range(1, NG):
            self.tile(("G", f, g))
            self.tile(("U", f, g))
            self.tile(("D", f, g - 1))
            gate_up(g)
            down(g - 1)
        self.tile(("D", f, NG - 1))
        first, second = last_slots(f)
        for s in (first, second):
            for j in range(KD):
                self.slot(("d", f, NG - 1, j, s))
                if s == second and j == 3:
                    self.slot(("stat", after, seg_order(after)[0]))
        self.used(("D", f, NG - 1), ("d", f, NG - 1, KD - 1, second))
        self.slot(("stat", after, seg_order(after)[1]))

    def mix(self, l):
        ms = mix_segs(l)
        for v in range(2):
            self.tile(("V", l, v))
        for ts in ((4, 5), (0, 1, 2, 3)):
            for v in range(2):
                for t in ts:
                    self.slot(("V", l, v, t))
        for v in range(2):
            self.used(("V", l, v), ("V", l, v, 3))
        for c in range(2):
            self.tile(("conv", l, c))
            for w in "ga":
                for s in range(len(ms)):
                    self.slot(("conv" + w, l, c, s))
            self.used(("conv", l, c), ("conva", l, c, len(ms) - 1))
        self.tile(("four", l))
        nt = sum(n for _, n in ms) // 128
        for t in range(nt):
            self.slot(("X", l, t))
        self.used(("four", l), ("X", l, nt - 1))
        for w, ss in (("Q", ms), ("K", BOTH)):
            for v in range(2):
                self.tile((w, l, v))
                for c in range(2):
                    for s in range(len(ss)):
                        self.slot((w, l, 2 * v + c, s))
                self.used((w, l, v), (w, l, 2 * v + 1, len(ss) - 1))
        for k in ("C", "S", "W"):
            self.tile((k, l), split=False)
        for j in range(2):
            for w in "CS":
                for s in range(len(ms)):
                    self.slot(("Z", l, j, w, s))
        self.used(("C", l), ("Z", l, 1, "S", len(ms) - 1))
        self.used(("S", l), ("Z", l, 1, "S", len(ms) - 1))
        for j in range(2):
            for s in range(len(ms)):
                self.slot(("F", l, j, s))
        for o in range(2):
            for s in range(len(ms)):
                self.slot(("Fo", l, o, s))
        u = units_of(l)
        self.before_att.append(list(self.uses))
        for i in range(steps_of(l)):
            if i < len(u):
                self.slots[("score", l, i)] = (self.n, None, None)
                self.n += 1
            if 0 <= i - 2 < len(u):
                self.slot(("T", l, i - 2, 0), 6)
            if 0 <= i - 3 < len(u):
                h, s, t = u[i - 3]
                if t == 0:
                    self.slots[("O", l, h, s)] = (None, 7, self.uses[7])
                    self.uses[7] += 1
                if t == ms[s][1] // 128 - 1:
                    self.slots[("O", l, h, s)] = (self.n,) + self.slots[("O", l, h, s)][1:]
                    self.n += 1
            if 0 <= i - 2 < len(u) and u[i - 2][1] == 0:
                self.slot(("T", l, i - 2, 1), 6)
            for key in extras(l, i):
                self.slot(key, 6)
        self.used(("W", l), ("pw", l, 1, len(ms) - 1))
        self.bank = 0
        for v in range(4):
            self.tile(("out", l, v))
        for v, s in out_order(l):
            for c in range(2):
                self.slot(("out", l, 2 * v + c, s))
                if (v, c, s) == (2, 0, seg_order(3 * l + 2)[1]):
                    self.slot(("stat", 3 * l + 2, seg_order(3 * l + 2)[0]))
            self.used(("out", l, v), ("out", l, 2 * v + 1, s))
        self.slot(("stat", 3 * l + 2, seg_order(3 * l + 2)[1]))

    def build(self):
        for s in (1, 0):
            for j in range(KD):
                self.slot(("xin", s, j))
            for i in range(4 if s else 0):
                self.slot(("vec", i))
        self.ada(BEFORE)
        for l in range(DEPTH):
            self.ffn(2 * l)
            self.mix(l)
            self.ffn(2 * l + 1)
        for t in OUT_ORDER:
            for half in range(2):
                self.slot(("xout", t, half))


POOL_SPLITS = {1: (("V", 0, 0), ("V", 0, 1)), 2: (("U", 1, 0),), 3: (("G", 2, 0), ("U", 2, 0)),
               4: (("V", 1, 0), ("V", 1, 1)), 5: (("U", 3, 0),)}
POOL_TILES = [key for keys in POOL_SPLITS.values() for key in keys] + [("out", l, v) for l in range(DEPTH) for v in range(3)]


def trunk(nc, a):
    F, R = mybir.dt.float32, mybir.dt.float32r
    ALU, ACT, AX = mybir.AluOpType, mybir.ActivationFunctionType, mybir.AxisListType
    plan = Plan()
    ctx = ExitStack()
    with ctx:
        used = [0]
        used[0] = (nc.sbuf_base + 31) // 32 * 32

        def at(name, shape, dt, offset):
            return nc.alloc_sbuf_tensor_at(name, shape, dt, offset=offset, align_bytes=4)

        def sb(name, shape, dt=F):
            t = at(name, shape, dt, used[0])
            used[0] += 4 * math.prod(shape[1:])
            return t

        xT = sb("xT", [128, KD, TOK])
        h_at = used[0]
        h_hi = sb("h_hi", [128, KD, TOK], R)
        h_lo_at = used[0]
        h_lo = sb("h_lo", [128, KD, TOK], R)
        raw = [sb(f"raw{i}", [128, TILE]) for i in range(RING)]
        w_hi = [sb(f"w_hi{i}", [128, TILE], R) for i in range(RING)]
        w_lo = [sb(f"w_lo{i}", [128, TILE], R) for i in range(RING)]
        ones = sb("ones", [128, 128])
        ident = sb("ident", [128, 128])
        rope_c = sb("rope_c", [128, LAT])
        rope_s = sb("rope_s", [128, LAT])
        dft = sb("dft", [128, 2, 128])
        vcol = sb("vcol", [128, DEPTH, NROW])
        wdw = sb("wdw", [128, DEPTH, TAPS, 2])
        ccol = sb("ccol", [128, 3, KD])
        mod = sb("mod", [128, DEPTH, 72, 2])
        amul = sb("amul", [128, DEPTH, 3, KD, 2])
        gate = sb("gate", [128, DEPTH, 3, KD, 2])
        gsub = sb("gsub", [128, DEPTH])
        epsc = sb("epsc", [128, 1])
        neglam = sb("neglam", [128, DEPTH])
        nb = sb("nb", [128, 2, 2])
        sums = sb("sums", [128, 2, 2])
        rs = sb("rs", [128, 2, 2])
        M = (used[0] + 31) // 32 * 32
        S3 = 4 * TOK
        hid_hi = at("hid_hi", [128, 2, 2, TOK], R, M)
        hid_lo = at("hid_lo", [128, 2, 2, TOK], R, M + 4 * S3)
        sil = at("sil", [128, 2, TOK], F, M + 8 * S3)
        prod = at("prod", [128, 2, TOK], F, M + 10 * S3)
        sq = at("sq", [128, 2, TOK], F, M + 12 * S3)
        std = at("std", [128, TOK], F, M + 2 * S3)
        rstd = at("rstd", [128, TOK], F, M + 3 * S3)
        tn = at("tn", [128, 2, TOK], F, M + 6 * S3)
        sqsum = at("sqsum", [128, TOK], F, M + 8 * S3)
        cpad = at("cpad", [128, KD, 32], F, M + 9 * S3)
        side_raw = [at(f"side_raw{i}", [128, 2, 512], F, M + 14 * S3 + 4096 * i) for i in range(2)]
        side_acc = at("side_acc", [128, 2, 512], F, M + 14 * S3 + 8192)
        side_col = at("side_col", [128, 8, 32], F, M + 12 * S3)
        sel = at("sel", [128, 2], F, M + 9 * S3 + 1024)
        lamw = at("lamw", [128, 4], F, M + 9 * S3 + 1024 + 8)
        xnat = at("xnat", [128, TOK // 128, D], F, M)
        vstage = at("vstage", [128, 4, 128], F, M + 10 * S3)
        lamv = at("lamv", [128, DEPTH, 4, HD], F, M + 10 * S3 + 2048)
        lamp = at("lamp", [128, HD], F, M + 10 * S3 + 2048 + 2048)
        part = at("part", [128, 2, 512], F, M + 10 * S3)
        kT = at("kT", [128, HEADS, TOK], F, M)
        qT = at("qT", [128, HEADS, TOK], F, M + 4 * S3)
        vN = at("vN", [128, TOK // 128, QKW], F, M + 8 * S3)
        xN = at("xN", [128, TOK // 128, CONVW], F, M + 12 * S3)
        yline = at("yline", [128, 2, LINE], F, M + 14 * S3)
        acc_at = M + 14 * S3 + 4 * 2 * LINE
        acc = at("acc", [128, 2, LINE - 2 * HALF], F, (acc_at + 31) // 32 * 32)
        e0 = at("e0", [128, 3, TOK], F, M + 12 * S3)
        zT = at("zT", [128, 2, 2, TOK], F, h_lo_at)
        fT = at("fT", [128, 2, TOK], F, M + 12 * S3)
        csq = at("csq", [128, 2, TOK], F, h_at + 4 * S3)
        cst = at("cst", [128, TOK], F, h_at + 4 * S3)
        crs = at("crs", [128, TOK], F, h_at + 5 * S3)
        krope = at("krope", [128, LAT], F, M + 14 * S3)
        pT = at("pT", [128, 2, TOK // 128, 128], F, h_lo_at)
        e1 = at("e1", [128, 2, TOK], F, h_lo_at + 2 * S3)
        qpad = at("qpad", [128, 2, 2, TOK], F, h_at)
        hsq = at("hsq", [128, HEADS, TOK], F, M)
        onat = at("onat", [128, 2, D], F, M + 14 * S3)

        ps = ctx.enter_context(nc.psum_tensor("ps", [128, 8, 512], F))
        pflat = ps[:].rearrange("p b n -> p (b n)")

        def sem(name):
            return ctx.enter_context(nc.semaphore(name))

        products = sem("products")
        bank_free = [sem(f"bank_free{b}") for b in range(8)]
        raw_landed = [sem(f"raw_landed{i}") for i in range(RING)]
        w_hi_done = sem("w_hi_done")
        w_split = sem("w_split")
        const_landed = sem("const_landed")
        ident_landed = sem("ident_landed")
        tables_landed = sem("tables_landed")
        x_landed = sem("x_landed")
        ctx_landed = sem("ctx_landed")
        out_landed = [sem(f"out_landed{i}") for i in range(2)]
        out_ready = sem("out_ready")
        pool_const = sem("pool_const")
        act_step = sem("act_step")
        dve_step = sem("dve_step")
        cpad_ready = sem("cpad_ready")
        side_landed = [sem(f"side_landed{i}") for i in range(2)]
        side_summed = sem("side_summed")
        side_done = sem("side_done")
        sq_done = sem("sq_done")
        squares_added = sem("squares_added")
        ada_half = sem("ada_half")
        t_done = sem("t_done")
        h_hi_done = sem("h_hi_done")
        h_ready = sem("h_ready")
        hid_hi_done = sem("hid_hi_done")
        hid_ready = sem("hid_ready")
        line_ready = sem("line_ready")
        k_ready = sem("k_ready")
        acc_ready = sem("acc_ready")
        csq_done = sem("csq_done")
        cn_done = sem("cn_done")
        cs_done = sem("cs_done")
        q_ready = sem("q_ready")
        conv_root = sem("conv_root")
        conv_scale = sem("conv_scale")
        head_root = sem("head_root")
        max_done = sem("max_done")
        exp_done = sem("exp_done")
        p_ready = sem("p_ready")
        mix_hi_done = sem("mix_hi_done")
        mix_ready = sem("mix_ready")
        hsq_done = sem("hsq_done")
        ht_done = sem("ht_done")
        y_done = sem("y_done")
        lam_dot = sem("lam_dot")
        lam_exp = sem("lam_exp")
        pad_zeroed = sem("pad_zeroed")
        block = ctx.enter_context(nc.Block())

        def lin(value, key, g, it):
            v = value(key(g))
            if it is None:
                return v
            step = value(key(g + 2)) - v
            return it * step + v

        def number(key):
            return plan.slots[key][0] + 1

        def freed(key):
            return plan.slots[key][2] + 1

        def wait_products(eng, key, g=None, it=None):
            eng.wait_ge(products, number(key) if g is None else lin(number, key, g, it))

        def wait_bank(pe, key, g=None, it=None):
            k0 = key if g is None else key(g)
            use = plan.slots[k0][2]
            if use or it is not None:
                pe.wait_ge(bank_free[plan.slots[k0][1]], use if g is None else lin(lambda k: plan.slots[k][2], key, g, it))

        def wait_freed(eng, key, g=None, it=None):
            k0 = key if g is None else key(g)
            eng.wait_ge(bank_free[plan.slots[k0][1]], freed(key) if g is None else lin(freed, key, g, it))

        def bank_of(key):
            return plan.slots[key][1]

        def pt(key, n=512):
            return ps[:, plan.slots[key][1], 0:n]

        def raw_of(key):
            return raw[plan.raw[key] % RING]

        arrived, total = {}, [0] * RING
        for key in plan.tiles:
            total[plan.raw[key] % RING] += 16 * {"conv": 2, "W": 4}.get(key[0], 1)
            arrived[key] = total[plan.raw[key] % RING]

        def wait_landed(eng, key, g=None, it=None):
            k0 = key if g is None else key(g)
            eng.wait_ge(raw_landed[plan.raw[k0] % RING],
                        arrived[key] if g is None else lin(arrived.__getitem__, key, g, it))

        def ring(key):
            return plan.split[key] % RING

        split_keys = [k for k in plan.tiles if k in plan.split]

        def hcount(q, j, s):
            return 16 * q + 8 * seg_order(q).index(s) + j + 1

        def sqcount(q, s, j):
            return 16 * q + square_order(q).index((s, j)) + 1

        def addcount(q, s, j):
            o = square_order(q)
            return 14 * q + sum(1 for x in o[:o.index((s, j)) + 1] if x[1])

        NORM_OF = (0, 2, 3, 5)
        side_list = [(f, g) for f in range(2 * DEPTH) for g in SIDE_GROUPS[f]]

        def side_number(key):
            return side_list.index(key)

        consts = []

        def load_sizes(key):
            dst = raw_of(key)
            k = key[0]
            if k == "ada":
                _, l, b, half = key
                return [(a["w_ada"][l, 512 * half:512 * half + 512, 512 * b:512 * b + 512]
                         .rearrange("(k p) n -> p k n", p=128), dst[:].rearrange("p (k n) -> p k n", k=4))]
            if k in ("C", "S"):
                src = a["dft_cos"] if k == "C" else a["dft_sin"]
                return [(src.rearrange("(k p) n -> p k n", p=128), dst[:].rearrange("p (k n) -> p k n", k=4))]
            l = key[1]
            if k == "W":
                out = []
                for i, src in enumerate((a["w_pw"][l, :, :], a["w_fourier"][l, :, :], a["dft_cos_ctx"], a["dft_sin_ctx"])):
                    out.append((src.rearrange("(k p) n -> p k n", p=128),
                                dst[:, 512 * i:512 * i + 512].rearrange("p (k n) -> p k n", k=2)))
                return out
            d8 = dst[:].rearrange("p (k n) -> p k n", k=KD)
            if k == "conv":
                c = key[2]
                out = []
                for i, at_ in enumerate((1536 + 128 * c, 1536 + 256 + 128 * c)):
                    out.append((a["w_in"][l, :, at_:at_ + 128].rearrange("(k p) n -> p k n", p=128),
                                d8[:, :, 128 * i:128 * i + 128]))
                return out
            if k == "out":
                at_, src = 256 * key[2], a["w_out"]
            else:
                at_ = {"four": 2048, "V": 1024, "K": 512, "Q": 0}[k] + (256 * key[2] if k != "four" else 0)
                src = a["w_in"]
            return [(src[l, :, at_:at_ + 256].rearrange("(k p) n -> p k n", p=128), d8)]

        def ffn_source(f, k, col):
            l, which = f // 2, f % 2 + 1
            if k == "D":
                return a[f"w_ffn{which}_down"][l, bass.ds(col, GW), :].rearrange("(c p) n -> p c n", p=128)
            name = f"w_ffn{which}_{'gate' if k == 'G' else 'up'}"
            return a[name][l, :, bass.ds(col, GW)].rearrange("(k p) n -> p k n", p=128)

        @block.sync
        def _(sp):
            def load_tokens(t, landed):
                src = a["x"][0, 128 * t:128 * t + 128, :] if t < 4 else a["ctx"][0, 128 * (t - 4):128 * (t - 4) + 128, :]
                sp.dma_start(xnat[:, t, :], src).then_inc(landed, 16)

            sp.dma_start(ident[:], a["ident"]).then_inc(ident_landed, 16)
            for t in (4, 5):
                load_tokens(t, ctx_landed)
            for src, dst in ((a["vec0"], vstage[0:NROW, 0, :]), (a["vec1"], vstage[0:NROW, 1, :]),
                             (a["vecw"], vstage[0:4 * TAPS, 2, :]), (a["vecc"], vstage[0:3 * KD, 3, :]), (a["sel"], sel[:]),
                             (a["lams"].broadcast_to((128, DEPTH * 4 * HD)), lamv[:].rearrange("p l i n -> p (l i n)"))):
                sp.dma_start(dst, src).then_inc(const_landed, 16)
            for t in range(4):
                load_tokens(t, x_landed)

            def release(key):
                t = plan.raw[key] - RING
                if t < 0:
                    return
                old = plan.tiles[t]
                if old in plan.split:
                    sp.wait_ge(w_split, plan.split[old] + 1)
                elif old[0] == "ada" and old[3] == 0:
                    sp.wait_ge(ada_half, FIRST_BLOCKS.index(old[2]) + 1)
                else:
                    wait_products(sp, plan.lastuse[old])

            def load(key):
                release(key)
                if key[0] in "GUD":
                    pairs = [(ffn_source(key[1], key[0], GW * key[2]), ffn_dst(key))]
                else:
                    pairs = load_sizes(key)
                for i, (src, dst) in enumerate(pairs):
                    sp.dma_start(dst, src).then_inc(raw_landed[plan.raw[key] % RING], 16)

            def ffn_dst(key):
                return raw_of(key)[:].rearrange("p (k n) -> p k n", k=2 if key[0] == "D" else KD)

            def in_loop(f, k, g, it):
                key = (k, f, g)
                old, later = plan.tiles[plan.raw[key] - RING], plan.tiles[plan.raw[(k, f, g + 2)] - RING]
                was, step = plan.split[old] + 1, plan.split[later] - plan.split[old]
                sp.wait_ge(w_split, it * step + was)
                sp.dma_start(ffn_dst(key), ffn_source(f, k, it * (2 * GW) + GW * g))\
                    .then_inc(raw_landed[plan.raw[key] % RING], 16)

            def side(f, g, quarters, it=None):
                if g not in SIDE_GROUPS[f]:
                    return
                l, b = SIDE_GROUPS[f][g]
                n = side_number((f, g))
                for q in quarters:
                    done = 16 * n + 4 * (q - 1)
                    if it is None:
                        if done > 0:
                            sp.wait_ge(side_summed, done)
                        src = a["w_ada"][l, 256 * q:256 * q + 256, 512 * b:512 * b + 512]
                    else:
                        sp.wait_ge(side_summed, it * 32 + done)
                        src = a["w_ada"][l, 256 * q:256 * q + 256, bass.ds(it * 1024 + 512 * b, 512)]
                    sp.dma_start(side_raw[q % 2][:], src.rearrange("(k p) n -> p k n", p=128)).then_inc(side_landed[q % 2], 16)

            order = list(plan.tiles)
            i = 0
            while i < len(order):
                key = order[i]
                if key[0] == "G" and key[2] == 3:
                    f = key[1]
                    with sp.Fori(0, 3) as it:
                        for g in (3, 4):
                            in_loop(f, "G", g, it)
                            in_loop(f, "U", g, it)
                            in_loop(f, "D", g - 1, it)
                            side(f, g - 1, (2, 3), it)
                            side(f, g, (0, 1), it)
                    i += 18
                    continue
                load(key)
                i += 1
                if key == ("U", 0, 0):
                    for dst, name in ((rope_c[:], "rope_cos"), (rope_s[:], "rope_sin"), (dft[:], "dft_groups")):
                        sp.dma_start(dst, a[name]).then_inc(tables_landed, 16)
                if key[0] == "U" and key[2] == 0:
                    f = key[1]
                    if f == 1:
                        wait_products(sp, ("O", 0, HEADS - 1, len(mix_segs(0)) - 1))
                    side(f, 0, (0, 1))
                if key[0] == "D":
                    f, g = key[1], key[2]
                    side(f, g, (2, 3))
                    side(f, g + 1, (0, 1))
            for i, t in enumerate(OUT_ORDER):
                wait_freed(sp, ("xout", t, 1))
                sp.dma_start(a["out"][0, 128 * t:128 * t + 128, :], onat[:, i % 2, :]).then_inc(out_landed[i % 2], 16)
            for i in range(2):
                sp.wait_ge(out_landed[i], 16 * (LAT // 128 // 2))

        @block.gpsimd
        def _(pool):
            nc.gpsimd.memset(ones[:], 1.0).then_inc(pool_const, 1)
            nc.gpsimd.memset(epsc[:], EPS).then_inc(pool_const, 1)

            def split(key):
                n = plan.split[key]
                pool.wait_ge(w_hi_done, n + 1)
                pool.wait_ge(w_split, n)
                nc.gpsimd.tensor_tensor(w_lo[n % RING][:], raw_of(key)[:], w_hi[n % RING][:].bitcast(F), ALU.subtract)\
                    .then_inc(w_split, 1)

            def attention_help(l):
                ms = mix_segs(l)
                ns = len(ms)
                split(("out", l, 0))
                split(("out", l, 1))
                for s, (o, n) in enumerate(ms):
                    ao = 0 if s == 0 else C_CTX - HALF
                    pool.wait_ge(conv_scale, sum(len(mix_segs(x)) for x in range(l)) + s + 1)
                    for c in range(2):
                        nc.gpsimd.tensor_tensor(acc[:, c, ao:ao + n], acc[:, c, ao:ao + n], crs[:, o:o + n], ALU.mult)\
                            .then_inc(cn_done, 1)
                split(("out", l, 2))
                wait_products(pool, ("O", l, HEADS - 1, ns - 1))
                before = 8 * sum(len(mix_segs(x)) for x in range(l)) + 4 * ns
                for h in range(HEADS):
                    for s, (o, n) in enumerate(ms):
                        pool.wait_ge(mix_hi_done, before + h * ns + s + 1)
                        nc.gpsimd.tensor_tensor(h_lo[:, h, o:o + n], qT[:, h, o:o + n], h_hi[:, h, o:o + n].bitcast(F),
                                                ALU.subtract).then_inc(mix_ready, 1)

            for q in range(3 * DEPTH + 1):
                if q % 3 == 2:
                    attention_help(q // 3)
                for key in POOL_SPLITS.get(q, ()):
                    if q % 3 != 2:
                        split(key)
                for s, j in square_order(q):
                    if q % 3 == 2 and (s, j) == (seg_order(q)[1], 6):
                        for key in POOL_SPLITS[q]:
                            split(key)
                    if j == 0:
                        continue
                    o, n = PIECES[s][:2]
                    pool.wait_ge(sq_done, sqcount(q, s, j))
                    if j > 1:
                        pool.wait_ge(squares_added, addcount(q, s, j - 1))
                    nc.gpsimd.tensor_tensor(sqsum[:, o:o + n], sqsum[:, o:o + n], sq[:, j % 2, o:o + n], ALU.add)\
                        .then_inc(squares_added, 1)

        mm = nc.tensor.matmul

        def mm3(out, wh, wl, xh, xl, start, stop):
            mm(out, wh, xh, start=start, stop=False)
            mm(out, wh, xl, start=False, stop=False)
            return mm(out, wl, xh, start=False, stop=stop)

        def wk(key, k):
            i = ring(key)
            return (w_hi[i][:].rearrange("p (k n) -> p k n", k=k), w_lo[i][:].rearrange("p (k n) -> p k n", k=k))

        @block.tensor
        def _(pe):
            def wait_h(q, j, s):
                pe.wait_ge(h_ready, hcount(q, j, s))

            def wait_split(key, g=None, it=None):
                pe.wait_ge(w_split, (plan.split[key] + 1) if g is None else lin(lambda k: plan.split[k] + 1, key, g, it))

            def stat(q, s):
                o, n = PIECES[s][:2]
                wait_bank(pe, ("stat", q, s))
                pe.wait_ge(squares_added, addcount(q, s, KD - 1))
                mm(pt(("stat", q, s), n), ones[:], sqsum[:, o:o + n], start=True, stop=True).then_inc(products, 1)

            def ada(blocks):
                pe.wait_ge(cpad_ready, 4)
                for n, b in enumerate(blocks):
                    if b == 3:
                        for s in seg_order(0):
                            stat(0, s)
                    key = ("ada", 0, b)
                    wait_bank(pe, key)
                    for k in range(KD):
                        if k % 4 == 0:
                            wait_landed(pe, key + (k // 4,))
                        q = k % 4
                        src = raw_of(key + (k // 4,))[:].rearrange("p (k n) -> p k n", k=4)
                        last = mm(ps[32 * q:32 * q + 32, bank_of(key), :], cpad[:, k, :], src[:, q, :],
                                  start=(k < 4), stop=(k >= 4), skip_group_check=True)
                        if k == 3:
                            last.then_inc(ada_half, 1)
                    last.then_inc(products, 1)
                    if n:
                        turn(blocks[n - 1])
                turn(blocks[-1])

            def turn(b):
                wait_freed(pe, ("ada", 0, b))
                key = ("adaT", 0, b)
                wait_bank(pe, key)
                for i in range(4):
                    last = mm(ps[:, bank_of(key), 2 * i:2 * i + 2],
                              part[:, FIRST_BLOCKS.index(b) % 2, 128 * i:128 * i + 128], sel[:],
                              start=True, stop=True, skip_group_check=True)
                last.then_inc(products, 1)

            def ffn(f):
                q = NORM_OF[f]
                ss = segs_of(q)

                def gate_up(g, it=None):
                    for c in range(2):
                        for w in "gu":
                            if c == 0:
                                wait_split(lambda x: (w.upper(), f, x), g, it)
                            for s in range(len(ss)):
                                wait_bank(pe, lambda x: (w, f, x, c, s), g, it)
                            wh, wl = wk((w.upper(), f, g), KD)
                            for k in range(KD):
                                for s, (o, n) in enumerate(ss):
                                    last = mm3(pt((w, f, g, c, s), n), wh[:, k, 128 * c:128 * c + 128],
                                               wl[:, k, 128 * c:128 * c + 128], h_hi[:, k, o:o + n], h_lo[:, k, o:o + n],
                                               k == 0, k == KD - 1)
                                    if k == KD - 1:
                                        last.then_inc(products, 1)

                def gate_up_first():
                    wait_split(("U", f, 0))
                    first, second = seg_order(q)
                    for s in (first, second):
                        o, n = PIECES[s][:2]
                        for cs_ in ((0, 1),) if s == first else ((0,), (1,)):
                            for c in cs_:
                                for w in "gu":
                                    wait_bank(pe, (w, f, 0, c, s))
                            for k in range(KD):
                                if k == 2 and s == first and q:
                                    stat(q, second)
                                wait_h(q, k, s)
                                for c in cs_:
                                    for w in "gu":
                                        wh, wl = wk((w.upper(), f, 0), KD)
                                        last = mm3(pt((w, f, 0, c, s), n), wh[:, k, 128 * c:128 * c + 128],
                                                   wl[:, k, 128 * c:128 * c + 128], h_hi[:, k, o:o + n],
                                                   h_lo[:, k, o:o + n], k == 0, k == KD - 1)
                                        if k == KD - 1:
                                            last.then_inc(products, 1)
                        if f == 0 and s == 1:
                            ada(BETWEEN)

                def down(g, it=None):
                    wait_split(lambda x: ("D", f, x), g, it)
                    n0 = 2 * NG * f + 2 * g + 2
                    pe.wait_ge(hid_ready, n0 if it is None else it * 4 + n0)
                    wh, wl = wk(("D", f, g), 2)
                    for j in range(KD):
                        for s, (o, n) in enumerate(ss):
                            wait_bank(pe, lambda x: ("d", f, x, j, s), g, it)
                            for c in range(2):
                                last = mm3(pt(("d", f, g, j, s), n), wh[:, c, 128 * j:128 * j + 128],
                                           wl[:, c, 128 * j:128 * j + 128], hid_hi[:, g % 2, c, o:o + n],
                                           hid_lo[:, g % 2, c, o:o + n], c == 0, c == 1)
                            last.then_inc(products, 1)
                        if j == SIDE_AT:
                            side(g + 1, it)

                def side(g, it=None):
                    if g not in SIDE_GROUPS[f]:
                        return
                    key = lambda x: ("side", f, x)
                    n16 = 16 * (side_number((f, g)) + 1)
                    pe.wait_ge(side_summed, n16 if it is None else it * 32 + n16)
                    wait_bank(pe, key, g, it)
                    rows = side_acc[:].rearrange("p v (j q n) -> p q (v j) n", q=4, n=32)
                    for q in range(4):
                        last = mm(ps[32 * q:32 * q + 32, bank_of(key(g)), 0:256].rearrange("p (j n) -> p j n", n=32),
                                  ones[:, 0:32], rows[:, q], start=True, stop=True, skip_group_check=True)
                    last.then_inc(products, 1)

                gate_up_first()
                side(0)
                with pe.Fori(0, (NG - 3) // 2) as it:
                    gate_up(1, it)
                    down(0, it)
                    gate_up(2, it)
                    down(1, it)
                for g in (NG - 2, NG - 1):
                    gate_up(g)
                    down(g - 1)
                g, after = NG - 1, (1, 3, 4, 6)[f]
                wait_split(("D", f, g))
                pe.wait_ge(hid_ready, 2 * NG * f + 2 * g + 2)
                wh, wl = wk(("D", f, g), 2)
                first, second = last_slots(f)
                for s in (first, second):
                    o, n = PIECES[s][:2]
                    for j in range(KD):
                        key = ("d", f, g, j, s)
                        wait_bank(pe, key)
                        for c in range(2):
                            last = mm3(pt(key, n), wh[:, c, 128 * j:128 * j + 128], wl[:, c, 128 * j:128 * j + 128],
                                       hid_hi[:, g % 2, c, o:o + n], hid_lo[:, g % 2, c, o:o + n], c == 0, c == 1)
                        last.then_inc(products, 1)
                        if s == second and j == 3:
                            stat(after, seg_order(after)[0])
                if after == 3 * DEPTH:
                    stat(after, seg_order(after)[1])

            def columns(key, outs, q):
                wait_split(key)
                wh, wl = wk(key, KD)
                for slot, _, _ in outs:
                    wait_bank(pe, slot)
                for k in range(KD):
                    for slot, col, (o, n) in outs:
                        last = mm3(pt(slot, n), wh[:, k, col:col + 128], wl[:, k, col:col + 128],
                                   h_hi[:, k, o:o + n], h_lo[:, k, o:o + n], k == 0, k == KD - 1)
                        if k == KD - 1:
                            last.then_inc(products, 1)

            def rows(key, slots, q=None):
                wait_split(key)
                wh, wl = wk(key, KD)
                for t, slot in slots:
                    wait_bank(pe, slot)
                for k in range(KD):
                    if q is not None:
                        if k == 5 and slots[0][1] == ("V", key[1], 0, 4):
                            stat(q, 0)
                        wait_h(q, k, 0 if slots[0][0] < 4 else 1)
                    for t, slot in slots:
                        last = mm3(pt(slot, 256), h_hi[:, k, 128 * t:128 * t + 128], h_lo[:, k, 128 * t:128 * t + 128],
                                   wh[:, k, :], wl[:, k, :], k == 0, k == KD - 1)
                        if k == KD - 1:
                            last.then_inc(products, 1)

            def mix(l):
                ms = mix_segs(l)
                ns = len(ms)
                q = 3 * l + 1
                for ts in ((4, 5), (0, 1, 2, 3)):
                    for v in range(2):
                        rows(("V", l, v), [(t, ("V", l, v, t)) for t in ts], q)
                for c in range(2):
                    columns(("conv", l, c), [(("conv" + w, l, c, s), 128 if w == "g" else 0, ms[s])
                                             for w in "ga" for s in range(ns)], q)
                rows(("four", l), [(t, ("X", l, t)) for t in range(sum(n for _, n in ms) // 128)])
                for w, ss in (("Q", ms), ("K", BOTH)):
                    for v in range(2):
                        columns((w, l, v), [((w, l, 2 * v + c, s), 128 * c, ss[s]) for c in range(2)
                                            for s in range(len(ss))], q)
                fourier(l)
                attention(l)
                order = (6, 7, 4, 5, 0, 1, 2, 3)
                for v, s in out_order(l):
                    key = ("out", l, v)
                    wait_split(key)
                    wh, wl = wk(key, KD)
                    o, n = PIECES[s][:2]
                    outs = [(("out", l, 2 * v + c, s), 128 * c) for c in range(2)]
                    for slots in ((outs,) if v == 0 else ((x,) for x in outs)):
                        for slot, _ in slots:
                            wait_bank(pe, slot)
                        for i, k in enumerate(order):
                            if v == 0 and k >= 6:
                                wait_freed(pe, ("Fo", l, k - 6, s))
                            elif v == 0 and k >= 4:
                                wait_freed(pe, ("pw", l, k - 4, s))
                            elif v == 0:
                                pe.wait_ge(mix_ready, HEADS * sum(len(mix_segs(x)) for x in range(l)) + k * ns + s + 1)
                            for slot, col in slots:
                                last = mm3(pt(slot, n), wh[:, k, col:col + 128], wl[:, k, col:col + 128],
                                           h_hi[:, k, o:o + n], h_lo[:, k, o:o + n], i == 0, i == KD - 1)
                                if i == KD - 1:
                                    last.then_inc(products, 1)
                        if slots[0][0] == ("out", l, 4, seg_order(q + 1)[1]):
                            stat(q + 1, seg_order(q + 1)[0])

            def fourier(l):
                ms = mix_segs(l)
                small = raw_of(("W", l))[:].rearrange("p (i k n) -> p i k n", i=4, k=2)
                pe.wait_ge(tables_landed, 48)
                wait_landed(pe, ("C", l))
                wait_landed(pe, ("S", l))
                wait_landed(pe, ("W", l))
                wait_freed(pe, ("X", l, sum(n for _, n in ms) // 128 - 1))
                wait_freed(pe, ("X", l, sum(n for _, n in ms) // 128 - 2))
                for j in range(2):
                    for w in "CS":
                        big = raw_of((w, l))[:].rearrange("p (k n) -> p k n", k=4)
                        for s, (o, n) in enumerate(ms):
                            key = ("Z", l, j, w, s)
                            wait_bank(pe, key)
                            nk = n // 128
                            for k in range(nk):
                                table = big[:, k, :] if s == 0 else small[:, 2 if w == "C" else 3, k, :]
                                last = mm(pt(key, n), xN[:, o // 128 + k, 128 * j:128 * j + 128], table,
                                          start=(k == 0), stop=(k == nk - 1))
                            last.then_inc(products, 1)
                for j in range(2):
                    for s, (o, n) in enumerate(ms):
                        key = ("F", l, j, s)
                        wait_bank(pe, key)
                        for i, w in enumerate("CS"):
                            wait_freed(pe, ("Z", l, j, w, s))
                            last = mm(pt(key, n), dft[:, i, :], zT[:, j, i, o:o + n], start=(i == 0), stop=(i == 1))
                        last.then_inc(products, 1)
                for p in range(2):
                    for s, (o, n) in enumerate(ms):
                        key = ("Fo", l, p, s)
                        wait_bank(pe, key)
                        for j in range(2):
                            wait_freed(pe, ("F", l, j, s))
                            last = mm(pt(key, n), small[:, 1, j, 128 * p:128 * p + 128], fT[:, j, o:o + n],
                                      start=(j == 0), stop=(j == 1))
                        last.then_inc(products, 1)

            def extra(key):
                kind, l = key[:2]
                ms = mix_segs(l)
                s = key[-1]
                o, n = ms[s]
                ao = 0 if s == 0 else C_CTX - HALF
                before = 2 * sum(len(mix_segs(x)) for x in range(l))
                wait_bank(pe, key)
                if kind == "hn":
                    pe.wait_ge(hsq_done, 2 * before + key[2] * len(ms) + s + 1)
                    mm(pt(key, n), ones[:], hsq[:, key[2], o:o + n], start=True, stop=True).then_inc(products, 1)
                    return
                if kind == "mean":
                    pe.wait_ge(acc_ready, 2 * (l + 1))
                elif kind == "var":
                    pe.wait_ge(csq_done, before + 2 * s + 2)
                else:
                    pe.wait_ge(cs_done, before + 2 * s + 2)
                small = raw_of(("W", l))[:].rearrange("p (i k n) -> p i k n", i=4, k=2)
                for c in range(2):
                    if kind == "var":
                        w, x = ones[:], csq[:, c, o:o + n]
                    elif kind == "mean":
                        w, x = ones[:], acc[:, c, ao:ao + n]
                    else:
                        w, x = small[:, 0, c, 128 * key[2]:128 * key[2] + 128], acc[:, c, ao:ao + n]
                    last = mm(pt(key, n), w, x, start=(c == 0), stop=(c == 1))
                last.then_inc(products, 1)

            def attention(l):
                us = units_of(l)
                ms = mix_segs(l)
                e_before = 2 * sum(len(units_of(x)) for x in range(l))
                u_before = e_before // 2
                for b in range(6):
                    pe.wait_ge(bank_free[b], plan.before_att[l][b])
                for i in range(steps_of(l)):
                    if i < len(us):
                        h, s, t = us[i]
                        if t == 0 and s == 0:
                            pe.wait_ge(q_ready, HEADS * l + h + 1)
                            pe.wait_ge(k_ready, HEADS * l + h + 1)
                            wait_freed(pe, ("K", l, h, 1))
                        if i >= 2:
                            pe.wait_ge(exp_done, e_before + 2 * (i - 1))
                        at0 = 1536 * (i % 2)
                        o = ms[s][0] + 128 * t
                        if s == 0:
                            parts = ((0, 0, 0, 512), (0, 512, 512, 256), (1, 768, 0, 256), (1, 1024, 256, 512))
                        else:
                            parts = ((0, 0, 512, 256), (1, 256, 512, 256))
                        for st, po, ko, n in parts:
                            last = mm(pflat[:, at0 + po:at0 + po + n], qpad[:, h % 2, st, o:o + 128],
                                      kT[:, h, ko:ko + n], start=True, stop=True, skip_group_check=True)
                        last.then_inc(products, 1)

                    def turn_p(half):
                        u = i - 2
                        h, s, t = us[u]
                        key = ("T", l, u, half)
                        wait_bank(pe, key)
                        if half == 0:
                            pe.wait_ge(p_ready, u_before + u + 1)
                        ks = range(0, 4) if (s == 0 and half == 0) else range(4, 6) if s == 0 else range(2)
                        for n, k in enumerate(ks):
                            last = nc.tensor.transpose(ps[:, 6, 128 * n:128 * n + 128], e0[:, u % 3, 128 * k:128 * k + 128], ident[:])
                        last.then_inc(products, 1)

                    if 0 <= i - 2 < len(us):
                        turn_p(0)
                    if 0 <= i - 3 < len(us):
                        u = i - 3
                        h, s, t = us[u]
                        key = ("O", l, h, s)
                        if t == 0:
                            wait_bank(pe, key)
                        wait_freed(pe, ("T", l, u, 1 if s == 0 else 0))
                        ks = range(6) if s == 0 else range(4, 6)
                        for k in ks:
                            last = mm(ps[:, 7, 128 * t:128 * t + 128], vN[:, k, 128 * h:128 * h + 128],
                                      pT[:, u % 2, k if s == 0 else k - 4, :], start=(k == ks[0]), stop=(k == 5),
                                      skip_group_check=True)
                        if t == ms[s][1] // 128 - 1:
                            last.then_inc(products, 1)
                    if 0 <= i - 2 < len(us) and us[i - 2][1] == 0:
                        turn_p(1)
                    for key in extras(l, i):
                        extra(key)
                pe.wait_ge(exp_done, e_before + 2 * len(us))

            pe.wait_ge(ident_landed, 16)
            for s in (1, 0):
                o, n = BOTH[s]
                pe.wait_ge(ctx_landed if s else x_landed, 16 * (n // 128))
                for j in range(KD):
                    key = ("xin", s, j)
                    wait_bank(pe, key)
                    for t in range(n // 128):
                        last = nc.tensor.transpose(ps[:, bank_of(key), 128 * t:128 * t + 128],
                                                   xnat[:, o // 128 + t, 128 * j:128 * j + 128], ident[:])
                    last.then_inc(products, 1)
                if s:
                    pe.wait_ge(const_landed, 16 * N_CONST)
                    for i, n in enumerate((NROW, NROW, 2 * 2 * TAPS, 3 * KD)):
                        wait_bank(pe, ("vec", i))
                        nc.tensor.transpose(ps[:, bank_of(("vec", i)), 0:n], vstage[0:n, i, :], ident[0:n, 0:n]).then_inc(products, 1)
            pe.wait_ge(pool_const, 2)
            ada(BEFORE)
            for l in range(DEPTH):
                ffn(2 * l)
                mix(l)
                ffn(2 * l + 1)
            for i, t in enumerate(OUT_ORDER):
                pe.wait_ge(y_done, KD * (i // 2 + 1))
                for half in range(2):
                    key = ("xout", t, half)
                    wait_bank(pe, key)
                    for k in range(4):
                        last = nc.tensor.transpose(ps[:, bank_of(key), 128 * k:128 * k + 128],
                                                   xT[:, 4 * half + k, 128 * t:128 * t + 128], ident[:])
                    last.then_inc(products, 1)

        act_fn = nc.scalar.activation

        def x_written(q, j, s):
            if q == 0:
                return ("xin", s, j)
            if q == 5 and j < 4:
                return ("out", 1, j, 0)
            return ("out", (q - 2) // 3, j, s) if q % 3 == 2 else ("d", {1: 0, 3: 1, 4: 2, 6: 3}[q], NG - 1, j, s)

        @block.scalar
        def _(act):
            steps = [0]

            def split(key, g=None, it=None):
                k0 = key if g is None else key(g)
                wait_landed(act, key, g, it)
                s = plan.split[k0]
                if s >= RING:
                    old = plan.lastuse[split_keys[s - RING]]
                    if g is None:
                        wait_products(act, old)
                    else:
                        step = number(plan.lastuse[split_keys[plan.split[key(g + 2)] - RING]]) - number(old)
                        act.wait_ge(products, number(old) if it is None else it * step + number(old))
                act_fn(w_hi[s % RING][:], raw_of(k0)[:], ACT.Copy).then_inc(w_hi_done, 1)

            def square(q, s, j):
                o, n = PIECES[s][:2]
                wait_freed(act, x_written(q, j, s))
                if j >= 3:
                    act.wait_ge(squares_added, addcount(q, s, j - 2))
                act_fn(sqsum[:, o:o + n] if j == 0 else sq[:, j % 2, o:o + n], xT[:, j, o:o + n], ACT.Square)\
                    .then_inc(sq_done, 1)

            def root(q, s):
                o, n = PIECES[s][:2]
                key = ("stat", q, s)
                wait_products(act, key)
                act_fn(std[:, o:o + n], pt(key, n), ACT.Sqrt, bias=epsc[:], scale=1.0 / D).then_inc(bank_free[bank_of(key)], 1)

            def high(q, s, js=range(KD)):
                o, n, v = PIECES[s]
                for j in js:
                    act.wait_ge(t_done, hcount(q, j, s))
                    act_fn(h_hi[:, j, o:o + n], tn[:, j % 2, o:o + n], ACT.Identity,
                           bias=mod[:, q // 3, 24 * (q % 3) + j, v:v + 1], scale=1.0).then_inc(h_hi_done, 1)

            def ada(blocks):
                for b in blocks:
                    if b == 1:
                        for s, j in square_order(0):
                            square(0, s, j)
                    if b == 3:
                        for s in seg_order(0):
                            root(0, s)
                    key = ("ada", 0, b)
                    if b == 3:
                        split(("G", 0, 0))
                    wait_products(act, key)
                    n = FIRST_BLOCKS.index(b)
                    if n >= 2:
                        wait_products(act, ("adaT", 0, FIRST_BLOCKS[n - 2]))
                    act_fn(part[:, n % 2, :], pt(key), ACT.Copy).then_inc(bank_free[bank_of(key)], 1)

            def ffn(f, nxt):
                ss = segs_of(NORM_OF[f])

                def hidden(g, it=None):
                    pieces = sorted(last_slots(f)) if g == 0 else range(len(ss))
                    for c in range(2):
                        for s, (o, n) in [(s, PIECES[s][:2]) for s in pieces]:
                            wait_products(act, lambda x: ("g", f, x, c, s), g, it)
                            act_fn(sil[:, c, o:o + n], pt(("g", f, g, c, s), n), ACT.Silu)\
                                .then_inc(bank_free[bank_of(("g", f, g, c, s))], 1)
                        wait_freed(act, lambda x: ("u", f, x, c, pieces[-1]), g, it)
                        if g == 0:
                            wait_freed(act, ("u", f, 0, c, pieces[0]))
                        last_o = ss[-1][0] + ss[-1][1]
                        act_fn(hid_hi[:, g % 2, c, 0:last_o], prod[:, c, 0:last_o], ACT.Copy).then_inc(hid_hi_done, 1)

                def groups(g, it=None):
                    hidden(g, it)
                    split(lambda x: ("G", f, x), g + 1, it)
                    split(lambda x: ("U", f, x), g + 1, it)
                    split(lambda x: ("D", f, x), g, it)

                split(("G", f, 1))
                hidden(0)
                split(("U", f, 1))
                split(("D", f, 0))
                with act.Fori(0, (NG - 3) // 2) as it:
                    groups(1, it)
                    groups(2, it)
                hidden(NG - 2)
                split(("G", f, NG - 1))
                split(("U", f, NG - 1))
                split(("D", f, NG - 2))
                hidden(NG - 1)
                split(("D", f, NG - 1))
                for key in nxt:
                    split(key)
                q = (1, 3, 4, 6)[f]
                first, second = seg_order(q)
                for j in range(KD):
                    square(q, first, j)
                for j in range(4):
                    square(q, second, j)
                root(q, first)
                for j in range(4, KD):
                    square(q, second, j)
                    if q < 3 * DEPTH:
                        high(q, first, (j - 4,))
                if q < 3 * DEPTH:
                    high(q, first, range(4, KD))
                root(q, second)
                if q < 3 * DEPTH:
                    high(q, second)

            def mix(l):
                ms = mix_segs(l)
                ns = len(ms)

                def copy(key, dst, n):
                    wait_products(act, key)
                    act_fn(dst, pt(key, n), ACT.Copy).then_inc(bank_free[bank_of(key)], 1)

                rest = iter([("conv", l, 0), ("conv", l, 1), ("four", l), ("Q", l, 0), ("Q", l, 1), ("K", l, 0), ("K", l, 1),
                             ("out", l, 0), ("out", l, 1), ("out", l, 2), ("out", l, 3)])
                split(next(rest))
                for ts in ((4, 5), (0, 1, 2, 3)):
                    for v in range(2):
                        for t in ts:
                            copy(("V", l, v, t), vN[:, t, 256 * v:256 * v + 256], 256)
                        if t == 3:
                            split(next(rest))
                for c in range(2):
                    for s, (o, n) in enumerate(ms):
                        key = ("convg", l, c, s)
                        wait_products(act, key)
                        at0 = (C_LAT, C_CTX)[s]
                        act_fn(yline[:, c, at0:at0 + n], pt(key, n), ACT.Sigmoid).then_inc(bank_free[bank_of(key)], 1)
                    split(next(rest))
                for t in range(sum(n for _, n in ms) // 128):
                    copy(("X", l, t), xN[:, t, :], 256)
                split(next(rest))
                for h in range(HEADS):
                    for s, (o, n) in enumerate(ms):
                        copy(("Q", l, h, s), qT[:, h, o:o + n], n)
                    if h == 1:
                        split(next(rest))
                for h in range(HEADS):
                    copy(("K", l, h, 1), kT[:, h, LAT:TOK], CTX)
                for j in range(2):
                    for i, w in enumerate("CS"):
                        for s, (o, n) in enumerate(ms):
                            copy(("Z", l, j, w, s), zT[:, j, i, o:o + n], n)
                for j in range(2):
                    for s, (o, n) in enumerate(ms):
                        copy(("F", l, j, s), fT[:, j, o:o + n], n)

                def biased(kind, name, chunk0, p, s):
                    o, n = ms[s]
                    key = (kind, l, p, s)
                    wait_products(act, key)
                    col = ROW[name][0] + p
                    act_fn(h_hi[:, chunk0 + p, o:o + n], pt(key, n), ACT.Identity,
                           bias=vcol[:, l, col:col + 1], scale=1.0).then_inc(mix_hi_done, 1)

                for p in range(2):
                    for s in range(ns):
                        biased("Fo", "b_fourier", 6, p, s)
                us = units_of(l)
                u_before = sum(len(units_of(x)) for x in range(l))
                before = 2 * sum(len(mix_segs(x)) for x in range(l))
                all_n = sum(n for _, n in ms)

                def beside(i):
                    for s, (o, n) in enumerate(ms):
                        ao = 0 if s == 0 else C_CTX - HALF
                        if i == CONV_MEAN + s + 1:
                            wait_freed(act, ("mean", l, s))
                            for c in range(2):
                                act_fn(csq[:, c, o:o + n], acc[:, c, ao:ao + n], ACT.Square).then_inc(csq_done, 1)
                        if i == CONV_VAR + s:
                            key = ("var", l, s)
                            wait_products(act, key)
                            act_fn(cst[:, o:o + n], pt(key, n), ACT.Copy, scale=1.0 / CONVW).then_inc(bank_free[6], 1)
                    if i == CONV_VAR + ns - 1:
                        for s in range(ns):
                            wait_freed(act, ("var", l, s))
                        act_fn(cst[:, 0:all_n], cst[:, 0:all_n], ACT.Sqrt, bias=epsc[:]).then_inc(conv_root, 1)
                    if i == CONV_PW - 1:
                        g0, b0 = ROW["g_conv_ln"][0], ROW["b_conv_ln"][0]
                        for s, (o, n) in enumerate(ms):
                            ao = 0 if s == 0 else C_CTX - HALF
                            for c in range(2):
                                act.wait_ge(cn_done, before + 2 * s + c + 1)
                                act_fn(acc[:, c, ao:ao + n], acc[:, c, ao:ao + n], ACT.Silu,
                                       bias=vcol[:, l, b0 + c:b0 + c + 1], scale=vcol[:, l, g0 + c:g0 + c + 1]).then_inc(cs_done, 1)
                    for key in extras(l, i):
                        if key[0] == "pw":
                            biased("pw", "b_pw", 4, key[2], key[3])
                    for h in range(HEADS):
                        if i == head_end(l, h):
                            for s, (o, n) in enumerate(ms):
                                wait_freed(act, ("O", l, h, s))
                                act_fn(hsq[:, h, o:o + n], qT[:, h, o:o + n], ACT.Square).then_inc(hsq_done, 1)
                        for s, (o, n) in enumerate(ms):
                            if i == head_end(l, h) + 1 + s:
                                key = ("hn", l, h, s)
                                wait_products(act, key)
                                act_fn(hsq[:, h, o:o + n], pt(key, n), ACT.Copy, scale=1.0 / 128).then_inc(bank_free[6], 1)
                        if i == head_end(l, h) + ns:
                            for s in range(ns):
                                wait_freed(act, ("hn", l, h, s))
                            act_fn(hsq[:, h, 0:all_n], hsq[:, h, 0:all_n], ACT.Sqrt, bias=epsc[:]).then_inc(head_root, 1)

                for i in range(steps_of(l)):
                    if 0 <= i - 2 < len(us):
                        u = i - 2
                        h, s, t = us[u]
                        for half in range(2 if s == 0 else 1):
                            key = ("T", l, u, half)
                            wait_products(act, key)
                            k0, n = (4, 2) if half else (0, 4 if s == 0 else 2)
                            act_fn(pT[:, u % 2, k0:k0 + n, :], ps[:, 6, 0:128 * n].rearrange("p (k n) -> p k n", k=n),
                                   ACT.Copy).then_inc(bank_free[6], 1)
                    if i < len(us):
                        h, s, t = us[i]
                        act.wait_ge(max_done, u_before + i + 1)
                        at0, n = 1536 * (i % 2), TOK if s == 0 else CTX
                        for st, dst in ((0, e0[:, i % 3, 0:n]), (1, e1[:, i % 2, 0:n])):
                            act_fn(dst, pflat[:, at0 + n * st:at0 + n * st + n], ACT.Exp, bias=nb[:, i % 2, st:st + 1],
                                   scale=1.0, accum_out=sums[:, i % 2, st:st + 1]).then_inc(exp_done, 1)
                    if 0 <= i - 3 < len(us):
                        h, s, t = us[i - 3]
                        if t == ms[s][1] // 128 - 1:
                            o, n = ms[s]
                            copy(("O", l, h, s), qT[:, h, o:o + n], n)
                    beside(i)
                    if i in (3, 4, 14):
                        split(next(rest))
                hbefore = HEADS * sum(len(mix_segs(x)) for x in range(l))
                for h in range(HEADS):
                    for s, (o, n) in enumerate(ms):
                        act.wait_ge(ht_done, hbefore + h * ns + s + 1)
                        act_fn(h_hi[:, h, o:o + n], qT[:, h, o:o + n], ACT.Copy).then_inc(mix_hi_done, 1)
                split(next(rest))
                q = 3 * l + 2
                first, second = seg_order(q)
                for j in range(4):
                    square(q, second, j)
                    square(q, first, j)
                split(("G", 2 * l + 1, 0))
                for j in range(4, KD):
                    square(q, first, j)
                square(q, second, 4)
                root(q, first)
                high(q, first, (0, 1))
                square(q, second, 5)
                split(("U", 2 * l + 1, 0))
                high(q, first, (2, 3, 4))
                square(q, second, 6)
                high(q, first, (5, 6, 7))
                square(q, second, 7)
                root(q, second)
                high(q, second)

            for i, (n, dst) in enumerate(((NROW, vcol[:, 0, :]), (NROW, vcol[:, 1, :]),
                                          (4 * TAPS, wdw[:].rearrange("p l t c -> p (l t c)")),
                                          (3 * KD, ccol[:].rearrange("p i k -> p (i k)")))):
                wait_products(act, ("vec", i))
                act_fn(dst, ps[:, bank_of(("vec", i)), 0:n], ACT.Copy).then_inc(bank_free[bank_of(("vec", i))], 1)
            act.wait_ge(pool_const, 2)
            wait_freed(act, ("vec", 3))
            act.wait_ge(lam_dot, 1)
            act_fn(lamw[:, 0:2 * DEPTH], lamw[:, 0:2 * DEPTH], ACT.Exp).then_inc(lam_exp, 1)
            act.wait_ge(pad_zeroed, 1)
            for v in range(2):
                act_fn(cpad[:, :, v], ccol[:, v, :], ACT.Silu).then_inc(cpad_ready, 1)
                act_fn(ccol[:, v, :], ccol[:, v, :], ACT.Silu).then_inc(cpad_ready, 1)
            ada(BEFORE)
            high(0, 1, (0,))
            split(("U", 0, 0))
            high(0, 1, (1,))
            high(0, 1, range(2, KD))
            ada(BETWEEN)
            high(0, 0)
            for l in range(DEPTH):
                ffn(2 * l, [("V", l, 0), ("V", l, 1)])
                mix(l)
                ffn(2 * l + 1, [("G", 2 * l + 2, 0), ("U", 2 * l + 2, 0)] if l < DEPTH - 1 else [])
            for i, t in enumerate(OUT_ORDER):
                if i >= 2:
                    act.wait_ge(out_landed[i % 2], 16 * (i // 2))
                for half in range(2):
                    key = ("xout", t, half)
                    wait_products(act, key)
                    act_fn(onat[:, i % 2, 512 * half:512 * half + 512], pt(key), ACT.Copy)\
                        .then_inc(bank_free[bank_of(key)], 1)

        dve_ = nc.vector
        tt, stt = dve_.tensor_tensor, dve_.scalar_tensor_tensor

        @block.vector
        def _(dve):
            steps = [0]

            def step(ins):
                ins.then_inc(dve_step, 1)
                steps[0] += 1
                return steps[0]

            def settle(back=0):
                if steps[0] - back > 0:
                    dve.wait_ge(dve_step, steps[0] - back)

            def split(key, g=None, it=None):
                k0 = key if g is None else key(g)
                s = plan.split[k0]
                if g is None and s and split_keys[s - 1] in POOL_TILES:
                    dve.wait_ge(w_split, s)
                dve.wait_ge(w_hi_done, s + 1 if g is None else lin(lambda k: plan.split[k] + 1, key, g, it))
                tt(w_lo[s % RING][:], raw_of(k0)[:], w_hi[s % RING][:].bitcast(F), ALU.subtract).then_inc(w_split, 1)

            def over_rms(q, s):
                o, n = PIECES[s][:2]
                wait_freed(dve, ("stat", q, s))
                step(dve_.reciprocal(rstd[:, o:o + n], std[:, o:o + n]))
                settle()

            def scaled(q, s, js=range(KD)):
                o, n, v = PIECES[s]
                for j in js:
                    if j >= 2:
                        dve.wait_ge(h_ready, hcount(q, j - 2, s))
                    stt(out=tn[:, j % 2, o:o + n], in0=xT[:, j, o:o + n], scalar=amul[:, q // 3, q % 3, j, v:v + 1],
                        in1=rstd[:, o:o + n], op0=ALU.mult, op1=ALU.mult).then_inc(t_done, 1)
                    if j:
                        low(q, s, j - 1)
                    if j == KD - 1:
                        low(q, s, j)

            def low(q, s, j):
                o, n, v = PIECES[s]
                dve.wait_ge(h_hi_done, hcount(q, j, s))
                stt(out=h_lo[:, j, o:o + n], in0=tn[:, j % 2, o:o + n], scalar=mod[:, q // 3, 24 * (q % 3) + j, v:v + 1],
                    in1=h_hi[:, j, o:o + n].bitcast(F), op0=ALU.add, op1=ALU.subtract).then_inc(h_ready, 1)

            def ada(blocks):
                for b in blocks:
                    key = ("adaT", 0, b)
                    wait_products(dve, key)
                    dve_.tensor_copy(mod[:, 0, 4 * b:4 * b + 4, :],
                                     ps[:, bank_of(key), 0:8].rearrange("p (j v) -> p j v", v=2)).then_inc(bank_free[bank_of(key)], 1)
                    if b == 1:
                        over_rms(0, 1)
                        split(("G", 0, 0))
                for b in blocks:
                    wait_freed(dve, ("adaT", 0, b))

            def shift_scale(l, i):
                m = slice(24 * i, 24 * i + 16)
                for v in range(2):
                    step(tt(mod[:, l, m, v], mod[:, l, m, v], vcol[:, l, m], ALU.add))
                settle()
                g0 = ROW[("g_ffn1", "g_mix", "g_ffn2")[i]][0]
                for v in range(2):
                    step(stt(out=amul[:, l, i, :, v], in0=mod[:, l, 24 * i + 8:24 * i + 16, v], scalar=1.0,
                             in1=vcol[:, l, g0:g0 + KD], op0=ALU.add, op1=ALU.mult))
                settle()

            def gates(l, i):
                m = slice(24 * i + 16, 24 * i + 24)
                for v in range(2):
                    step(tt(mod[:, l, m, v], mod[:, l, m, v], vcol[:, l, m], ALU.add))
                settle()
                step(dve_.tensor_scalar(gate[:, l, i, :, :], mod[:, l, m, :], 1.0 if i == 1 else 0.5, None, ALU.mult))
                settle()

            def ffn(f):
                ss = segs_of(NORM_OF[f])
                i = 2 * (f % 2)

                def side(g, quarters, it=None):
                    if g not in SIDE_GROUPS[f]:
                        return
                    n = side_number((f, g))

                    def counted(extra):
                        return 16 * n + extra if it is None else it * 32 + (16 * n + extra)

                    for q in quarters:
                        landed = 16 * (2 * n + q // 2 + 1)
                        dve.wait_ge(side_landed[q % 2], landed if it is None else it * 64 + landed)
                        for k in range(2):
                            for v in range(2):
                                w, c = side_raw[q % 2][:, k, :], ccol[:, v, 2 * q + k:2 * q + k + 1]
                                m = 4 * q + 2 * k + v
                                if m < 2:
                                    ins = dve_.tensor_scalar(side_acc[:, v, :], w, c, None, ALU.mult)
                                else:
                                    dve.wait_ge(side_summed, counted(m - 1))
                                    ins = stt(out=side_acc[:, v, :], in0=w, scalar=c, in1=side_acc[:, v, :],
                                              op0=ALU.mult, op1=ALU.add)
                                ins.then_inc(side_summed, 1)

                def side_end(g, it=None):
                    if g not in SIDE_GROUPS[f]:
                        return
                    key = lambda x: ("side", f, x)
                    l, b = SIDE_GROUPS[f][g]
                    n = side_number((f, g))
                    wait_products(dve, key, g, it)
                    if n:
                        dve.wait_ge(side_done, n if it is None else it * 2 + n)
                    dve_.transpose(side_col[:].rearrange("p j n -> p (j n)"), ps[:, bank_of(key(g)), 0:256])\
                        .then_inc(bank_free[bank_of(key(g))], 1)
                    wait_freed(dve, key, g, it)
                    at_ = 4 * b if it is None else it * 8 + 4 * b
                    dve_.tensor_copy(mod[:, l, bass.ds(at_, 4), :],
                                     side_col[:, :, 0].rearrange("p (v j) -> p j v", v=2)).then_inc(side_done, 1)

                def hidden(g, it=None):
                    pieces = sorted(last_slots(f)) if g == 0 else range(len(ss))
                    side(g, (0, 1), it)
                    for c in range(2):
                        if c == 1:
                            side(g, (2, 3), it)
                        n0 = 2 * NG * f + 2 * g + c + 1
                        if n0 > 2:
                            dve.wait_ge(hid_ready, n0 - 2 if it is None else it * 4 + (n0 - 2))
                        for s, (o, n) in [(s, PIECES[s][:2]) for s in pieces]:
                            wait_freed(dve, lambda x: ("g", f, x, c, s), g, it)
                            wait_products(dve, lambda x: ("u", f, x, c, s), g, it)
                            tt(prod[:, c, o:o + n], sil[:, c, o:o + n], pt(("u", f, g, c, s), n), ALU.mult)\
                                .then_inc(bank_free[bank_of(("u", f, g, c, s))], 1)
                        dve.wait_ge(hid_hi_done, n0 if it is None else it * 4 + n0)
                        e = ss[-1][0] + ss[-1][1]
                        tt(hid_lo[:, g % 2, c, 0:e], prod[:, c, 0:e], hid_hi[:, g % 2, c, 0:e].bitcast(F), ALU.subtract)\
                            .then_inc(hid_ready, 1)

                def add(g, js, it=None):
                    for j in js:
                        for s, (o, n) in enumerate(ss):
                            wait_products(dve, lambda x: ("d", f, x, j, s), g, it)
                            stt(out=xT[:, j, o:o + n], in0=pt(("d", f, g, j, s), n), scalar=gate[:, f // 2, i, j, s:s + 1],
                                in1=xT[:, j, o:o + n], op0=ALU.mult, op1=ALU.add)\
                                .then_inc(bank_free[bank_of(("d", f, g, j, s))], 1)

                def add_one(j, s):
                    o, n, v = PIECES[s]
                    key = ("d", f, NG - 1, j, s)
                    wait_products(dve, key)
                    stt(out=xT[:, j, o:o + n], in0=pt(key, n), scalar=gate[:, f // 2, i, j, v:v + 1],
                        in1=xT[:, j, o:o + n], op0=ALU.mult, op1=ALU.add).then_inc(bank_free[bank_of(key)], 1)

                def groups(g, it=None):
                    hidden(g, it)
                    add(g - 1, range(0, 2), it)
                    split(lambda x: ("G", f, x), g + 1, it)
                    add(g - 1, range(2, 4), it)
                    split(lambda x: ("U", f, x), g + 1, it)
                    add(g - 1, range(4, SIDE_AT + 1), it)
                    side_end(g, it)
                    add(g - 1, range(SIDE_AT + 1, KD), it)
                    split(lambda x: ("D", f, x), g, it)

                split(("G", f, 1))
                hidden(0)
                split(("U", f, 1))
                split(("D", f, 0))
                side_end(0)
                with dve.Fori(0, (NG - 3) // 2) as it:
                    groups(1, it)
                    groups(2, it)
                groups_last = NG - 2
                hidden(groups_last)
                add(groups_last - 1, range(0, 2))
                split(("G", f, NG - 1))
                add(groups_last - 1, range(2, 4))
                split(("U", f, NG - 1))
                add(groups_last - 1, range(4, SIDE_AT + 1))
                side_end(NG - 2)
                add(groups_last - 1, range(SIDE_AT + 1, KD))
                split(("D", f, NG - 2))
                hidden(NG - 1)
                add(NG - 2, range(0, 4))
                split(("D", f, NG - 1))
                add(NG - 2, range(4, SIDE_AT + 1))
                side_end(NG - 1)
                add(NG - 2, range(SIDE_AT + 1, KD))
                q = (1, 3, 4, 6)[f]
                first, second = last_slots(f)
                for j in range(KD):
                    add_one(j, first)
                for j in range(4):
                    add_one(j, second)
                if q == 3 * DEPTH:
                    over_rms(q, first)
                    for j in range(4, KD):
                        add_one(j, second)
                    for s in (first, second):
                        if s == second:
                            over_rms(q, s)
                        o, n = PIECES[s][:2]
                        for j in range(KD):
                            stt(out=xT[:, j, o:o + n], in0=xT[:, j, o:o + n], scalar=ccol[:, 2, j:j + 1],
                                in1=rstd[:, o:o + n], op0=ALU.mult, op1=ALU.mult).then_inc(y_done, 1)
                    return
                if SIDE_GROUPS[f]:
                    dve.wait_ge(side_done, side_number((f, max(SIDE_GROUPS[f]))) + 1)
                shift_scale(q // 3, q % 3)
                first, second = seg_order(q)
                over_rms(q, first)
                for j in range(4, KD):
                    add_one(j, second)
                    scaled(q, first, (j - 4,))
                scaled(q, first, range(4, KD))
                over_rms(q, second)
                scaled(q, second)

            def mix(l):
                ms = mix_segs(l)
                ns = len(ms)
                n_line = LAT if ns == 1 else LAT + HALF + CTX
                gates(l, 1)
                shift_scale(l, 2)
                gates(l, 2)
                for c in range(2):
                    for at0 in (0, C_LAT + LAT, C_CTX + CTX)[:ns + 1]:
                        step(dve_.memset(yline[:, c, at0:at0 + HALF], 0.0))
                rest = iter([("conv", l, 0), ("conv", l, 1), ("four", l), ("Q", l, 0), ("Q", l, 1), ("K", l, 0), ("K", l, 1),
                             ("out", l, 0), ("out", l, 1), ("out", l, 2), ("out", l, 3)])
                for _ in range(3):
                    split(next(rest))
                for c in range(2):
                    for s, (o, n) in enumerate(ms):
                        at0 = (C_LAT, C_CTX)[s]
                        wait_freed(dve, ("convg", l, c, s))
                        key = ("conva", l, c, s)
                        wait_products(dve, key)
                        tt(yline[:, c, at0:at0 + n], pt(key, n), yline[:, c, at0:at0 + n], ALU.mult)\
                            .then_inc(bank_free[bank_of(key)], 1)
                    split(next(rest))
                settle()
                for c in range(2):
                    for s in range(ns):
                        wait_freed(dve, ("conva", l, c, s))
                b0 = ROW["b_dw"][0]
                for tap in range(TAPS):
                    for c in range(2):
                        w = wdw[:, l, tap, c:c + 1]
                        src = yline[:, c, tap:tap + n_line]
                        if tap == 0:
                            step(dve_.tensor_scalar(acc[:, c, 0:n_line], src, w, vcol[:, l, b0 + c:b0 + c + 1], ALU.mult, ALU.add))
                            continue
                        settle(0 if tap == TAPS - 1 and c == 1 else 1)
                        ins = stt(out=acc[:, c, 0:n_line], in0=src, scalar=w, in1=acc[:, c, 0:n_line], op0=ALU.mult, op1=ALU.add)
                        if tap < TAPS - 1:
                            step(ins)
                        else:
                            ins.then_inc(acc_ready, 1)
                    if tap in (10, 18):
                        split(next(rest))
                dve.wait_ge(tables_landed, 48)
                for h in range(HEADS):
                    key = ("K", l, h, 0)
                    wait_products(dve, key)
                    dve.wait_ge(acc_ready, 2 * (l + 1))
                    if h:
                        dve.wait_ge(k_ready, HEADS * l + h)
                    step(dve_.stream_shuffle(krope[:], pt(key), SWAP))
                    step(tt(kT[:, h, 0:LAT], pt(key), rope_c[:], ALU.mult))
                    settle(1)
                    tt(krope[:], krope[:], rope_s[:], ALU.mult).then_inc(bank_free[bank_of(key)], 1)
                    wait_freed(dve, key)
                    settle()
                    tt(kT[:, h, 0:LAT], kT[:, h, 0:LAT], krope[:], ALU.add).then_inc(k_ready, 1)

                for h in range(HEADS):
                    for s in range(ns):
                        wait_freed(dve, ("Q", l, h, s))
                    if h:
                        settle()
                    else:
                        dve.wait_ge(k_ready, HEADS * (l + 1))
                    step(dve_.stream_shuffle(krope[:], qT[:, h, 0:LAT], SWAP))
                    settle()
                    step(tt(krope[:], krope[:], rope_s[:], ALU.mult))
                    step(tt(qT[:, h, 0:LAT], qT[:, h, 0:LAT], rope_c[:], ALU.mult))
                    settle()
                    step(tt(qT[:, h, 0:LAT], qT[:, h, 0:LAT], krope[:], ALU.add))
                for v in range(2):
                    wait_products(dve, plan.lastuse[("K", l, v)])
                for b in range(2):
                    step(dve_.memset(qpad[64:128, b, 0, :], 0.0))
                    step(dve_.memset(qpad[0:64, b, 1, :], 0.0))

                def pad_q(h):
                    if h >= 2:
                        wait_products(dve, ("score", l, max(i for i, u in enumerate(us) if u[0] == h - 2)))
                    settle()
                    for st in range(2):
                        r = slice(64 * st, 64 * st + 64)
                        ins = dve_.tensor_scalar(qpad[r, h % 2, st, 0:all_n], qT[r, h, 0:all_n], HD ** -0.5, None, ALU.mult)
                        if st == 0:
                            step(ins)
                        else:
                            ins.then_inc(q_ready, 1)

                us = units_of(l)
                u_before = sum(len(units_of(x)) for x in range(l))
                all_n = sum(n for _, n in ms)
                mbefore = 8 * sum(len(mix_segs(x)) for x in range(l))

                def biased_low(kind, name, chunk0, before, p, s):
                    o, n = ms[s]
                    key = (kind, l, p, s)
                    col = ROW[name][0] + p
                    dve.wait_ge(mix_hi_done, before + p * ns + s + 1)
                    stt(out=h_lo[:, chunk0 + p, o:o + n], in0=pt(key, n), scalar=vcol[:, l, col:col + 1],
                        in1=h_hi[:, chunk0 + p, o:o + n].bitcast(F), op0=ALU.add, op1=ALU.subtract)\
                        .then_inc(bank_free[bank_of(key)], 1)

                pad_q(0)
                for p in range(2):
                    for s in range(ns):
                        biased_low("Fo", "b_fourier", 6, mbefore, p, s)

                def beside(i):
                    for s, (o, n) in enumerate(ms):
                        ao = 0 if s == 0 else C_CTX - HALF
                        if i == CONV_MEAN + s:
                            key = ("mean", l, s)
                            wait_products(dve, key)
                            dve.wait_ge(acc_ready, 2 * (l + 1))
                            for c in range(2):
                                ins = stt(out=acc[:, c, ao:ao + n], in0=pt(key, n), scalar=-1.0 / CONVW,
                                          in1=acc[:, c, ao:ao + n], op0=ALU.mult, op1=ALU.add)
                                if c == 0:
                                    step(ins)
                                else:
                                    ins.then_inc(bank_free[bank_of(key)], 1)
                        if i == CONV_VAR + ns + s:
                            dve.wait_ge(conv_root, l + 1)
                            dve_.reciprocal(crs[:, o:o + n], cst[:, o:o + n]).then_inc(conv_scale, 1)
                    for key in extras(l, i):
                        if key[0] == "pw":
                            biased_low("pw", "b_pw", 4, mbefore + 2 * ns, key[2], key[3])
                    for h in range(HEADS):
                        for s, (o, n) in enumerate(ms):
                            if i == head_end(l, h) + ns + 1 + s:
                                dve.wait_ge(head_root, HEADS * l + h + 1)
                                step(dve_.reciprocal(hsq[:, h, o:o + n], hsq[:, h, o:o + n]))
                                settle()
                                stt(out=qT[:, h, o:o + n], in0=qT[:, h, o:o + n], scalar=gsub[:, l:l + 1],
                                    in1=hsq[:, h, o:o + n], op0=ALU.mult, op1=ALU.mult).then_inc(ht_done, 1)

                def combine(i):
                    h, s, t = us[i]
                    dve.wait_ge(exp_done, 2 * (u_before + i + 1))
                    p, n = i % 2, TOK if s == 0 else CTX
                    if i >= 2:
                        dve.wait_ge(p_ready, u_before + i - 1)
                    step(dve_.reciprocal(rs[:, p, :], sums[:, p, :]))
                    settle()
                    step(dve_.tensor_scalar(e1[:, p, 0:n], e1[:, p, 0:n], rs[:, p, 1:2], neglam[:, l:l + 1], ALU.mult, ALU.mult))
                    settle()
                    stt(out=e0[:, i % 3, 0:n], in0=e0[:, i % 3, 0:n], scalar=rs[:, p, 0:1], in1=e1[:, p, 0:n],
                        op0=ALU.mult, op1=ALU.add).then_inc(p_ready, 1)

                for i in range(steps_of(l)):
                    if i < len(us):
                        h, s, t = us[i]
                        wait_products(dve, ("score", l, i))
                        at0, n, p = 1536 * (i % 2), TOK if s == 0 else CTX, i % 2
                        dve_.reduce_max(nb[:, p, :], pflat[:, at0:at0 + 2 * n].rearrange("p (s n) -> p s n", s=2), AX.X,
                                        negate=True).then_inc(max_done, 1)
                    if 1 <= i <= len(us):
                        combine(i - 1)
                    if i < len(us) and s == 0 and t == 1 and h < HEADS - 1:
                        pad_q(h + 1)
                    beside(i)
                def add_out(j, s):
                    o, n, v = PIECES[s]
                    key = ("out", l, j, s)
                    wait_products(dve, key)
                    stt(out=xT[:, j, o:o + n], in0=pt(key, n), scalar=gate[:, l, 1, j, v:v + 1], in1=xT[:, j, o:o + n],
                        op0=ALU.mult, op1=ALU.add).then_inc(bank_free[bank_of(key)], 1)

                q = 3 * l + 2
                for _ in range(3):
                    next(rest)
                first, second = seg_order(q)
                for v, s in out_order(l):
                    add_out(2 * v, s)
                    if (v, s) == (2, second):
                        over_rms(q, first)
                        scaled(q, first, (0, 1))
                    if (v, s) == (3, second):
                        scaled(q, first, (5, 6, 7))
                    add_out(2 * v + 1, s)
                    if (v, s) == (2, second):
                        scaled(q, first, (2, 3, 4))
                    if (v, s) == (0, ns - 1):
                        split(next(rest))
                    if (v, s) == (1, ns - 1):
                        split(("G", 2 * l + 1, 0))
                over_rms(q, second)
                scaled(q, second)

            dve_.memset(cpad[:], 0.0).then_inc(pad_zeroed, 1)
            def take_tokens(s):
                o, n = BOTH[s]
                for j in range(KD):
                    key = ("xin", s, j)
                    wait_products(dve, key)
                    dve_.tensor_copy(xT[:, j, o:o + n], pt(key, n)).then_inc(bank_free[bank_of(key)], 1)

            take_tokens(1)
            dve.wait_ge(const_landed, 16 * N_CONST)
            for l in range(DEPTH):
                for i in range(2):
                    settle()
                    step(tt(lamp[:], lamv[:, l, 2 * i, :], lamv[:, l, 2 * i + 1, :], ALU.mult))
                    settle()
                    ins = dve_.reduce_sum(lamw[:, 2 * l + i:2 * l + i + 1], lamp[:], AX.X)
                    if l == DEPTH - 1 and i == 1:
                        ins.then_inc(lam_dot, 1)
                    else:
                        step(ins)
            dve.wait_ge(lam_exp, 1)
            for l in range(DEPTH):
                step(tt(neglam[:, l:l + 1], lamw[:, 2 * l + 1:2 * l + 2], lamw[:, 2 * l:2 * l + 1], ALU.subtract))
                settle()
                step(dve_.tensor_scalar(neglam[:, l:l + 1], neglam[:, l:l + 1], -LAM_INIT[l], None, ALU.add))
                wait_freed(dve, ("vec", l))
                g0 = ROW["g_subln"][0]
                step(dve_.tensor_scalar(gsub[:, l:l + 1], vcol[:, l, g0:g0 + 1], 1.0 - LAM_INIT[l], None, ALU.mult))
            take_tokens(0)
            for i in range(4):
                wait_freed(dve, ("vec", i))
            dve.wait_ge(cpad_ready, 4)
            ada(BEFORE)
            shift_scale(0, 0)
            scaled(0, 1, (0, 1))
            split(("U", 0, 0))
            scaled(0, 1, range(2, KD))
            over_rms(0, 0)
            ada(BETWEEN)
            gates(0, 0)
            scaled(0, 0)
            for l in range(DEPTH):
                if l:
                    gates(l, 0)
                ffn(2 * l)
                mix(l)
                ffn(2 * l + 1)


LAM_INIT = [0.8 - 0.6 * math.exp(-0.3 * l) for l in range(DEPTH)]
SWAP = [(i + 16) % 32 for i in range(32)]
SMALL = ("dft_cos", "dft_sin", "dft_cos_ctx", "dft_sin_ctx")
N_CONST = 6


def shape_tables():
    def dft(n, norm):
        i = np.arange(n)
        ang = 2.0 * np.pi * ((i[:, None] * i[None, :]) % n) / n
        return (np.cos(ang) * norm).astype(np.float32), (np.sin(ang) * norm).astype(np.float32)

    c, s = dft(LAT, LAT ** -0.5)
    cc, sc = dft(CTX, CTX ** -0.5)
    cd, sd = dft(64, 64 ** -0.5)
    both = np.zeros((128, 2, 128), np.float32)
    for g in range(2):
        both[64 * g:64 * g + 64, 0, 64 * g:64 * g + 64] = cd
        both[64 * g:64 * g + 64, 1, 64 * g:64 * g + 64] = -sd
    rot = HD // 2
    inv = (10000.0 ** (-np.arange(0, rot, 2, dtype=np.float32) / np.float32(rot))).astype(np.float32)
    t = np.arange(LAT)
    pos = np.stack([t // GRID_W, t % GRID_W]).astype(np.float32)
    rc, rsn = np.zeros((128, LAT), np.float32), np.zeros((128, LAT), np.float32)
    for p in range(128):
        d = p % HD
        ang = (pos[d // rot] * inv[d % (rot // 2)]).astype(np.float32)
        rc[p] = np.cos(ang)
        rsn[p] = np.sin(ang) * (-1.0 if d % rot < rot // 2 else 1.0)
    sel = np.zeros((128, 2), np.float32)
    for v in range(2):
        sel[v::32, v] = 1.0
    return {"dft_cos": c, "dft_sin": s, "dft_cos_ctx": cc, "dft_sin_ctx": sc, "dft_groups": both,
            "rope_cos": rc, "rope_sin": rsn, "ident": np.eye(128, dtype=np.float32), "sel": sel}


WEIGHTS = ("x", "ctx", "w_ada", "w_ffn1_gate", "w_ffn1_up", "w_ffn1_down", "w_ffn2_gate", "w_ffn2_up", "w_ffn2_down",
           "w_in", "w_pw", "w_fourier", "w_out")


def kernel(**inputs):
    import concourse.bacc as bacc
    from concourse.bass_utils import run_bass_kernel_spmd

    nc = bacc.Bacc("TRN2", target_bir_lowering=False, num_devices=1)
    arr = {k: np.ascontiguousarray(inputs[k]) for k in WEIGHTS}

    def stack(parts):
        return np.ascontiguousarray(np.concatenate([np.asarray(p).reshape(-1, 128) for p in parts], axis=0))

    for l in range(DEPTH):
        arr[f"vec{l}"] = stack([np.asarray(inputs[n])[l] for n in ROW])
    arr["vecw"] = stack([inputs["w_dw"]])
    arr["vecc"] = stack([inputs["c"], inputs["c_ctx"], inputs["g_final"]])
    arr["lams"] = np.ascontiguousarray(np.stack([np.asarray(inputs[n]) for n in ("lambda_q1", "lambda_k1", "lambda_q2", "lambda_k2")], axis=1)).reshape(1, -1)
    arr.update(shape_tables())
    a = {k: nc.dram_tensor(f"in_{k}", v.shape, mybir.dt.from_np(v.dtype), kind="ExternalInput").ap() for k, v in arr.items()}
    a["out"] = nc.dram_tensor("out_0", (1, LAT, D), mybir.dt.float32, kind="ExternalOutput").ap()
    trunk(nc, a)
    r = run_bass_kernel_spmd(nc, [{f"in_{k}": v for k, v in arr.items()}], core_ids=[0])
    return r.results[0]["out_0"]
```
